# Optimizing a Trainium2 kernel written in Bass

```python
import math
import jax, jax.numpy as jnp
from jax import lax
import numpy as np

D_MODEL = 1024
BATCH = 1
SEQ = 512
DEPTH = 1

PLE_DIM = 256
A_HEADS = 8
A_HEAD_DIM = 64
A_WIDTH = A_HEADS * A_HEAD_DIM
DILATED_PATTERNS = ((128, 1), (512, 4), (2048, 16))
ATT_BLOCK = 128
B_HEADS = 4
B_HEAD_DIM = 128
B_WIDTH = B_HEADS * B_HEAD_DIM
CONV_WIDTH = 4
DELTA_CHUNK = 64
MIX_WIDTH = A_WIDTH + B_WIDTH
IN_SIZES = (A_WIDTH, A_WIDTH, A_WIDTH, B_WIDTH, B_WIDTH, B_WIDTH, B_WIDTH, B_HEADS, B_HEADS)
IN_COLS = sum(IN_SIZES)
N_EXPERTS = 32
TOP_K = 4
D_EXPERT = D_MODEL
SWIGLU_LIMIT = 7.0
SWIGLU_ALPHA = 1.702
MOE_BLOCK = 128
LN_EPS = 1e-5
RMS_EPS = 1e-6
L2_EPS = 1e-6
DEEPNORM_ALPHA = (2.0 * DEPTH) ** 0.25
DEEPNORM_BETA = (8.0 * DEPTH) ** -0.25

kernel_name = "hymba_dilated_deltanet_moe_deepnorm"

def layer_norm(x, g, b):
    xf = x.astype(jnp.float32)
    mu = jnp.mean(xf, axis=-1, keepdims=True)
    xc = xf - mu
    var = jnp.mean(xc * xc, axis=-1, keepdims=True)
    y = xc * lax.rsqrt(var + LN_EPS) * g.astype(jnp.float32) + b.astype(jnp.float32)
    return y.astype(x.dtype)

def _dilated_branch(q, k, v, window, dilation):
    b, s, h, e = q.shape
    n_back = window // dilation
    L = s // dilation
    nb = -(-L // ATT_BLOCK)
    Lp = nb * ATT_BLOCK

    def split(t):
        t = t.reshape(b, L, dilation, h, e).transpose(0, 2, 3, 1, 4)
        return jnp.pad(t, ((0, 0), (0, 0), (0, 0), (0, Lp - L), (0, 0)))

    def band(t):
        t = jnp.pad(t, ((0, 0), (0, 0), (0, 0), (ATT_BLOCK, 0), (0, 0)))
        t = t.reshape(b, dilation, h, nb + 1, ATT_BLOCK, e)
        return jnp.concatenate([t[:, :, :, :-1], t[:, :, :, 1:]], axis=4)

    qb = split(q).reshape(b, dilation, h, nb, ATT_BLOCK, e)
    kb = band(split(k))
    vb = band(split(v))

    qi = jnp.arange(ATT_BLOCK)[:, None]
    kc = jnp.arange(2 * ATT_BLOCK)[None, :]
    dist = ATT_BLOCK + qi - kc
    key_pos = jnp.arange(nb)[:, None, None] * ATT_BLOCK + kc[None] - ATT_BLOCK
    valid = (dist >= 0) & (dist <= n_back) & (key_pos >= 0)

    scores = jnp.einsum('bdhnqe,bdhnke->bdhnqk', qb, kb,
                        preferred_element_type=jnp.float32) * (1.0 / math.sqrt(e))
    scores = jnp.where(valid, scores, -jnp.inf)
    m = jnp.max(scores, axis=-1, keepdims=True)
    pr = jnp.exp(scores - m)
    den = jnp.sum(pr, axis=-1, keepdims=True)
    o = jnp.einsum('bdhnqk,bdhnke->bdhnqe', pr.astype(vb.dtype), vb,
                   preferred_element_type=jnp.float32) / den
    lse = (m + jnp.log(den))[..., 0]

    o = o.reshape(b, dilation, h, Lp, e)[:, :, :, :L].transpose(0, 3, 1, 2, 4).reshape(b, s, h, e)
    lse = lse.reshape(b, dilation, h, Lp)[..., :L].transpose(0, 3, 1, 2).reshape(b, s, h)
    return o, lse

def dilated_attention(q, k, v):
    outs, lses = [], []
    for window, dilation in DILATED_PATTERNS:
        o, lse = _dilated_branch(q, k, v, window, dilation)
        outs.append(o)
        lses.append(lse)
    wts = jax.nn.softmax(jnp.stack(lses, 0), axis=0)
    return jnp.einsum('pbsh,pbshe->bshe', wts, jnp.stack(outs, 0))

def _causal_depthwise_conv(x, w):
    c = x.shape[-1]
    return lax.conv_general_dilated(x, w[:, None, :].astype(x.dtype), window_strides=(1,),
                                    padding=[(CONV_WIDTH - 1, 0)],
                                    dimension_numbers=('NWC', 'WIO', 'NWC'),
                                    feature_group_count=c)

def _l2norm(t):
    return t * lax.rsqrt(jnp.sum(t * t, axis=-1, keepdims=True) + L2_EPS)

def _gated_delta_rule(q, k, v, g, beta):
    b, s, h, dk = q.shape
    dv = v.shape[-1]
    c = DELTA_CHUNK
    n = s // c

    def chunk(t):
        t = t.reshape((b, n, c, h) + t.shape[3:])
        return jnp.moveaxis(t, 3, 1)

    q, k, v, g, beta = [chunk(t) for t in (q, k, v, g, beta)]
    gc = jnp.cumsum(g, axis=-1)
    diff = gc[..., :, None] - gc[..., None, :]
    strict = jnp.tril(jnp.ones((c, c), bool), -1)
    causal = jnp.tril(jnp.ones((c, c), bool))
    decay_strict = jnp.where(strict, jnp.exp(jnp.where(strict, diff, 0.0)), 0.0)
    decay_causal = jnp.where(causal, jnp.exp(jnp.where(causal, diff, 0.0)), 0.0)

    kbeta = k * beta[..., None]
    a_mat = jnp.eye(c, dtype=jnp.float32) + jnp.einsum('bhnid,bhnjd->bhnij', kbeta, k) * decay_strict
    rhs = jnp.concatenate([v * beta[..., None], kbeta * jnp.exp(gc)[..., None]], axis=-1)
    sol = lax.linalg.triangular_solve(a_mat, rhs, left_side=True, lower=True, unit_diagonal=True)
    u, w = sol[..., :dv], sol[..., dv:]

    attn = jnp.einsum('bhnid,bhnjd->bhnij', q, k) * decay_causal
    q_dec = q * jnp.exp(gc)[..., None]
    g_last = gc[..., -1]
    k_dec = k * jnp.exp(g_last[..., None] - gc)[..., None]
    xs = [jnp.moveaxis(t, 2, 0) for t in (u, w, attn, q_dec, k_dec, g_last)]

    def step(state, inp):
        u_n, w_n, attn_n, qd_n, kd_n, gl_n = inp
        v_new = u_n - jnp.einsum('bhck,bhkv->bhcv', w_n, state)
        out = (jnp.einsum('bhck,bhkv->bhcv', qd_n, state)
               + jnp.einsum('bhij,bhjv->bhiv', attn_n, v_new))
        state = state * jnp.exp(gl_n)[..., None, None] + jnp.einsum('bhck,bhcv->bhkv', kd_n, v_new)
        return state, out

    s0 = jnp.zeros((b, h, dk, dv), jnp.float32)
    _, out = lax.scan(step, s0, xs)
    return out.transpose(1, 0, 3, 2, 4).reshape(b, s, h, dv)

def gated_deltanet(qkv, z, b_logit, a_logit, conv_w, a_log, dt_bias, norm_w):
    bsz, s, _ = qkv.shape
    qkv = jax.nn.silu(_causal_depthwise_conv(qkv, conv_w)).astype(jnp.float32)
    q, k, v = jnp.split(qkv, 3, axis=-1)
    q = _l2norm(q.reshape(bsz, s, B_HEADS, B_HEAD_DIM)) * (B_HEAD_DIM ** -0.5)
    k = _l2norm(k.reshape(bsz, s, B_HEADS, B_HEAD_DIM))
    v = v.reshape(bsz, s, B_HEADS, B_HEAD_DIM)
    beta = jax.nn.sigmoid(b_logit.astype(jnp.float32))
    g = -jnp.exp(a_log.astype(jnp.float32)) * jax.nn.softplus(
        a_logit.astype(jnp.float32) + dt_bias.astype(jnp.float32))
    o = _gated_delta_rule(q, k, v, g, beta)
    o = o * lax.rsqrt(jnp.mean(o * o, axis=-1, keepdims=True) + RMS_EPS) * norm_w.astype(jnp.float32)
    o = o * jax.nn.silu(z.astype(jnp.float32).reshape(bsz, s, B_HEADS, B_HEAD_DIM))
    return o.reshape(bsz, s, B_WIDTH)

def moe(x, w_router, b_router, w_gate_up, b_gate_up, w_down, b_down):
    bsz, s, d = x.shape
    t = bsz * s
    xt = x.reshape(t, d)
    logits = jnp.dot(xt, w_router, preferred_element_type=jnp.float32) + b_router.astype(jnp.float32)
    top_val, top_idx = lax.top_k(logits, TOP_K)
    gates = jax.nn.softmax(top_val, axis=-1)

    flat_e = top_idx.reshape(-1).astype(jnp.int32)
    flat_tok = jnp.repeat(jnp.arange(t, dtype=jnp.int32), TOP_K)
    flat_g = gates.reshape(-1)
    order = jnp.argsort(flat_e)
    sorted_e = flat_e[order]
    counts = jnp.bincount(flat_e, length=N_EXPERTS)
    padded = (counts + MOE_BLOCK - 1) // MOE_BLOCK * MOE_BLOCK
    start = jnp.cumsum(counts) - counts
    pad_end = jnp.cumsum(padded)
    pad_start = pad_end - padded
    dest = pad_start[sorted_e] + (jnp.arange(t * TOP_K) - start[sorted_e])

    n_blocks = -(-(t * TOP_K) // MOE_BLOCK) + N_EXPERTS
    n_rows = n_blocks * MOE_BLOCK
    buf_tok = jnp.full((n_rows,), t, jnp.int32).at[dest].set(flat_tok[order])
    buf_gate = jnp.zeros((n_rows,), jnp.float32).at[dest].set(flat_g[order])
    block_e = jnp.minimum(jnp.searchsorted(pad_end, jnp.arange(n_blocks) * MOE_BLOCK, side='right'),
                          N_EXPERTS - 1)

    x_pad = jnp.concatenate([xt, jnp.zeros((1, d), xt.dtype)], axis=0)
    xb = x_pad[buf_tok].reshape(n_blocks, MOE_BLOCK, d)

    def expert_block(args):
        xblk, e = args
        hgu = jnp.dot(xblk, w_gate_up[e]) + b_gate_up[e]
        gate = jnp.minimum(hgu[:, :D_EXPERT], SWIGLU_LIMIT)
        up = jnp.clip(hgu[:, D_EXPERT:], -SWIGLU_LIMIT, SWIGLU_LIMIT)
        act = (up + 1.0) * (gate * jax.nn.sigmoid(SWIGLU_ALPHA * gate))
        return jnp.dot(act, w_down[e]) + b_down[e]

    yb = lax.map(expert_block, (xb, block_e)).reshape(n_rows, d)
    y = jax.ops.segment_sum(yb * buf_gate[:, None].astype(yb.dtype), buf_tok, num_segments=t + 1)[:t]
    return y.reshape(bsz, s, d).astype(x.dtype)

def setup_inputs(seed: int = 0) -> dict:
    key = jax.random.key(seed)
    ks = jax.random.split(key, 24)
    f32 = jnp.float32
    nrm = lambda k, shape, scale: jax.random.normal(k, shape, f32) * scale

    x = jax.random.normal(ks[0], (BATCH, SEQ, D_MODEL), f32)
    p = jax.random.normal(ks[1], (DEPTH, BATCH, SEQ, PLE_DIM), f32)

    w_in = nrm(ks[2], (DEPTH, D_MODEL, IN_COLS), D_MODEL ** -0.5)
    offs = np.cumsum((0,) + IN_SIZES)
    col_scale = np.ones((IN_COLS,), np.float32)
    col_scale[offs[2]:offs[3]] = DEEPNORM_BETA
    col_scale[offs[5]:offs[6]] = DEEPNORM_BETA
    w_in = w_in * jnp.asarray(col_scale)

    conv_w = nrm(ks[3], (DEPTH, CONV_WIDTH, 3 * B_WIDTH), CONV_WIDTH ** -0.5)
    a_log = jnp.log(jax.random.uniform(ks[4], (DEPTH, B_HEADS), f32, 1.0, 16.0))
    dt = jnp.exp(jax.random.uniform(ks[5], (DEPTH, B_HEADS), f32, math.log(1e-3), math.log(1e-1)))
    dt_bias = dt + jnp.log(-jnp.expm1(-dt))
    gnorm_w = 1.0 + nrm(ks[6], (DEPTH, B_HEAD_DIM), 0.02)
    w_out = nrm(ks[7], (DEPTH, MIX_WIDTH, D_MODEL), MIX_WIDTH ** -0.5 * DEEPNORM_BETA)
    ln1_g = 1.0 + nrm(ks[8], (DEPTH, D_MODEL), 0.02)
    ln1_b = nrm(ks[9], (DEPTH, D_MODEL), 0.02)

    w_router = nrm(ks[10], (DEPTH, D_MODEL, N_EXPERTS), D_MODEL ** -0.5)
    b_router = nrm(ks[11], (DEPTH, N_EXPERTS), 0.01)
    w_gate_up = nrm(ks[12], (DEPTH, N_EXPERTS, D_MODEL, 2 * D_EXPERT), D_MODEL ** -0.5)
    b_gate_up = nrm(ks[13], (DEPTH, N_EXPERTS, 2 * D_EXPERT), 0.01)
    w_down = nrm(ks[14], (DEPTH, N_EXPERTS, D_EXPERT, D_MODEL), D_EXPERT ** -0.5 * DEEPNORM_BETA)
    b_down = nrm(ks[15], (DEPTH, N_EXPERTS, D_MODEL), 0.01)

    w_ple_gate = nrm(ks[16], (DEPTH, D_MODEL, D_MODEL), D_MODEL ** -0.5)
    b_ple_gate = nrm(ks[17], (DEPTH, D_MODEL), 0.01)
    w_ple_proj = nrm(ks[18], (DEPTH, PLE_DIM, D_MODEL), PLE_DIM ** -0.5 * DEEPNORM_BETA)
    ln2_g = 1.0 + nrm(ks[19], (DEPTH, D_MODEL), 0.02)
    ln2_b = nrm(ks[20], (DEPTH, D_MODEL), 0.02)

    return {"x": x, "p": p, "w_in": w_in, "conv_w": conv_w, "a_log": a_log, "dt_bias": dt_bias,
            "gnorm_w": gnorm_w, "w_out": w_out, "ln1_g": ln1_g, "ln1_b": ln1_b,
            "w_router": w_router, "b_router": b_router, "w_gate_up": w_gate_up,
            "b_gate_up": b_gate_up, "w_down": w_down, "b_down": b_down,
            "w_ple_gate": w_ple_gate, "b_ple_gate": b_ple_gate, "w_ple_proj": w_ple_proj,
            "ln2_g": ln2_g, "ln2_b": ln2_b}

def reference(x, p, w_in, conv_w, a_log, dt_bias, gnorm_w, w_out, ln1_g, ln1_b,
              w_router, b_router, w_gate_up, b_gate_up, w_down, b_down,
              w_ple_gate, b_ple_gate, w_ple_proj, ln2_g, ln2_b):
    bsz, s, _ = x.shape
    split_at = [int(o) for o in np.cumsum(IN_SIZES)[:-1]]
    for i in range(DEPTH):
        hproj = jnp.dot(x, w_in[i])
        qa, ka, va, qb, kb, vb, zb, bb, ab = jnp.split(hproj, split_at, axis=-1)
        shp = (bsz, s, A_HEADS, A_HEAD_DIM)
        ya = dilated_attention(qa.reshape(shp), ka.reshape(shp), va.reshape(shp))
        ya = ya.reshape(bsz, s, A_WIDTH).astype(x.dtype)
        yb = gated_deltanet(jnp.concatenate([qb, kb, vb], axis=-1), zb, bb, ab,
                            conv_w[i], a_log[i], dt_bias[i], gnorm_w[i]).astype(x.dtype)
        mix = jnp.dot(jnp.concatenate([ya, yb], axis=-1), w_out[i])
        x = layer_norm(DEEPNORM_ALPHA * x + mix, ln1_g[i], ln1_b[i])
        ffn = moe(x, w_router[i], b_router[i], w_gate_up[i], b_gate_up[i], w_down[i], b_down[i])
        ple = jax.nn.sigmoid(jnp.dot(x, w_ple_gate[i]) + b_ple_gate[i]) * jnp.dot(p[i], w_ple_proj[i])
        x = layer_norm(DEEPNORM_ALPHA * x + ffn + ple.astype(x.dtype), ln2_g[i], ln2_b[i])
    return x


_drawn_inputs = setup_inputs


def setup_inputs(seed=0):
    import zlib

    import numpy as np

    out = dict(_drawn_inputs(seed))
    spreads = {}
    factors = {'gnorm_w': 4.195,
     'b_router': 2.966,
     'b_gate_up': 8.0,
     'b_down': 8.0,
     'b_ple_gate': 57.844,
     'ln2_g': 8.089,
     'ln2_b': 8.383}
    for name, (base, spread) in spreads.items():
        noise = np.random.default_rng([zlib.crc32(name.encode()), seed]).standard_normal(out[name].shape)
        drawn = base * np.exp(spread * noise) if base else spread * noise
        out[name] = __import__('jax').numpy.asarray(drawn.astype(out[name].dtype))
    for name, factor in factors.items():
        out[name] = (out[name] * factor).astype(out[name].dtype)
    return out
```

```python
import math
from contextlib import ExitStack

import numpy as np
import concourse.bass as bass
from concourse import mybir

F32 = mybir.dt.float32
F32R = mybir.dt.float32r
BF16 = mybir.dt.bfloat16
I32 = mybir.dt.int32
U32 = mybir.dt.uint32
ALU = mybir.AluOpType
ACT = mybir.ActivationFunctionType
AX = mybir.AxisListType

P = 128
SEQ = 512
D = 1024
NT = SEQ // P
KD = D // P
HA, EA = 8, 64
HB = 4
PLE = 256
NE = 32
TOPK = 4
FE = 1024
KF = FE // P
TW = 2 * FE
BLOCK_TILES = KD + KF // 2
ALPHA = 2.0 ** 0.25
LN_EPS, RMS_EPS, L2_EPS = 1e-5, 1e-6, 1e-6
NEG = -1.0e30
LEVELS = 7
NBLK = 7
SLOTS = 6
CAP = SEQ
SKIP = 1 << 20

C_IDENT, C_ONES, C_UPPER, C_NEGM, C_STRICT = 0, 128, 256, 384, 512
C_STRIP = 640
C_LEVEL = C_STRIP + SEQ
C_ESEL = C_LEVEL + LEVELS * P
C_EBASE = C_ESEL + NE
C_TOTAL = C_EBASE + NE


def constants():
    c = np.zeros((P, C_TOTAL), np.float32)
    r = np.arange(P)
    c[:, C_IDENT:C_IDENT + P] = np.eye(P)
    c[:, C_ONES:C_ONES + P] = 1.0
    c[:, C_UPPER:C_UPPER + P] = r[:, None] <= r[None, :]
    c[:, C_NEGM:C_NEGM + P] = np.where(r[:, None] <= r[None, :], 0.0, NEG)
    c[:, C_STRICT:C_STRICT + P] = r[:, None] < r[None, :]
    dist = (SEQ - P) + r[:, None] - np.arange(SEQ)[None, :]
    count = np.zeros((P, SEQ))
    for window, dil in ((128, 1), (512, 4), (2048, 16)):
        count += (dist >= 0) & (dist % dil == 0) & (dist <= window // dil * dil)
    c[:, C_STRIP:C_STRIP + SEQ] = np.where(count > 0, np.log(np.maximum(count, 1)), NEG)
    for lv in range(LEVELS):
        m = 1 << lv
        same = (r[:, None] // (2 * m)) == (r[None, :] // (2 * m))
        off = ((r[:, None] // m) % 2 == 1) & ((r[None, :] // m) % 2 == 0)
        c[:, C_LEVEL + lv * P:C_LEVEL + (lv + 1) * P] = same & off
    c[:, C_ESEL:C_ESEL + NE] = np.arange(NE)
    c[:, C_EBASE:C_EBASE + NE] = np.arange(NE) * CAP
    return c


def table_rows():
    t = np.zeros((P, NE * CAP // P * 4), np.int32)
    t[:, 0::4] = SKIP
    t[:, 1::4] = SKIP
    return t


def payload():
    t = np.zeros((P, NT, TOPK, 4), np.int32)
    for tt in range(NT):
        tok = tt * P + np.arange(P)
        t[:, tt, :, 0] = tok[:, None]
        t[:, tt, :, 1] = tok[:, None] * TOPK + np.arange(TOPK)
    return t.reshape(P, NT * TOPK * 4)


def hybrid_layer(nc, x, xT, pT, w_in, conv_w, a_log, dt_bias, gnorm_w, w_out, ln1_g, ln1_b,
                 w_router, b_router, w_gate_up, b_gate_up, w_down, b_down,
                 w_ple_gate, b_ple_gate, w_ple_proj, ln2_g, ln2_b, consts, table0, pay0, out):
    ctx = ExitStack()
    with ctx:
        def sb(name, shape, dt=F32):
            return ctx.enter_context(nc.sbuf_tensor(name, shape, dt))

        def sem(name):
            return ctx.enter_context(nc.semaphore(name))

        x1_rows = nc.dram_tensor("x1_rows", (SEQ, D), F32, kind="Internal").ap()
        y_rows = nc.dram_tensor("y_rows", (SEQ * TOPK, D), F32, kind="Internal").ap()
        table = nc.dram_tensor("dispatch_table", (NE * CAP, 4), I32, kind="Internal").ap()
        bias_parts = nc.dram_tensor("bias_parts", (NE, 3, 2 * FE), BF16, kind="Internal").ap()

        W = sb("W", [P, 3 * FE * KD])
        w_in_slot = [W[:, s * 4096:(s + 1) * 4096].rearrange("p (k n) -> p k n", k=KD) for s in range(SLOTS)]
        gu_tile = [W[:, k * 2 * FE:(k + 1) * 2 * FE] for k in range(KD)]
        dn_tile = [W[:, (2 * KD + k) * FE:(2 * KD + k + 1) * FE] for k in range(KF)]
        LT = W[:, 0:2048].rearrange("p (h n) -> p h n", h=HB)
        KB = W[:, 2048:4096].rearrange("p (h n) -> p h n", h=HB)
        KDEC = W[:, 4096:6144].rearrange("p (h n) -> p h n", h=HB)
        VB = W[:, 6144:8192].rearrange("p (h n) -> p h n", h=HB)
        AT = W[:, 8192:10240].rearrange("p (h n) -> p h n", h=HB)
        T1 = W[:, 10240:12288].rearrange("p (h n) -> p h n", h=HB)
        DD = W[:, 12288:16384].rearrange("p (h c s n) -> p h c s n", h=HB, c=NT, s=2)
        ple_tile = [W[:, 8192 + k * D:8192 + (k + 1) * D] for k in range(KD)]

        QK = sb("QK", [P, KD, SEQ])
        X1 = QK[:, :, :].rearrange("p k n -> p (k n)").rearrange("p (t n) -> p t n", t=NT)
        ZT = sb("ZT", [P, NT, SEQ])
        S2 = sb("S2", [P, 3, SEQ])
        with ExitStack() as front:
            def sf(name, shape):
                return front.enter_context(nc.sbuf_tensor(name, shape, F32))

            XA = sf("XA", [P, KD, SEQ])
            MXA = sf("MXA", [P, 4, SEQ])
            PT = sf("PT", [P, 4, SEQ])
            DT = sf("DT", [P, 12, SEQ])
            VT = sf("VT", [P, NT, SEQ])
        w_hi = sb("w_hi", [P, 2, TW], F32R)
        w_lo = sb("w_lo", [P, 2, TW], F32R)
        xh, xl, ah, al = (sb(n, [P, KD, P], F32R) for n in ("xh", "xl", "ah", "al"))
        ET = sb("ET", [P, 4, FE])
        g_t, u_t, s_t, y_t = (ET[:, j, :] for j in range(4))
        MXB = XA[:, 0:4, :]
        ST = [XA[:, 4, :], XA[:, 5, :]]
        VN = XA[:, 6, :]
        YT = XA[:, 7, :]
        X1T = DT[:, 4:12, :]
        xg = ZT[:, 0:2, :].rearrange("p a n -> p (a n)")
        PJ = VT[:, :, :].rearrange("p a n -> p (a n)").rearrange("p (k n) -> p k n", k=2)
        LN = PT[:, :, :].rearrange("p a n -> p (a n)").rearrange("p (k n) -> p k n", k=2)
        LN2 = W[:, 8 * TW:9 * TW].rearrange("p (k n) -> p k n", k=2)
        C = sb("C", [P, C_TOTAL])
        ident = C[:, C_IDENT:C_IDENT + P]
        ones = C[:, C_ONES:C_ONES + P]
        upper = C[:, C_UPPER:C_UPPER + P]
        negm = C[:, C_NEGM:C_NEGM + P]
        strict = C[:, C_STRICT:C_STRICT + P]
        w_ba = sb("w_ba", [P, KD, 2 * HB])
        cw = sb("cw", [P, 12, 4])
        na = sb("na", [P, HB])
        dtb = sb("dtb", [P, HB])
        nw = sb("nw", [P, P])
        w_rt = sb("w_rt", [P, KD, NE])
        b_rt = sb("b_rt", [1, NE])
        b_dn = MXA[0:NE, 0:2, :].rearrange("p a n -> p (a n)")
        b_pg = MXA[0:1, 2:4, :].rearrange("p a n -> p (a n)")
        small = sb("small", [P, 512])
        cols = [small[:, j * 16:(j + 1) * 16] for j in range(32)]
        BA = small[:, 0:32]
        BETA, GG, GC, GL, EGC, EGL, EKD, BKE, XX, E1, SP1 = cols[2:13]
        nmax, den, rden = (small[:, 208 + 32 * j:240 + 32 * j] for j in range(3))
        MS, RSD = cols[19], cols[20]
        stat = small[:, 336:336 + 12]
        mv = small[:, 348:350]
        rstd = small[:, 350:352]
        junk = sb("junk", [P, P])
        eps_l2, eps_rms, eps_ln, one_c = (sb(n, [P, 1]) for n in ("eps_l2", "eps_rms", "eps_ln", "one_c"))
        s_ple = DT[:, 2:4, :]
        logit = sb("logit", [P, NT, NE])
        topv = sb("topv", [P, NT, 8])
        topi = sb("topi", [P, NT, 8], U32)
        topf = sb("topf", [P, NT, TOPK])
        gate = sb("gate", [P, NT, TOPK])
        gsum = sb("gsum", [P, NT, 1])
        memb = sb("memb", [P, NT, NE])
        onehot = S2[:, 2, :].rearrange("p (n e) -> p n e", e=NE)
        work = DT[:, 1, :].rearrange("p (n e) -> p n e", e=NE)
        rowf = sb("rowf", [P, NT * TOPK])
        rowi = sb("rowi", [P, NT * TOPK], U32)
        gmat = sb("gmat", [P, NT, NE])
        gT = XA[0:NE, 0, :]
        pay = sb("pay", [P, NT * TOPK, 4], I32)
        slots = sb("slots", [P, NE, 4], I32)
        xslot = sb("xslot", [P, 4], I32)
        extra_f = sb("extra_f", [P, 128])
        extra_i = sb("extra_i", [P, 64], I32)
        g_idx = sb("g_idx", [P, 1], I32)
        d_idx = sb("d_idx", [P, 2], I32)
        bias_t = S2[0:3, 0:2, :].rearrange("p a n -> p (a n)").bitcast(BF16)
        ones3 = sb("ones3", [3, P], BF16)
        PS = ctx.enter_context(nc.psum_tensor("PS", [P, 8, 512], F32))
        bank = [PS[:, b, :] for b in range(8)]

        ld_c, ld_xa, ld_xb, ld_small, ld_bgu = (sem(n) for n in ("ld_c", "ld_xa", "ld_xb", "ld_small", "ld_bgu"))
        ld_w = [sem(f"ld_w{j}") for j in range(NBLK)]
        ld_wout, ld_x, ld_ln, ld_pt, ld_pj, ld_pg, ld_ln2, ld_pb = (
            sem(n) for n in ("ld_wout", "ld_x", "ld_ln", "ld_pt", "ld_pj", "ld_pg", "ld_ln2", "ld_pb"))
        st_bias, st_table, st_x1, ld_slots = (sem(n) for n in ("st_bias", "st_table", "st_x1", "ld_slots"))
        ld_gu = [sem(f"ld_gu{k}") for k in range(KD)]
        ld_dn = [sem(f"ld_dn{q}") for q in range(KF // 2)]
        ld_bias, ld_xslot, ld_y, st_out = (sem(n) for n in ("ld_bias", "ld_xslot", "ld_y", "st_out"))
        (split_done, proj_done, evac_done, conv_done, ba_done, silu_done,
         sc_mm, sc_read, sc_exp, sc_max, p_norm, tr_mm, tr_evac, o_mm, o_evac,
         sq_done, nrm_mm, nrm_rs, nrm_done, gates_f, gc_mm, gsc_done,
         dp_bc, dp_arg, dp_kb, dp_e, dp_dec, dp_decs, dp_la, dp_lt, dp_tr, dp_kdec, dp_kbvb, dp_qdec,
         dd_ready, inv_a, inv_t1, inv_b, w_mm, w_evac,
         st_zero, scan_v, scan_vn, scan_s, scan_st, scan_o, rms_done, y_norm, y_gated, yt_mm, mix_ready,
         mix_mm, mix_read, ln_var, ln_rstd, ln_norm, x1_ready, xt_mm, xt_evac,
         rt_mm, rt_memb, pos_mm, route_exp, route_e, gm_ready, gT_mm, gT_evac, extra_ready,
         ple_mm, ple_sig, ple_read, rows_ready, tab_done,
         dch, ach, pch) = (sem(n) for n in (
            "split_done proj_done evac_done conv_done ba_done silu_done "
            "sc_mm sc_read sc_exp sc_max p_norm tr_mm tr_evac o_mm o_evac "
            "sq_done nrm_mm nrm_rs nrm_done gates_f gc_mm gsc_done "
            "dp_bc dp_arg dp_kb dp_e dp_dec dp_decs dp_la dp_lt dp_tr dp_kdec dp_kbvb dp_qdec "
            "dd_ready inv_a inv_t1 inv_b w_mm w_evac "
            "st_zero scan_v scan_vn scan_s scan_st scan_o rms_done y_norm y_gated yt_mm mix_ready "
            "mix_mm mix_read ln_var ln_rstd ln_norm x1_ready xt_mm xt_evac "
            "rt_mm rt_memb pos_mm route_exp route_e gm_ready gT_mm gT_evac extra_ready "
            "ple_mm ple_sig ple_read rows_ready tab_done dch ach pch").split())
        (xg_zero, gathered, xgt_mm, xh_ready, xl_ready, hi_ready, lo_ready, w_used, h_read, g_ready, sig_ready, u_ready, m_ready,
         act_ready, at_mm, ah_ready, al_ready, y_evac, y_sent, dg_ready, gi_ready,
         fin_mv, fin_rstd, fin_norm, fin_done, pool_steps) = (sem(n) for n in (
            "xg_zero gathered xgt_mm xh_ready xl_ready hi_ready lo_ready w_used h_read g_ready sig_ready u_ready m_ready "
            "act_ready at_mm ah_ready al_ready y_evac y_sent dg_ready gi_ready "
            "fin_mv fin_rstd fin_norm fin_done pool_steps").split())

        block = ctx.enter_context(nc.Block())
        w_in_k = w_in[0].rearrange("(k p) n -> p k n", p=P)
        w_out_k = w_out[0].rearrange("(k p) n -> p k n", p=P)
        w_pg_k = w_ple_gate[0].rearrange("(k p) n -> p k n", p=P)
        w_pj_k = w_ple_proj[0].rearrange("(k p) n -> p k n", p=P)
        gu_d = w_gate_up[0].rearrange("e (k p) n -> e k p n", p=P)
        dn_d = w_down[0].rearrange("e (q j p) n -> e q p j n", p=P, j=2)
        dn_raw = [W[:, (KD + q) * TW:(KD + q + 1) * TW] for q in range(KF // 2)]
        dn_pair = [t.rearrange("p (j n) -> p j n", j=2) for t in dn_raw]

        def gu_at(i):
            return 0 if isinstance(i, int) and i == 0 else i * BLOCK_TILES - KF // 2

        def dn_at(i):
            return i * BLOCK_TILES + KD + BLOCK_TILES - KF // 2

        DN_LAST = NE * BLOCK_TILES - KF // 2

        def extra_at(j):
            return j * BLOCK_TILES + NE * BLOCK_TILES

        def bank_free(eng, g):
            if g >= 2:
                f = g - 2
                if f < 12:
                    eng.wait_ge(evac_done, f + 1)
                elif f < 24:
                    eng.wait_ge(conv_done, f - 11)
                else:
                    eng.wait_ge(evac_done, f - 11)

        @block.sync
        def _(sp):
            sp.dma_start(XA[:, 0:4, :], xT[:, 0:4, :]).then_inc(ld_xa, 16)
            sp.dma_start(w_in_slot[0], w_in_k[:, :, 0:512]).then_inc(ld_w[0], 16)
            sp.dma_start(XA[:, 4:8, :], xT[:, 4:8, :]).then_inc(ld_xb, 16)
            sp.dma_start(w_in_slot[1], w_in_k[:, :, 512:1024]).then_inc(ld_w[1], 16)
            sp.dma_start(C[:, :], consts).then_inc(ld_c, 16)
            sp.dma_start(DT[0:NE, 0:4, :].rearrange("p a n -> p (a n)"), b_gate_up[0]).then_inc(ld_bgu, 16)
            sp.dma_start(w_in_slot[2], w_in_k[:, :, 1024:1536]).then_inc(ld_w[2], 16)
            sp.dma_start(w_ba[:, :, :], w_in_k[:, :, 3584:3592]).then_inc(ld_small, 16)
            sp.dma_start(cw[:, :, :], conv_w).then_inc(ld_small, 16)
            sp.dma_start(na[:, :], a_log.partition_broadcast(P)).then_inc(ld_small, 16)
            sp.dma_start(dtb[:, :], dt_bias.partition_broadcast(P)).then_inc(ld_small, 16)
            sp.dma_start(nw[:, :], gnorm_w.partition_broadcast(P)).then_inc(ld_small, 16)
            sp.dma_start(w_rt[:, :, :], w_router[0].rearrange("(k p) n -> p k n", p=P)).then_inc(ld_small, 16)
            sp.dma_start(b_rt[:, :], b_router).then_inc(ld_small, 16)
            sp.dma_start(pay[:, :, :].rearrange("p n w -> p (n w)"), pay0).then_inc(ld_small, 16)
            sp.dma_start(table.rearrange("(p r) w -> p (r w)", p=P), table0).then_inc(st_table, 16)
            for j in range(3, SLOTS):
                sp.dma_start(w_in_slot[j], w_in_k[:, :, j * 512:(j + 1) * 512]).then_inc(ld_w[j], 16)
            sp.wait_ge(split_done, 3)
            parts = DT[0:NE, 8:12, :].rearrange("p a n -> p (a n)").bitcast(BF16)
            sp.dma_start(bias_parts[:, 0, :], parts[:, 0:2 * FE]).then_inc(st_bias, 16)
            sp.dma_start(bias_parts[:, 1, :], parts[:, 2 * FE:4 * FE]).then_inc(st_bias, 16)
            low = DT[0:NE, 4:6, :].rearrange("p a n -> p (a n)").bitcast(BF16)
            sp.dma_start(bias_parts[:, 2, :], low[:, 0:2 * FE]).then_inc(st_bias, 16)
            sp.wait_ge(proj_done, 4)
            sp.dma_start(w_in_slot[0], w_in_k[:, :, 6 * 512:7 * 512]).then_inc(ld_w[6], 16)
            sp.wait_ge(proj_done, 24)
            sp.dma_start(W[:, 16384:24576].rearrange("p (k n) -> p k n", k=KD), w_out_k).then_inc(ld_wout, 16)
            sp.wait_ge(o_mm, HA)
            sp.dma_start(PJ, w_pj_k).then_inc(ld_pj, 16)
            sp.wait_ge(dp_la, HB)
            sp.wait_ge(dp_qdec, HB)
            sp.dma_start(X1, x.rearrange("(t p) n -> p t n", p=P)).then_inc(ld_x, 16)
            sp.wait_ge(dp_lt, 2 * HB)
            sp.dma_start(LN[:, 0, :], ln1_g.partition_broadcast(P)).then_inc(ld_ln, 16)
            sp.dma_start(LN[:, 1, :], ln1_b.partition_broadcast(P)).then_inc(ld_ln, 16)
            sp.dma_start(S2[:, 0:2, :], pT).then_inc(ld_pt, 16)
            sp.wait_ge(scan_o, NT)
            for k in range(KD):
                sp.dma_start(ple_tile[k], w_pg_k[:, k, :]).then_inc(ld_pg, 16)
            for k in range(4):
                sp.dma_start(gu_tile[k], gu_d[0, k]).then_inc(ld_gu[k], 16)
            for t in range(NT):
                sp.wait_ge(x1_ready, t + 1)
                sp.dma_start(x1_rows[t * P:(t + 1) * P, :], X1[:, t, :]).then_inc(st_x1, 16)
            sp.wait_ge(mix_mm, NT)
            sp.dma_start(b_pg, b_ple_gate).then_inc(ld_pb, 16)
            sp.dma_start(b_dn, b_down[0]).then_inc(ld_pb, 16)
            for q in range(KF // 2):
                sp.dma_start(dn_pair[q], dn_d[0, q]).then_inc(ld_dn[q], 16)
            sp.wait_ge(tab_done, 16 * NT * TOPK)
            sp.dma_start(slots[:, :, :], table.rearrange("(e c) w -> c e w", c=CAP)[0:P]).then_inc(ld_slots, 16)
            sp.wait_ge(ple_mm, NT)
            for k in range(4, KD):
                sp.dma_start(gu_tile[k], gu_d[0, k]).then_inc(ld_gu[k], 16)
            sp.wait_ge(st_bias, 48)
            sp.dma_start(bias_t, bias_parts[0]).then_inc(ld_bias, 16)

            def load_gate_up(e, before):
                for k in range(KD):
                    sp.wait_ge(lo_ready, before + k + 1)
                    sp.dma_start(gu_tile[k], gu_d[e, k]).then_inc(ld_gu[k], 16)
                    if k == 0:
                        sp.wait_ge(w_used, before + 1)
                        sp.dma_start(bias_t, bias_parts[e]).then_inc(ld_bias, 16)

            def load_down(e, before):
                for q in range(KF // 2):
                    sp.wait_ge(lo_ready, before + q + 1)
                    sp.dma_start(dn_pair[q], dn_d[e, q]).then_inc(ld_dn[q], 16)

            load_gate_up(1, 0)
            load_gate_up(2, gu_at(1))
            load_down(1, dn_at(0))
            with sp.Fori(2, NE - 1) as i:
                load_gate_up(i + 1, gu_at(i))
                load_down(i, dn_at(i - 1))
            load_down(NE - 1, dn_at(NE - 2))
            sp.wait_ge(extra_ready, 1)
            n_extra = sp.value_load(extra_i[0:1, 32:33], min_val=0, max_val=15)
            with sp.If(n_extra > 0):
                with sp.Fori(0, n_extra) as j:
                    e = sp.value_load(extra_i[0:1, bass.ds(j, 1)], min_val=0, max_val=NE - 1)
                    row = sp.value_load(extra_i[0:1, bass.ds(j + 16, 1)], min_val=0, max_val=NE * CAP - P)
                    sp.wait_ge(y_sent, (j + NE) * 16)
                    sp.dma_start(xslot[:, :], table[bass.ds(row, P), :]).then_inc(ld_xslot, 16)
                    load_gate_up(e, extra_at(j - 1))
                    load_down(e, extra_at(j - 1) + KD)
            sp.wait_ge(y_sent, (n_extra + NE) * 16)
            sp.dma_start(LN2[:, 0, :], ln2_g.partition_broadcast(P)).then_inc(ld_ln2, 16)
            sp.dma_start(LN2[:, 1, :], ln2_b.partition_broadcast(P)).then_inc(ld_ln2, 16)
            for t in range(NT):
                sp.dma_start(W[:, t * 4096:(t + 1) * 4096],
                             y_rows[t * P * TOPK:(t + 1) * P * TOPK, :].rearrange("(p k) n -> p (k n)", k=TOPK)
                             ).then_inc(ld_y, 16)
            for t in range(NT):
                sp.wait_ge(fin_done, t + 1)
                sp.dma_start(out[t * P:(t + 1) * P, :], X1[:, t, :]).then_inc(st_out, 16)
            sp.wait_ge(st_out, 16 * NT)

        @block.tensor
        def _(pe):
            mm, tr = nc.tensor.matmul, nc.tensor.transpose

            def project(g):
                blk, j = divmod(g, 4)
                if j == 0:
                    pe.wait_ge(ld_w[blk], 16)
                bank_free(pe, g)
                for k in range(KD):
                    if g == 0 and k == 4:
                        pe.wait_ge(ld_xb, 16)
                    w = w_in_slot[blk % SLOTS][:, k, :]
                    if blk in (2, 6):
                        last = mm(bank[g % 2], XA[:, k, j * P:(j + 1) * P], w, start=(k == 0), stop=(k == KD - 1))
                    else:
                        last = mm(bank[g % 2], w[:, j * P:(j + 1) * P], XA[:, k, :], start=(k == 0), stop=(k == KD - 1))
                last.then_inc(proj_done, 1)

            def scores(n):
                h, i = divmod(n, NT)
                r0, c = (h % 2) * EA, h // 2
                if n >= 2:
                    pe.wait_ge(sc_read, n - 1)
                mm(bank[2 + n % 2][:, 0:(i + 1) * P], QK[r0:r0 + EA, c, i * P:(i + 1) * P],
                   QK[r0:r0 + EA, 4 + c, 0:(i + 1) * P], start=True, stop=True).then_inc(sc_mm, 1)

            def transpose_probs(n):
                i = n % NT
                pe.wait_ge(p_norm, n + 1)
                if n >= 2:
                    pe.wait_ge(tr_evac, n - 1)
                for kt in range(i + 1):
                    last = tr(bank[4 + n % 2][:, kt * P:(kt + 1) * P], S2[:, n % 3, kt * P:(kt + 1) * P], ident)
                last.then_inc(tr_mm, 1)

            def attend(h):
                r0 = (h % 2) * EA
                pe.wait_ge(tr_evac, NT * (h + 1))
                if h:
                    pe.wait_ge(o_evac, h)
                for kt in range(NT):
                    last = mm(bank[6][r0:r0 + EA, kt * P:SEQ], VT[:, kt, h * EA:(h + 1) * EA],
                              PT[:, kt, kt * P:SEQ], start=(kt == 0), stop=(kt == NT - 1))
                last.then_inc(o_mm, 1)

            pe.wait_ge(ld_xa, 16)
            for g in range(12):
                project(g)
            pe.wait_ge(ld_small, 128)
            for t in range(NT):
                for k in range(KD):
                    last = mm(bank[7][:, t * 8:(t + 1) * 8], XA[:, k, t * P:(t + 1) * P], w_ba[:, k, :],
                              start=(k == 0), stop=(k == KD - 1))
            last.then_inc(ba_done, 1)
            pe.wait_ge(ld_c, 16)
            pe.wait_ge(evac_done, 12)
            for m in range(16):
                scores(2 * m)
                scores(2 * m + 1)
                if m >= 2 and m % 2 == 0:
                    attend(m // 2 - 1)
                project(12 + m)
                transpose_probs(2 * m)
                transpose_probs(2 * m + 1)
            attend(HA - 1)

            pe.wait_ge(gates_f, 1)
            mm(bank[7][:, 0:16], upper, GG, start=True, stop=True)
            mm(bank[7][:, 16:32], ones, GG, start=True, stop=True).then_inc(gc_mm, 1)
            for n in range(8):
                pe.wait_ge(sq_done, n + 1)
                if n >= 2:
                    pe.wait_ge(nrm_rs, n - 1)
                mm(bank[2 + n % 2], ones, S2[:, n % 2, :], start=True, stop=True).then_inc(nrm_mm, 1)
            pe.wait_ge(gsc_done, 1)
            pe.wait_ge(nrm_rs, 8)
            pe.wait_ge(evac_done, 16)
            pe.wait_ge(o_evac, HA)

            def spread(h):
                a = 4 * (h % 2)
                if h >= 2:
                    pe.wait_ge(dp_kdec, h - 1)
                    pe.wait_ge(dp_kbvb, h - 1)
                for t in range(NT):
                    mm(bank[a][:, t * P:(t + 1) * P], GG[:, t * HB + h:t * HB + h + 1].to_broadcast([P, P]), upper,
                       start=True, stop=True)
                    last = mm(bank[a + 1][:, t * P:(t + 1) * P],
                              BETA[:, t * HB + h:t * HB + h + 1].to_broadcast([P, P]), ident, start=True, stop=True)
                last.then_inc(dp_bc, 1)

            def grams(h):
                a = 4 * (h % 2)
                pe.wait_ge(nrm_done, 8)
                pe.wait_ge(dp_kb, h + 1)
                if h >= 2:
                    pe.wait_ge(dp_lt, 2 * (h - 1))
                for t in range(NT):
                    s = slice(t * P, (t + 1) * P)
                    mm(bank[a + 2][:, s], DT[:, 4 + h, s], QK[:, h, s], start=True, stop=True)
                    last = mm(bank[a + 3][:, s], DT[:, 4 + h, s], DT[:, h, s], start=True, stop=True)
                last.then_inc(dp_la, 1)
                pe.wait_ge(dp_arg, h + 1)
                pe.wait_ge(dp_e, h + 1)
                for t in range(NT):
                    s = slice(t * P, (t + 1) * P)
                    tr(bank[a][:, s], DT[:, 4 + h, s], ident)
                    last = tr(bank[a + 1][:, s], DT[:, 8 + h, s], ident)
                last.then_inc(dp_tr, 1)

            spread(0)
            spread(1)
            for h in range(HB):
                grams(h)
                if h + 2 < HB:
                    spread(h + 2)

            pe.wait_ge(dd_ready, HB)
            pe.wait_ge(dp_kdec, HB)
            pe.wait_ge(dp_kbvb, HB)
            pe.wait_ge(dp_lt, 2 * HB)

            with pe.Fori(0, LEVELS) as lv:
                def times_l(h):
                    pe.wait_ge(dd_ready, lv * HB + h + 1)
                    for c in range(NT):
                        last = mm(bank[3 * (h % 2)][:, c * P:(c + 1) * P], LT[:, h, c * P:(c + 1) * P],
                                  DD[:, h, c, 0, :], start=True, stop=True)
                    last.then_inc(inv_a, 1)

                def correct(h):
                    pe.wait_ge(inv_t1, lv * HB + h + 1)
                    pe.wait_ge(dd_ready, lv * HB + h + 3)
                    for c in range(NT):
                        b = bank[3 * (h % 2) + 1 + c // 2]
                        o = (c % 2) * 2 * P
                        mm(b[:, o:o + P], DD[:, h, c, 1, :], T1[:, h, c * P:(c + 1) * P], start=True, stop=True)
                        last = mm(b[:, o + P:o + 2 * P], T1[:, h, c * P:(c + 1) * P], DD[:, h, c, 1, :],
                                  start=True, stop=True)
                    last.then_inc(inv_b, 1)

                times_l(0)
                times_l(1)
                correct(0)
                times_l(2)
                correct(1)
                times_l(3)
                correct(2)
                correct(3)

            for h in range(HB):
                pe.wait_ge(dd_ready, LEVELS * HB + h + 1)
                if h >= 2:
                    pe.wait_ge(w_evac, h - 1)
                for c in range(NT):
                    last = mm(bank[6 + h % 2][:, c * P:(c + 1) * P], KB[:, h, c * P:(c + 1) * P], DD[:, h, c, 1, :],
                              start=True, stop=True)
                last.then_inc(w_mm, 1)
            pe.wait_ge(w_evac, HB)
            pe.wait_ge(st_zero, 1)
            pe.wait_ge(dp_qdec, HB)

            def scan(c):
                s = slice(c * P, (c + 1) * P)
                cur = ST[c % 2]
                if c:
                    pe.wait_ge(scan_st, HB * c)
                for h in range(HB):
                    hs = slice(h * P, (h + 1) * P)
                    mm(bank[0][:, hs], DD[:, h, c, 1, :], VB[:, h, s], start=True, stop=False)
                    last = mm(bank[0][:, hs], T1[:, h, s], cur[:, hs], start=False, stop=True)
                last.then_inc(scan_v, 1)
                pe.wait_ge(scan_vn, c + 1)
                for h in range(HB):
                    hs = slice(h * P, (h + 1) * P)
                    last = mm(bank[1][:, hs], KDEC[:, h, s], VN[:, hs], start=True, stop=True)
                last.then_inc(scan_s, 1)
                if c >= 2:
                    pe.wait_ge(y_norm, c - 1)
                for h in range(HB):
                    hs = slice(h * P, (h + 1) * P)
                    mm(bank[2 + c % 2][:, hs], DT[:, h, s], cur[:, hs], start=True, stop=False)
                    last = mm(bank[2 + c % 2][:, hs], AT[:, h, s], VN[:, hs], start=False, stop=True)
                last.then_inc(scan_o, 1)

            def y_transpose(c):
                pe.wait_ge(y_gated, c + 1)
                if c:
                    pe.wait_ge(mix_ready, c)
                for h in range(HB):
                    last = tr(bank[4][:, h * P:(h + 1) * P], YT[:, h * P:(h + 1) * P], ident)
                last.then_inc(yt_mm, 1)

            def mix(c):
                s = slice(c * P, (c + 1) * P)
                if c == 0:
                    pe.wait_ge(ld_wout, 16)
                else:
                    pe.wait_ge(mix_read, c)
                pe.wait_ge(mix_ready, c + 1)
                for half in range(2):
                    for k in range(KD):
                        y = MXA[:, k, s] if k < 4 else MXB[:, k - 4, s]
                        last = mm(bank[5 + half], y, dn_tile[k][:, half * 512:(half + 1) * 512],
                                  start=(k == 0), stop=(k == KD - 1))
                last.then_inc(mix_mm, 1)

            def x1_transpose(t):
                pe.wait_ge(x1_ready, t + 1)
                for q in range(2):
                    if t or q:
                        pe.wait_ge(xt_evac, 2 * t + q)
                    for j in range(4):
                        k = 4 * q + j
                        last = tr(bank[7][:, j * P:(j + 1) * P], X1[:, t, k * P:(k + 1) * P], ident)
                    last.then_inc(xt_mm, 1)

            scan(0)
            y_transpose(0)
            scan(1)
            y_transpose(1)
            mix(0)
            scan(2)
            y_transpose(2)
            mix(1)
            x1_transpose(0)
            scan(3)
            y_transpose(3)
            mix(2)
            x1_transpose(1)
            mix(3)
            x1_transpose(2)
            x1_transpose(3)

            pe.wait_ge(xt_evac, 2 * NT)
            for t in range(NT):
                for k in range(KD):
                    mm(bank[0][:, t * NE:(t + 1) * NE], X1T[:, k, t * P:(t + 1) * P], w_rt[:, k, :],
                       start=(k == 0), stop=False)
                last = mm(bank[0][:, t * NE:(t + 1) * NE], ones[0:1, :], b_rt[:, :], start=False, stop=True)
            last.then_inc(rt_mm, 1)

            def ple(t):
                s = slice(t * P, (t + 1) * P)
                if t == 0:
                    pe.wait_ge(ld_pg, 16 * KD)
                    pe.wait_ge(ld_pt, 16)
                    pe.wait_ge(ld_pj, 16)
                    pe.wait_ge(ld_pb, 32)
                    pe.wait_ge(gT_evac, 1)
                else:
                    pe.wait_ge(ple_sig, t)
                for half in range(2):
                    hs = slice(half * 512, (half + 1) * 512)
                    for k in range(KD):
                        mm(bank[2 + half], X1T[:, k, s], ple_tile[k][:, hs], start=(k == 0), stop=False)
                    mm(bank[2 + half], ones[0:1, :], b_pg[:, hs], start=False, stop=True)
                if t:
                    pe.wait_ge(ple_read, t)
                for half in range(2):
                    hs = slice(half * 512, (half + 1) * 512)
                    for k in range(2):
                        mm(bank[4 + half], S2[:, k, s], PJ[:, k, hs], start=(k == 0), stop=(k == 1))
                    last = mm(bank[6 + half], gT[:, s], b_dn[:, hs], start=True, stop=True)
                last.then_inc(ple_mm, 1)

            pe.wait_ge(rt_memb, 1)
            for t in range(NT):
                for s in range(t):
                    mm(bank[1][:, t * NE:(t + 1) * NE], ones, memb[:, s, :], start=(s == 0), stop=False)
                mm(bank[1][:, t * NE:(t + 1) * NE], strict, memb[:, t, :], start=(t == 0), stop=True)
            for s in range(NT):
                last = mm(bank[1][:, 4 * NE:5 * NE], ones, memb[:, s, :], start=(s == 0), stop=(s == NT - 1))
            last.then_inc(pos_mm, 1)
            pe.wait_ge(gm_ready, 1)
            for t in range(NT):
                last = tr(bank[0][0:NE, t * P:(t + 1) * P], gmat[:, t, :], ident)
            last.then_inc(gT_mm, 1)
            for t in range(NT):
                ple(t)

            def transpose_rows(i, src, done):
                for q in range(2):
                    for j in range(4):
                        k = 4 * q + j
                        last = tr(bank[6 + q][:, j * P:(j + 1) * P], src[:, k * P:(k + 1) * P], ident)
                last.then_inc(done, 1)

            def gate_up(i, at):
                pe.wait_ge(ld_bias, i * 16 + 16)
                pe.wait_ge(xl_ready, i + 1)
                if not isinstance(i, int) or i:
                    pe.wait_ge(h_read, i)
                for n in range(4):
                    mm(bank[n], ones3[:, :], bias_t[:, n * 512:(n + 1) * 512], start=True, stop=False)
                for k in range(KD):
                    pe.wait_ge(hi_ready, at + k + 1)
                    for x in (xh, xl):
                        for n in range(4):
                            mm(bank[n], x[:, k, :], w_hi[:, k % 2, n * 512:(n + 1) * 512], start=False, stop=False)
                    pe.wait_ge(lo_ready, at + k + 1)
                    for n in range(4):
                        last = mm(bank[n], xh[:, k, :], w_lo[:, k % 2, n * 512:(n + 1) * 512],
                                  start=False, stop=(k == KD - 1))
                    last.then_inc(w_used, 1)

            def down(i, at):
                pe.wait_ge(al_ready, i + 1)
                pe.wait_ge(y_evac, i + 1)
                for q in range(KF // 2):
                    pe.wait_ge(hi_ready, at + q + 1)
                    for j in range(2):
                        k = 2 * q + j
                        for a in (ah, al):
                            for n in range(2):
                                mm(bank[4 + n], a[:, k, :], w_hi[:, q % 2, j * FE + n * 512:j * FE + (n + 1) * 512],
                                   start=(k == 0 and a is ah), stop=False)
                    pe.wait_ge(lo_ready, at + q + 1)
                    for j in range(2):
                        k = 2 * q + j
                        for n in range(2):
                            last = mm(bank[4 + n], ah[:, k, :], w_lo[:, q % 2, j * FE + n * 512:j * FE + (n + 1) * 512],
                                      start=False, stop=(k == KF - 1))
                    last.then_inc(w_used, 1)

            def rows_in(i):
                pe.wait_ge(gathered, i * 16 + 16)
                if not isinstance(i, int) or i >= 2:
                    pe.wait_ge(al_ready, i - 1)
                transpose_rows(i, xg, xgt_mm)

            def acts(i, rows):
                pe.wait_ge(act_ready, i + 1)
                pe.wait_ge(xl_ready, rows)
                transpose_rows(i, g_t, at_mm)

            pe.wait_ge(ple_read, NT)
            rows_in(0)
            gate_up(0, gu_at(0))
            pe.wait_ge(xl_ready, 1)
            rows_in(1)
            acts(0, 2)
            with pe.Fori(1, NE - 1) as i:
                gate_up(i, gu_at(i))
                rows_in(i + 1)
                down(i - 1, dn_at(i - 1))
                acts(i, i + 2)
            gate_up(NE - 1, gu_at(NE - 1))
            down(NE - 2, dn_at(NE - 2))
            acts(NE - 1, NE)
            down(NE - 1, DN_LAST)
            pe.wait_ge(extra_ready, 1)
            n_extra = pe.value_load(extra_i[0:1, 32:33], min_val=0, max_val=15)
            with pe.If(n_extra > 0):
                with pe.Fori(0, n_extra) as j:
                    pe.wait_ge(al_ready, j + NE)
                    rows_in(j + NE)
                    gate_up(j + NE, extra_at(j))
                    acts(j + NE, j + NE + 1)
                    down(j + NE, extra_at(j) + KD)

        @block.scalar
        def _(act):
            A = nc.scalar.activation
            chain = [0]

            def link(ins):
                chain[0] += 1
                ins.then_inc(ach, 1)
                act.wait_ge(ach, chain[0])

            act.wait_ge(ld_small, 128)
            act.wait_ge(dch, 1)
            link(A(na[:, :], na[:, :], ACT.Exp))
            link(nc.scalar.mul(na[:, :], na[:, :], -1.0))
            for g in range(12):
                act.wait_ge(proj_done, g + 1)
                blk, j = divmod(g, 4)
                dst = (QK[:, j, :], QK[:, 4 + j, :], VT[:, j, :])[blk]
                A(dst, bank[g % 2], ACT.Copy).then_inc(evac_done, 1)

            def exps(n):
                i = n % NT
                act.wait_ge(sc_max, n + 1)
                s = S2[:, n % 3, 0:(i + 1) * P]
                A(s, s, ACT.Exp, bias=nmax[:, n:n + 1], accum_out=den[:, n:n + 1]).then_inc(sc_exp, 1)

            def evac_probs(n):
                h, i = divmod(n, NT)
                act.wait_ge(tr_mm, n + 1)
                if h:
                    act.wait_ge(o_mm, h)
                A(PT[:, 0:i + 1, i * P:(i + 1) * P],
                  bank[4 + n % 2][:, 0:(i + 1) * P].rearrange("p (k n) -> p k n", n=P), ACT.Copy).then_inc(tr_evac, 1)

            def evac_out(h):
                r0 = (h % 2) * EA
                act.wait_ge(o_mm, h + 1)
                A(MXA[r0:r0 + EA, h // 2, :], bank[6][r0:r0 + EA, :], ACT.Copy).then_inc(o_evac, 1)

            def silu(t, n):
                A(t, t, ACT.Silu).then_inc(silu_done, 1)

            for m in range(16):
                if m >= 1:
                    evac_probs(2 * m - 2)
                    evac_probs(2 * m - 1)
                exps(2 * m)
                exps(2 * m + 1)
                if m >= 2 and m % 2 == 0:
                    evac_out(m // 2 - 1)
                if m in (5, 9, 13):
                    b = (m - 5) // 4
                    act.wait_ge(conv_done, 4 * (b + 1))
                    silu(DT[:, 4 * b:4 * b + 4, :], 4)
                if m >= 13:
                    g = 12 + m - 1
                    act.wait_ge(proj_done, g + 1)
                    A(ZT[:, g - 24, :], bank[g % 2], ACT.Copy).then_inc(evac_done, 1)
            evac_probs(30)
            evac_probs(31)
            evac_out(HA - 1)
            act.wait_ge(proj_done, 28)
            A(ZT[:, 3, :], bank[27 % 2], ACT.Copy).then_inc(evac_done, 1)
            act.wait_ge(evac_done, 16)
            silu(ZT[:, :, :], 4)

            act.wait_ge(route_e, 1)
            A(E1, BETA, ACT.Exp, scale=-1.0).then_inc(route_exp, 1)
            link(A(SP1, SP1, ACT.Exp, scale=-1.0))
            A(SP1, SP1, ACT.Ln, bias=one_c[:, :]).then_inc(route_exp, 1)
            act.wait_ge(route_e, 2)
            A(EGC, GC, ACT.Exp).then_inc(route_exp, 1)
            A(EGL, GL, ACT.Exp).then_inc(route_exp, 1)
            A(EKD, EKD, ACT.Exp).then_inc(route_exp, 1)

            for n in range(8):
                act.wait_ge(nrm_mm, n + 1)
                if n >= 2:
                    act.wait_ge(nrm_done, n - 1)
                if n == 0:
                    act.wait_ge(o_mm, HA)
                A(PT[:, n % 2, :], bank[2 + n % 2], ACT.Ln, bias=eps_l2[:, :]).then_inc(ach, 1)
                chain[0] += 1
                act.wait_ge(ach, chain[0])
                A(PT[:, n % 2, :], PT[:, n % 2, :], ACT.Exp, scale=-0.5).then_inc(nrm_rs, 1)
            def spread_exp(h):
                a = 4 * (h % 2)
                act.wait_ge(dp_bc, h + 1)
                A(QK[:, 4 + h, :], bank[a], ACT.Exp).then_inc(dp_e, 1)
                act.wait_ge(dp_arg, h + 1)
                A(PT[:, h, :], PT[:, h, :], ACT.Exp).then_inc(dp_dec, 1)

            def evac_v(h):
                a = 4 * (h % 2)
                act.wait_ge(dp_tr, h + 1)
                for t in range(NT):
                    s = slice(t * P, (t + 1) * P)
                    j = t * HB + h
                    last = A(VB[:, h, s], bank[a + 1][:, s], ACT.Copy, scale=BETA[:, j:j + 1])
                last.then_inc(dp_kbvb, 1)

            act.wait_ge(gsc_done, 1)
            spread_exp(0)
            spread_exp(1)
            for h in range(HB):
                evac_v(h)
                if h + 2 < HB:
                    spread_exp(h + 2)
            for h in range(HB):
                act.wait_ge(w_mm, h + 1)
                A(T1[:, h, :], bank[6 + h % 2], ACT.Copy, scale=-1.0).then_inc(w_evac, 1)

            def scan_evac(c):
                act.wait_ge(scan_v, c + 1)
                A(VN, bank[0], ACT.Copy).then_inc(scan_vn, 1)

            def rms(c):
                act.wait_ge(scan_o, c + 1)
                for h in range(HB):
                    last = A(junk[:, :], bank[2 + c % 2][:, h * P:(h + 1) * P], ACT.Square,
                             accum_out=MS[:, c * HB + h:c * HB + h + 1])
                    link(last)
                s = slice(c * HB, (c + 1) * HB)
                link(A(RSD[:, s], MS[:, s], ACT.Ln, scale=1.0 / P, bias=eps_rms[:, :]))
                A(RSD[:, s], RSD[:, s], ACT.Exp, scale=-0.5).then_inc(rms_done, 1)

            def y_evac_t(c):
                act.wait_ge(yt_mm, c + 1)
                A(MXB[:, :, c * P:(c + 1) * P], bank[4].rearrange("p (h n) -> p h n", n=P),
                  ACT.Copy).then_inc(mix_ready, 1)

            def ln_scale(t, ready, done):
                act.wait_ge(ready, t + 1)
                link(A(rstd[:, 0:1], mv[:, 1:2], ACT.Ln, bias=eps_ln[:, :]))
                A(rstd[:, 1:2], rstd[:, 0:1], ACT.Exp, scale=-0.5).then_inc(done, 1)

            def x1_evac(t):
                for q in range(2):
                    act.wait_ge(xt_mm, 2 * t + q + 1)
                    A(X1T[:, 4 * q:4 * q + 4, t * P:(t + 1) * P], bank[7].rearrange("p (k n) -> p k n", n=P),
                      ACT.Copy).then_inc(xt_evac, 1)

            for c in range(3):
                scan_evac(c)
                rms(c)
                y_evac_t(c)
            ln_scale(0, ln_var, ln_rstd)
            x1_evac(0)
            scan_evac(3)
            rms(3)
            y_evac_t(3)
            ln_scale(1, ln_var, ln_rstd)
            x1_evac(1)
            ln_scale(2, ln_var, ln_rstd)
            ln_scale(3, ln_var, ln_rstd)
            x1_evac(2)
            x1_evac(3)
            act.wait_ge(route_e, 3)
            A(gate[:, :, :], gate[:, :, :], ACT.Exp).then_inc(route_exp, 1)
            act.wait_ge(gT_mm, 1)
            A(gT, bank[0][0:NE, :], ACT.Copy).then_inc(gT_evac, 1)
            for t in range(NT):
                act.wait_ge(ple_mm, t + 1)
                if t:
                    act.wait_ge(ple_read, t)
                A(s_ple, PS[:, 2:4, :], ACT.Sigmoid).then_inc(ple_sig, 1)

            six_seven = PS[:, 6:8, :].rearrange("p b n -> p (b n)").rearrange("p (k n) -> p k n", k=KD)

            def rows_out(i):
                act.wait_ge(xgt_mm, i + 1)
                A(xh[:, :, :], six_seven, ACT.Copy).then_inc(xh_ready, 1)

            def sigmoid(i):
                act.wait_ge(g_ready, i + 1)
                A(s_t, g_t, ACT.Sigmoid, scale=1.702).then_inc(sig_ready, 1)

            def acts_out(i):
                act.wait_ge(at_mm, i + 1)
                A(ah[:, :, :], six_seven, ACT.Copy).then_inc(ah_ready, 1)

            def y_out(i, at):
                act.wait_ge(w_used, at + KF // 2)
                act.wait_ge(dg_ready, i + 1)
                A(y_t, PS[:, 4:6, :].rearrange("p b n -> p (b n)"), ACT.Copy,
                  scale=d_idx[:, 1:2].bitcast(F32)).then_inc(y_evac, 1)

            def hi_parts(i, raws, loads, at, first, last):
                for k in range(first, last):
                    act.wait_ge(loads[k], i * 16 + 16)
                    if not isinstance(at, int) or at + k >= 2:
                        act.wait_ge(w_used, at + k - 1)
                    A(w_hi[:, k % 2, :], raws[k], ACT.Copy).then_inc(hi_ready, 1)

            def hi_gu(i, at, first, last):
                hi_parts(i, gu_tile, ld_gu, at, first, last)

            def hi_dn(i, at, first, last):
                hi_parts(i, dn_raw, ld_dn, at, first, last)

            act.wait_ge(ple_read, NT)
            A(junk[:, 0:1], eps_ln[:, :], ACT.Copy).then_inc(y_evac, 1)
            rows_out(0)
            hi_gu(0, gu_at(0), 0, KD)
            rows_out(1)
            sigmoid(0)

            def turn(i, rows=True, y=True):
                hi_gu(i, gu_at(i), 0, 2)
                if y:
                    y_out(i - 2, dn_at(i - 2))
                acts_out(i - 1)
                hi_gu(i, gu_at(i), 2, KD)
                hi_dn(i - 1, dn_at(i - 1), 0, 2)
                if rows:
                    rows_out(i + 1)
                sigmoid(i)
                hi_dn(i - 1, dn_at(i - 1), 2, 4)

            turn(1, y=False)
            with act.Fori(2, NE - 1) as i:
                turn(i)
            turn(NE - 1, rows=False)
            hi_dn(NE - 1, DN_LAST, 0, 2)
            y_out(NE - 2, dn_at(NE - 2))
            acts_out(NE - 1)
            hi_dn(NE - 1, DN_LAST, 2, 4)
            y_out(NE - 1, DN_LAST)
            act.wait_ge(extra_ready, 1)
            n_extra = act.value_load(extra_i[0:1, 32:33], min_val=0, max_val=15)
            with act.If(n_extra > 0):
                with act.Fori(0, n_extra) as j:
                    rows_out(j + NE)
                    hi_gu(j + NE, extra_at(j), 0, KD)
                    sigmoid(j + NE)
                    acts_out(j + NE)
                    hi_dn(j + NE, extra_at(j) + KD, 0, 4)
                    y_out(j + NE, extra_at(j) + KD)
            for t in range(NT):
                ln_scale(t, fin_mv, fin_rstd)

        @block.vector
        def _(dve):
            V = nc.vector
            chain = [0]

            def link(ins):
                chain[0] += 1
                ins.then_inc(dch, 1)
                dve.wait_ge(dch, chain[0])

            V.memset(eps_l2[:, :], L2_EPS)
            V.memset(eps_rms[:, :], RMS_EPS)
            V.memset(eps_ln[:, :], LN_EPS)
            V.memset(one_c[:, :], 1.0)
            link(V.memset(ones3[:, :], 1.0))
            dve.wait_ge(ld_bgu, 16)
            b32 = DT[0:NE, 0:4, :].rearrange("p a n -> p (a n)")
            rest = DT[0:NE, 4:8, :].rearrange("p a n -> p (a n)")
            parts = DT[0:NE, 8:12, :].rearrange("p a n -> p (a n)").bitcast(BF16)
            hi, mid = parts[:, 0:2 * FE], parts[:, 2 * FE:4 * FE]
            low = DT[0:NE, 4:6, :].rearrange("p a n -> p (a n)").bitcast(BF16)
            link(V.tensor_copy(hi, b32))
            link(V.tensor_tensor(rest, b32, hi, ALU.subtract))
            link(V.tensor_copy(mid, rest))
            link(V.tensor_tensor(b32, rest, mid, ALU.subtract))
            V.tensor_copy(low, b32).then_inc(split_done, 3)
            dve.wait_ge(ba_done, 1)
            link(V.tensor_copy(BA, bank[7][:, 0:32]))
            ba = BA.rearrange("p (t c) -> p t c", c=8)
            xx = XX.rearrange("p (t h) -> p t h", h=HB)
            V.tensor_copy(BETA.rearrange("p (t h) -> p t h", h=HB), ba[:, :, 0:HB])
            link(V.tensor_tensor(xx, ba[:, :, HB:8], dtb[:, :].unsqueeze(1).to_broadcast([P, NT, HB]), ALU.add))
            V.scalar_tensor_tensor(SP1, XX, -1.0, XX, ALU.mult, ALU.max).then_inc(route_e, 1)

            def score(n):
                i = n % NT
                w = (i + 1) * P
                dve.wait_ge(sc_mm, n + 1)
                if n >= 3:
                    dve.wait_ge(tr_mm, n - 2)
                s = S2[:, n % 3, 0:w]
                V.scalar_tensor_tensor(s, bank[2 + n % 2][:, 0:w], EA ** -0.5,
                                       C[:, C_STRIP + P * (NT - 1 - i):C_STRIP + SEQ],
                                       ALU.mult, ALU.add).then_inc(sc_read, 1)
                dve.wait_ge(sc_read, n + 1)
                V.tensor_reduce(nmax[:, n:n + 1], s, AX.X, ALU.max, negate=True).then_inc(sc_max, 1)

            def normalise(n):
                i = n % NT
                dve.wait_ge(sc_exp, n + 1)
                link(V.reciprocal(rden[:, n:n + 1], den[:, n:n + 1]))
                s = S2[:, n % 3, 0:(i + 1) * P]
                V.tensor_scalar(s, s, rden[:, n:n + 1], None, ALU.mult).then_inc(p_norm, 1)

            def conv(c):
                g = 12 + c
                dve.wait_ge(proj_done, g + 1)
                src, dst = bank[g % 2], DT[:, c, :]
                link(V.tensor_scalar(dst, src, cw[:, c, 3:4], None, ALU.mult))
                for back in range(1, 4):
                    ins = V.scalar_tensor_tensor(dst[:, back:SEQ], src[:, 0:SEQ - back], cw[:, c, 3 - back:4 - back],
                                                 dst[:, back:SEQ], ALU.mult, ALU.add)
                    if back < 3:
                        link(ins)
                ins.then_inc(conv_done, 1)

            dve.wait_ge(ld_c, 16)
            for m in range(16):
                score(2 * m)
                score(2 * m + 1)
                if 1 <= m <= 12:
                    if m == 1:
                        dve.wait_ge(st_bias, 48)
                    conv(m - 1)
                normalise(2 * m)
                normalise(2 * m + 1)

            dve.wait_ge(route_exp, 2)
            link(V.tensor_scalar(E1, E1, 1.0, None, ALU.add))
            V.reciprocal(BETA, E1)
            link(V.scalar_tensor_tensor(SP1, XX, 0.0, SP1, ALU.max, ALU.add))
            V.tensor_tensor(GG.rearrange("p (t h) -> p t h", h=HB), SP1.rearrange("p (t h) -> p t h", h=HB),
                            na[:, :].unsqueeze(1).to_broadcast([P, NT, HB]), ALU.mult).then_inc(gates_f, 1)
            dve.wait_ge(gc_mm, 1)
            V.tensor_copy(GC, bank[7][:, 0:16])
            link(V.tensor_copy(GL, bank[7][:, 16:32]))
            V.tensor_tensor(EKD, GL, GC, ALU.subtract).then_inc(route_e, 1)
            dve.wait_ge(route_exp, 5)
            V.tensor_tensor(BKE, BETA, EGC, ALU.mult).then_inc(gsc_done, 1)
            for n in range(8):
                dve.wait_ge(nrm_rs, n + 1)
                d = DT[:, n, :]
                V.scalar_tensor_tensor(d, d, P ** -0.5 if n < HB else 1.0, PT[:, n % 2, :],
                                       ALU.mult, ALU.mult).then_inc(nrm_done, 1)
            dve.wait_ge(nrm_done, 8)

            def decays(h):
                a = 4 * (h % 2)
                dve.wait_ge(dp_e, h + 1)
                for t in range(NT):
                    s = slice(t * P, (t + 1) * P)
                    last = V.scalar_tensor_tensor(PT[:, h, s], bank[a][:, s], GC[:, t * HB + h:t * HB + h + 1], negm,
                                                  ALU.subtract, ALU.add)
                last.then_inc(dp_arg, 1)
                V.tensor_tensor(QK[:, h, :], DT[:, 4 + h, :], bank[a + 1], ALU.mult).then_inc(dp_kb, 1)

            def grams(h):
                a = 4 * (h % 2)
                dve.wait_ge(dp_la, h + 1)
                dve.wait_ge(dp_decs, h + 1)
                V.tensor_tensor(LT[:, h, :], bank[a + 2], S2[:, h % 2, :], ALU.mult).then_inc(dp_lt, 1)
                V.tensor_tensor(AT[:, h, :], bank[a + 3], PT[:, h, :], ALU.mult).then_inc(dp_lt, 1)
                dve.wait_ge(dp_tr, h + 1)
                for t in range(NT):
                    s = slice(t * P, (t + 1) * P)
                    last = V.tensor_scalar(KDEC[:, h, s], bank[a][:, s], EKD[:, t * HB + h:t * HB + h + 1], None,
                                           ALU.mult)
                    last = V.tensor_scalar(KB[:, h, s], bank[a][:, s], BKE[:, t * HB + h:t * HB + h + 1], None,
                                           ALU.mult)
                last.then_inc(dp_kdec, 1)

            dve.wait_ge(gsc_done, 1)
            decays(0)
            decays(1)
            for h in range(HB):
                grams(h)
                if h + 2 < HB:
                    decays(h + 2)

            dve.wait_ge(dd_ready, HB)
            with dve.Fori(0, LEVELS) as lv:
                level = C[:, bass.ds(lv * P + C_LEVEL, P)].unsqueeze(1).to_broadcast([P, NT, P])

                def mask_t1(h):
                    dve.wait_ge(inv_a, lv * HB + h + 1)
                    V.tensor_tensor(T1[:, h, :].rearrange("p (c n) -> p c n", n=P),
                                    bank[3 * (h % 2)].rearrange("p (c n) -> p c n", n=P), level,
                                    ALU.mult).then_inc(inv_t1, 1)

                def update(h):
                    dve.wait_ge(inv_b, lv * HB + h + 1)
                    b = 3 * (h % 2) + 1
                    d = DD[:, h, :, :, :].rearrange("p c s n -> p (c s n)")
                    V.tensor_tensor(d, d, PS[:, b:b + 2, :].rearrange("p b n -> p (b n)"),
                                    ALU.subtract).then_inc(dd_ready, 1)

                mask_t1(0)
                mask_t1(1)
                update(0)
                mask_t1(2)
                update(1)
                mask_t1(3)
                update(2)
                update(3)

            def state(c):
                dve.wait_ge(scan_s, c + 1)
                for h in range(HB):
                    hs = slice(h * P, (h + 1) * P)
                    V.scalar_tensor_tensor(ST[(c + 1) % 2][:, hs], ST[c % 2][:, hs],
                                           EGL[:, c * HB + h:c * HB + h + 1], bank[1][:, hs],
                                           ALU.mult, ALU.add).then_inc(scan_st, 1)
                dve.wait_ge(scan_st, HB * (c + 1))

            def y_scale(c):
                dve.wait_ge(rms_done, c + 1)
                if c:
                    dve.wait_ge(yt_mm, c)
                for h in range(HB):
                    hs = slice(h * P, (h + 1) * P)
                    last = V.scalar_tensor_tensor(YT[:, hs], bank[2 + c % 2][:, hs],
                                                  RSD[:, c * HB + h:c * HB + h + 1], nw[:, :], ALU.mult, ALU.mult)
                last.then_inc(y_norm, 1)

            def layer_norm(t, ready, scaled, after):
                row = X1[:, t, :]
                V.bn_stats(stat[:, 0:6], row[:, 0:512])
                link(V.bn_stats(stat[:, 6:12], row[:, 512:1024]))
                V.bn_aggr(mv, stat).then_inc(ready, 1)
                dve.wait_ge(ready, t + 1)
                dve.wait_ge(scaled, t + 1)
                V.tensor_scalar(row, row, mv[:, 0:1], rstd[:, 1:2], ALU.subtract, ALU.mult).then_inc(after, 1)
                dve.wait_ge(after, t + 1)

            def residual(c):
                dve.wait_ge(mix_mm, c + 1)
                if c == 0:
                    dve.wait_ge(ld_x, 16)
                V.scalar_tensor_tensor(X1[:, c, :], X1[:, c, :], ALPHA, PS[:, 5:7, :].rearrange("p b n -> p (b n)"),
                                       ALU.mult, ALU.add).then_inc(mix_read, 1)
                dve.wait_ge(mix_read, c + 1)
                layer_norm(c, ln_var, ln_rstd, ln_norm)

            state(0)
            y_scale(0)
            state(1)
            y_scale(1)
            state(2)
            y_scale(2)
            residual(0)
            y_scale(3)
            residual(1)
            residual(2)
            residual(3)

            dve.wait_ge(rt_mm, 1)
            link(V.tensor_copy(logit[:, :, :].rearrange("p t e -> p (t e)"), bank[0][:, 0:NT * NE]))
            for t in range(NT):
                link(V.max(topv[:, t, :], logit[:, t, :]))
                last = V.max_index(topi[:, t, :], topv[:, t, :], logit[:, t, :])
            link(last)
            link(V.tensor_copy(topf[:, :, :], topi[:, :, 0:TOPK]))
            V.tensor_tensor(gate[:, :, :], topv[:, :, 0:TOPK], topv[:, :, 0:1].to_broadcast([P, NT, TOPK]),
                            ALU.subtract).then_inc(route_e, 1)
            esel = C[:, C_ESEL:C_ESEL + NE]
            ebase = C[:, C_EBASE:C_EBASE + NE]
            n_tk = NT * TOPK
            link(V.tensor_tensor(onehot, esel.unsqueeze(1).to_broadcast([P, n_tk, NE]),
                                 topf[:, :, :].rearrange("p t k -> p (t k)").unsqueeze(2).to_broadcast([P, n_tk, NE]),
                                 ALU.is_equal))
            V.tensor_reduce(memb[:, :, :], onehot.rearrange("p (t k) e -> p t e k", k=TOPK), AX.X,
                            ALU.add).then_inc(rt_memb, 1)
            dve.wait_ge(route_exp, 6)
            link(V.tensor_reduce(gsum[:, :, 0], gate[:, :, :], AX.X, ALU.add))
            link(V.reciprocal(gsum[:, :, 0], gsum[:, :, 0]))
            link(V.tensor_tensor(gate[:, :, :], gate[:, :, :], gsum[:, :, :].to_broadcast([P, NT, TOPK]), ALU.mult))
            gate_f = gate[:, :, :].rearrange("p t k -> p (t k)").unsqueeze(2)
            V.tensor_copy(pay[:, :, 2:3].bitcast(F32), gate_f)
            link(V.tensor_tensor(work, onehot, gate_f.to_broadcast([P, n_tk, NE]), ALU.mult))
            V.tensor_reduce(gmat[:, :, :], work.rearrange("p (t k) e -> p t e k", k=TOPK), AX.X,
                            ALU.add).then_inc(gm_ready, 1)
            dve.wait_ge(pos_mm, 1)
            dve.wait_ge(gm_ready, 1)
            link(V.tensor_tensor(logit[:, :, :], bank[1][:, 0:NT * NE].rearrange("p (t e) -> p t e", e=NE),
                                 ebase.unsqueeze(1).to_broadcast([P, NT, NE]), ALU.add))
            for t in range(NT):
                ks = slice(t * TOPK, (t + 1) * TOPK)
                last = V.tensor_tensor(work[:, ks, :], onehot[:, ks, :],
                                       logit[:, t, :].unsqueeze(1).to_broadcast([P, TOPK, NE]), ALU.mult)
            link(last)
            link(V.tensor_reduce(rowf[:, :], work, AX.X, ALU.add))
            V.tensor_copy(rowi[:, :], rowf[:, :]).then_inc(rows_ready, 1)
            count = bank[1][:, NT * NE:(NT + 1) * NE]
            more, upto = extra_f[:, 0:NE], extra_f[:, NE:2 * NE]
            xe, xs = extra_f[:, 64:80], extra_f[:, 80:96]
            jj = C[:, C_ESEL:C_ESEL + 16]
            link(V.tensor_scalar(more, count, float(P), None, ALU.is_gt))
            link(V.scalar_tensor_tensor(more, count, 2.0 * P, more, ALU.is_gt, ALU.add))
            link(V.scalar_tensor_tensor(more, count, 3.0 * P, more, ALU.is_gt, ALU.add))
            link(V.tensor_tensor_scan(upto, ones[:, 0:NE], more, 0.0, ALU.mult, ALU.add))
            link(V.tensor_tensor(work, upto.unsqueeze(1).to_broadcast([P, 16, NE]),
                                 jj.unsqueeze(2).to_broadcast([P, 16, NE]), ALU.is_le))
            link(V.tensor_reduce(xe, work, AX.X, ALU.add))
            link(V.tensor_tensor(work, work, more.unsqueeze(1).to_broadcast([P, 16, NE]), ALU.mult))
            link(V.tensor_reduce(xs, work, AX.X, ALU.add))
            link(V.tensor_scalar(xe, xe, float(NE - 1), None, ALU.min))
            link(V.tensor_tensor(xs, jj, xs, ALU.subtract))
            link(V.tensor_scalar(xs, xs, 1.0, float(P), ALU.add, ALU.mult))
            link(V.scalar_tensor_tensor(xs, xe, float(CAP), xs, ALU.mult, ALU.add))
            link(V.tensor_scalar(xs, xs, float(NE * CAP - P), None, ALU.min))
            V.tensor_copy(extra_i[:, 0:16], xe)
            V.tensor_copy(extra_i[:, 16:32], xs)
            V.tensor_copy(extra_i[:, 32:33], upto[:, NE - 1:NE]).then_inc(extra_ready, 1)

            dve.wait_ge(st_x1, 16 * NT)
            for t in range(NT):
                dve.wait_ge(ple_sig, t + 1)
                link(V.tensor_tensor(s_ple, s_ple, PS[:, 4:6, :], ALU.mult))
                row = X1[:, t, :].rearrange("p (b n) -> p b n", b=2)
                link(V.scalar_tensor_tensor(row, row, ALPHA, s_ple, ALU.mult, ALU.add))
                V.tensor_tensor(row, row, PS[:, 6:8, :], ALU.add).then_inc(ple_read, 1)

            six_seven = PS[:, 6:8, :].rearrange("p b n -> p (b n)").rearrange("p (k n) -> p k n", k=KD)

            def lo_parts(raws, at, first, last):
                for k in range(first, last):
                    dve.wait_ge(hi_ready, at + k + 1)
                    V.tensor_tensor(w_lo[:, k % 2, :], raws[k], w_hi[:, k % 2, :].bitcast(F32),
                                    ALU.subtract).then_inc(lo_ready, 1)

            def clamp(i, at):
                dve.wait_ge(w_used, at + KD)
                if not isinstance(i, int) or i:
                    dve.wait_ge(at_mm, i)
                V.tensor_scalar(g_t, PS[:, 0:2, :].rearrange("p b n -> p (b n)"), 7.0, None,
                                ALU.min).then_inc(g_ready, 1)
                V.tensor_scalar(u_t, PS[:, 2:4, :].rearrange("p b n -> p (b n)"), 7.0, -7.0,
                                ALU.min, ALU.max).then_inc(h_read, 1)
                dve.wait_ge(sig_ready, i + 1)
                V.tensor_tensor(s_t, g_t, s_t, ALU.mult).then_inc(m_ready, 1)

            def swiglu(i):
                dve.wait_ge(h_read, i + 1)
                dve.wait_ge(m_ready, i + 1)
                V.scalar_tensor_tensor(g_t, u_t, 1.0, s_t, ALU.add, ALU.mult).then_inc(act_ready, 1)

            def rows_rest(i):
                dve.wait_ge(xh_ready, i + 1)
                V.tensor_tensor(xl[:, :, :], six_seven, xh[:, :, :].bitcast(F32), ALU.subtract).then_inc(xl_ready, 1)

            def acts_rest(i):
                dve.wait_ge(ah_ready, i + 1)
                V.tensor_tensor(al[:, :, :], six_seven, ah[:, :, :].bitcast(F32), ALU.subtract).then_inc(al_ready, 1)

            dve.wait_ge(ple_read, NT)
            rows_rest(0)
            lo_parts(gu_tile, gu_at(0), 0, KD)
            rows_rest(1)
            clamp(0, gu_at(0))
            swiglu(0)

            def turn(i, rows=True):
                lo_parts(gu_tile, gu_at(i), 0, 2)
                acts_rest(i - 1)
                lo_parts(gu_tile, gu_at(i), 2, KD)
                lo_parts(dn_raw, dn_at(i - 1), 0, 2)
                clamp(i, gu_at(i))
                lo_parts(dn_raw, dn_at(i - 1), 2, 3)
                swiglu(i)
                if rows:
                    rows_rest(i + 1)
                lo_parts(dn_raw, dn_at(i - 1), 3, 4)

            with dve.Fori(1, NE - 1) as i:
                turn(i)
            turn(NE - 1, rows=False)
            lo_parts(dn_raw, DN_LAST, 0, 2)
            acts_rest(NE - 1)
            lo_parts(dn_raw, DN_LAST, 2, 4)
            dve.wait_ge(extra_ready, 1)
            n_extra = dve.value_load(extra_i[0:1, 32:33], min_val=0, max_val=15)
            with dve.If(n_extra > 0):
                with dve.Fori(0, n_extra) as j:
                    rows_rest(j + NE)
                    lo_parts(gu_tile, extra_at(j), 0, KD)
                    clamp(j + NE, extra_at(j))
                    swiglu(j + NE)
                    acts_rest(j + NE)
                    lo_parts(dn_raw, extra_at(j) + KD, 0, 4)
            for t in range(NT):
                dve.wait_ge(ld_y, 16 * NT)
                for k in range(TOPK):
                    link(V.tensor_tensor(X1[:, t, :], X1[:, t, :], W[:, t * 4096 + k * D:t * 4096 + (k + 1) * D], ALU.add))
                layer_norm(t, fin_mv, fin_rstd, fin_norm)

        @block.gpsimd
        def _(pool):
            G = nc.gpsimd
            pool.wait_ge(proj_done, 28)
            G.memset(ST[0], 0.0).then_inc(st_zero, 1)
            pool.wait_ge(ld_c, 16)
            for h in range(HB):
                G.tensor_copy(DD[:, h, :, :, :].rearrange("p c s n -> p (c s) n"),
                              ident.unsqueeze(1).to_broadcast([P, 2 * NT, P])).then_inc(dd_ready, 1)
            pool.wait_ge(tr_mm, HA * NT)
            for n in range(8):
                pool.wait_ge(silu_done, 1 + n // 4)
                if n >= 2:
                    pool.wait_ge(nrm_mm, n - 1)
                G.tensor_tensor(S2[:, n % 2, :], DT[:, n, :], DT[:, n, :], ALU.mult).then_inc(sq_done, 1)

            def strict_decay(h):
                pool.wait_ge(dp_dec, h + 1)
                if h >= 2:
                    pool.wait_ge(dp_lt, 2 * (h - 1))
                G.tensor_tensor(S2[:, h % 2, :].rearrange("p (c n) -> p c n", n=P),
                                PT[:, h, :].rearrange("p (c n) -> p c n", n=P),
                                strict.unsqueeze(1).to_broadcast([P, NT, P]), ALU.mult).then_inc(dp_decs, 1)

            def decay_q(h):
                pool.wait_ge(dp_la, h + 1)
                pool.wait_ge(dp_e, h + 1)
                G.tensor_tensor(DT[:, h, :], DT[:, h, :], QK[:, 4 + h, :], ALU.mult).then_inc(dp_qdec, 1)

            pool.wait_ge(nrm_mm, 8)
            pool.wait_ge(nrm_done, 8)
            strict_decay(0)
            strict_decay(1)
            for h in range(HB):
                decay_q(h)
                if h + 2 < HB:
                    strict_decay(h + 2)

            def gate_y(c):
                pool.wait_ge(y_norm, c + 1)
                G.tensor_tensor(YT, YT, ZT[:, c, :], ALU.mult).then_inc(y_gated, 1)

            def affine(t, normed, done, scale, shift, step):
                pool.wait_ge(normed, t + 1)
                G.tensor_tensor(X1[:, t, :], X1[:, t, :], scale, ALU.mult).then_inc(pch, 1)
                pool.wait_ge(pch, step)
                G.tensor_tensor(X1[:, t, :], X1[:, t, :], shift, ALU.add).then_inc(done, 1)

            pool.wait_ge(silu_done, 4)
            gate_y(0)
            gate_y(1)
            gate_y(2)
            pool.wait_ge(ld_ln, 32)
            affine(0, ln_norm, x1_ready, LN[:, 0, :], LN[:, 1, :], 1)
            gate_y(3)
            for t in range(1, NT):
                affine(t, ln_norm, x1_ready, LN[:, 0, :], LN[:, 1, :], t + 1)
            pool.wait_ge(y_gated, NT)
            G.memset(xg, 0.0).then_inc(xg_zero, 1)
            pool.wait_ge(st_table, 16)
            pool.wait_ge(rows_ready, 1)
            for n in range(NT * TOPK):
                G.indirect_dma_start(table, bass.IndirectOffsetOnAxis(rowi[:, n:n + 1], 0), pay[:, n, :], None
                                     ).then_inc(tab_done, 16)
            pool.wait_ge(ld_slots, 16)
            pool.wait_ge(st_x1, 16 * NT)
            pool.wait_ge(xg_zero, 1)

            def held():
                pool.sem_inc(pool_steps, 1)

            def gather(i, tokens):
                G.tensor_copy(g_idx[:, :], tokens).then_inc(gi_ready, 1)
                pool.wait_ge(gi_ready, i + 1)
                held()
                G.indirect_dma_start(xg, None, x1_rows,
                                     bass.IndirectOffsetOnAxis(g_idx[:, :].bitcast(U32), 0),
                                     bounds_check=SEQ - 1, oob_is_err=False).then_inc(gathered, 16)

            def take_slots(what):
                G.tensor_copy(d_idx[:, :], what).then_inc(dg_ready, 1)

            def send(i):
                pool.wait_ge(y_evac, i + 2)
                held()
                G.indirect_dma_start(y_rows, bass.IndirectOffsetOnAxis(d_idx[:, 0:1].bitcast(U32), 0), y_t, None,
                                     bounds_check=SEQ * TOPK - 1, oob_is_err=False).then_inc(y_sent, 16)

            gather(0, slots[:, 0, 0:1])
            pool.wait_ge(xgt_mm, 1)
            gather(1, slots[:, 1, 0:1])
            take_slots(slots[:, 0, 1:3])
            with pool.Fori(1, NE - 1) as i:
                pool.wait_ge(xgt_mm, i + 1)
                held()
                gather(i + 1, slots[:, bass.ds(i + 1, 1), 0:1].rearrange("p a b -> p (a b)"))
                send(i - 1)
                pool.wait_ge(y_sent, i * 16)
                held()
                take_slots(slots[:, bass.ds(i, 1), 1:3].rearrange("p a b -> p (a b)"))
            send(NE - 2)
            pool.wait_ge(y_sent, (NE - 1) * 16)
            take_slots(slots[:, NE - 1, 1:3])
            send(NE - 1)
            pool.wait_ge(extra_ready, 1)
            n_extra = pool.value_load(extra_i[0:1, 32:33], min_val=0, max_val=15)
            with pool.If(n_extra > 0):
                with pool.Fori(0, n_extra) as j:
                    pool.wait_ge(ld_xslot, j * 16 + 16)
                    pool.wait_ge(xgt_mm, j + NE)
                    pool.wait_ge(y_sent, (j + NE) * 16)
                    held()
                    gather(j + NE, xslot[:, 0:1])
                    take_slots(xslot[:, 1:3])
                    send(j + NE)
            pool.wait_ge(ld_ln2, 32)
            for t in range(NT):
                affine(t, fin_norm, fin_done, LN2[:, 0, :], LN2[:, 1, :], NT + t + 1)


_OUT = (SEQ, D)


def kernel(**inputs):
    import numpy as _np
    import concourse.bacc as _bacc
    from concourse import mybir as _mybir
    from concourse.bass_utils import run_bass_kernel_spmd as _run

    a = {k: _np.asarray(v) for k, v in inputs.items()}
    arrays = {
        "x": a["x"].reshape(SEQ, D),
        "xT": a["x"].reshape(SEQ, KD, P).transpose(2, 1, 0),
        "pT": a["p"].reshape(SEQ, PLE // P, P).transpose(2, 1, 0),
        "w_in": a["w_in"],
        "conv_w": a["conv_w"].reshape(4, 12, P).transpose(2, 1, 0),
        "a_log": a["a_log"].reshape(HB), "dt_bias": a["dt_bias"].reshape(HB), "gnorm_w": a["gnorm_w"].reshape(P),
        "w_out": a["w_out"], "ln1_g": a["ln1_g"].reshape(D), "ln1_b": a["ln1_b"].reshape(D),
        "w_router": a["w_router"], "b_router": a["b_router"],
        "w_gate_up": a["w_gate_up"], "b_gate_up": a["b_gate_up"], "w_down": a["w_down"], "b_down": a["b_down"],
        "w_ple_gate": a["w_ple_gate"], "b_ple_gate": a["b_ple_gate"], "w_ple_proj": a["w_ple_proj"],
        "ln2_g": a["ln2_g"].reshape(D), "ln2_b": a["ln2_b"].reshape(D),
        "consts": constants(), "table0": table_rows(), "pay0": payload(),
    }
    arrays = {f"in_{k}_dram": _np.ascontiguousarray(v) for k, v in arrays.items()}
    nc = _bacc.Bacc("TRN2", target_bir_lowering=False, num_devices=1)
    args = [nc.dram_tensor(n, v.shape, _mybir.dt.from_np(v.dtype), kind="ExternalInput").ap()
            for n, v in arrays.items()]
    args.append(nc.dram_tensor("out_0_dram", _OUT, _mybir.dt.float32, kind="ExternalOutput").ap())
    hybrid_layer(nc, *args)
    r = _run(nc, [arrays], core_ids=[0])
    return r.results[0]["out_0_dram"].reshape(1, SEQ, D)
```

```python
import math
from contextlib import ExitStack

import numpy as np
import concourse.bass as bass
from concourse import mybir

F32 = mybir.dt.float32
F32R = mybir.dt.float32r
BF16 = mybir.dt.bfloat16
I32 = mybir.dt.int32
U32 = mybir.dt.uint32
ALU = mybir.AluOpType
ACT = mybir.ActivationFunctionType
AX = mybir.AxisListType

P = 128
SEQ = 512
D = 1024
NT = SEQ // P
KD = D // P
HA, EA = 8, 64
HB = 4
PLE = 256
NE = 32
TOPK = 4
FE = 1024
KF = FE // P
TW = 2 * FE
BLOCK_TILES = KD + KF // 2
ALPHA = 2.0 ** 0.25
LN_EPS, RMS_EPS, L2_EPS = 1e-5, 1e-6, 1e-6
NEG = -1.0e30
LEVELS = 7
NBLK = 7
SLOTS = 3
BLK = KD * 512
CAP = SEQ
SKIP = 1 << 20

C_IDENT, C_ONES, C_UPPER, C_NEGM, C_STRICT = 0, 128, 256, 384, 512
C_STRIP = 640
C_LEVEL = C_STRIP + SEQ
C_ESEL = C_LEVEL + LEVELS * P
C_EBASE = C_ESEL + NE
C_TOTAL = C_EBASE + NE


def constants():
    c = np.zeros((P, C_TOTAL), np.float32)
    r = np.arange(P)
    c[:, C_IDENT:C_IDENT + P] = np.eye(P)
    c[:, C_ONES:C_ONES + P] = 1.0
    c[:, C_UPPER:C_UPPER + P] = r[:, None] <= r[None, :]
    c[:, C_NEGM:C_NEGM + P] = np.where(r[:, None] <= r[None, :], 0.0, NEG)
    c[:, C_STRICT:C_STRICT + P] = r[:, None] < r[None, :]
    dist = (SEQ - P) + r[:, None] - np.arange(SEQ)[None, :]
    count = np.zeros((P, SEQ))
    for window, dil in ((128, 1), (512, 4), (2048, 16)):
        count += (dist >= 0) & (dist % dil == 0) & (dist <= window // dil * dil)
    c[:, C_STRIP:C_STRIP + SEQ] = np.where(count > 0, np.log(np.maximum(count, 1)), NEG)
    for lv in range(LEVELS):
        m = 1 << lv
        same = (r[:, None] // (2 * m)) == (r[None, :] // (2 * m))
        off = ((r[:, None] // m) % 2 == 1) & ((r[None, :] // m) % 2 == 0)
        c[:, C_LEVEL + lv * P:C_LEVEL + (lv + 1) * P] = same & off
    c[:, C_ESEL:C_ESEL + NE] = np.arange(NE)
    c[:, C_EBASE:C_EBASE + NE] = np.arange(NE) * CAP
    return c


def table_rows():
    t = np.zeros((P, NE * CAP // P * 4), np.int32)
    t[:, 0::4] = SKIP
    t[:, 1::4] = SKIP
    return t


def payload():
    t = np.zeros((P, NT, TOPK, 4), np.int32)
    for tt in range(NT):
        tok = tt * P + np.arange(P)
        t[:, tt, :, 0] = tok[:, None]
        t[:, tt, :, 1] = tok[:, None] * TOPK + np.arange(TOPK)
    return t.reshape(P, NT * TOPK * 4)


def hybrid_layer(nc, x, xT, pT, w_in, conv_w, a_log, dt_bias, gnorm_w, w_out, ln1_g, ln1_b,
                 w_router, b_router, w_gate_up, b_gate_up, w_down, b_down,
                 w_ple_gate, b_ple_gate, w_ple_proj, ln2_g, ln2_b, consts, table0, pay0, out):
    ctx = ExitStack()
    with ctx:
        def sb(name, shape, dt=F32):
            return ctx.enter_context(nc.sbuf_tensor(name, shape, dt))

        def sem(name):
            return ctx.enter_context(nc.semaphore(name))

        x1_rows = nc.dram_tensor("x1_rows", (SEQ, D), F32, kind="Internal").ap()
        y_rows = nc.dram_tensor("y_rows", (SEQ * TOPK, D), F32, kind="Internal").ap()
        table = nc.dram_tensor("dispatch_table", (NE * CAP, 4), I32, kind="Internal").ap()
        bias_parts = nc.dram_tensor("bias_parts", (NE, 3, 2 * FE), BF16, kind="Internal").ap()

        with nc.sbuf_tensor("W", [P, 3 * FE * KD], F32) as W:
            pass
        WR = sb("WR", [P, 3 * FE * KD], F32R)

        def w_in_view(ring, s):
            return ring[:, s * BLK:(s + 1) * BLK].rearrange("p (k n) -> p k n", k=KD)

        w_in_raw = [w_in_view(W, s) for s in range(SLOTS)]
        w_in_lo = [w_in_view(WR, s) for s in range(SLOTS)]
        w_in_hi = [w_in_view(WR, SLOTS + s) for s in range(2)]
        XTH = w_in_view(WR, SLOTS + 2)
        gu_tile = [W[:, k * 2 * FE:(k + 1) * 2 * FE] for k in range(KD)]
        dn_tile = [W[:, (2 * KD + k) * FE:(2 * KD + k + 1) * FE] for k in range(KF)]
        LT = W[:, 0:2048].rearrange("p (h n) -> p h n", h=HB)
        KB = W[:, 2048:4096].rearrange("p (h n) -> p h n", h=HB)
        KDEC = W[:, 4096:6144].rearrange("p (h n) -> p h n", h=HB)
        VB = W[:, 6144:8192].rearrange("p (h n) -> p h n", h=HB)
        AT = W[:, 8192:10240].rearrange("p (h n) -> p h n", h=HB)
        T1 = W[:, 10240:12288].rearrange("p (h n) -> p h n", h=HB)
        SQ = W[:, (SLOTS + 1) * BLK:(SLOTS + 2) * BLK].rearrange("p (n c) -> p n c", n=8)
        DD = W[:, 12288:16384].rearrange("p (h c s n) -> p h c s n", h=HB, c=NT, s=2)
        ple_tile = [W[:, 16384 + k * D:16384 + (k + 1) * D] for k in range(KD)]

        QK = sb("QK", [P, KD, SEQ])
        X1 = QK[:, :, :].rearrange("p k n -> p (k n)").rearrange("p (t n) -> p t n", t=NT)
        ZT = sb("ZT", [P, NT, SEQ])
        S2 = sb("S2", [P, 3, SEQ])
        with ExitStack() as front:
            def sf(name, shape):
                return front.enter_context(nc.sbuf_tensor(name, shape, F32))

            with nc.sbuf_tensor("XA", [P, KD, SEQ], F32) as XA:
                pass
            XTL = front.enter_context(nc.sbuf_tensor("XTL", [P, KD, SEQ], F32R))
            MXA = sf("MXA", [P, 4, SEQ])
            PT = sf("PT", [P, 4, SEQ])
            DT = sf("DT", [P, 12, SEQ])
            VT = sf("VT", [P, NT, SEQ])
        w_hi = sb("w_hi", [P, 2, TW], F32R)
        w_lo = sb("w_lo", [P, 2, TW], F32R)
        xh, xl, ah, al = (sb(n, [P, KD, P], F32R) for n in ("xh", "xl", "ah", "al"))
        ET = sb("ET", [P, 4, FE])
        g_t, u_t, s_t, y_t = (ET[:, j, :] for j in range(4))
        MXB = XA[:, 0:4, :]
        ST = [XA[:, 4, :], XA[:, 5, :]]
        VN = XA[:, 6, :]
        YT = XA[:, 7, :]
        X1T = DT[:, 4:12, :]
        xg = ZT[:, 0:2, :].rearrange("p a n -> p (a n)")
        PJ = VT[:, :, :].rearrange("p a n -> p (a n)").rearrange("p (k n) -> p k n", k=2)
        LN = PT[:, :, :].rearrange("p a n -> p (a n)").rearrange("p (k n) -> p k n", k=2)
        LN2 = W[:, 8 * TW:9 * TW].rearrange("p (k n) -> p k n", k=2)

        def y_in(t, k):
            return W[:, (t * TOPK + k) * D:(t * TOPK + k + 1) * D]

        C = sb("C", [P, C_TOTAL])
        ident = C[:, C_IDENT:C_IDENT + P]
        ones = C[:, C_ONES:C_ONES + P]
        upper = C[:, C_UPPER:C_UPPER + P]
        negm = C[:, C_NEGM:C_NEGM + P]
        strict = C[:, C_STRICT:C_STRICT + P]
        w_ba = sb("w_ba", [P, KD, 2 * HB])
        w_ba_hi, w_ba_lo = (sb(n, [P, KD, 2 * HB], F32R) for n in ("w_ba_hi", "w_ba_lo"))
        cw = sb("cw", [P, 12, 4])
        na = sb("na", [P, HB])
        dtb = sb("dtb", [P, HB])
        nw = sb("nw", [P, P])
        w_rt = sb("w_rt", [P, KD, NE])
        b_rt = sb("b_rt", [NE, 1])
        logitT = DT[0:NE, 1, :]
        b_dn = XA[0:NE, 6:8, :].rearrange("p a n -> p (a n)")
        b_pg = PT[0:1, 0:2, :].rearrange("p a n -> p (a n)")
        small = sb("small", [P, 512])
        cols = [small[:, j * 16:(j + 1) * 16] for j in range(32)]
        BA = small[:, 0:32]
        BAT = S2[0:2 * HB, 2, :]
        BETA, GG, GC, GL, EGC, EGL, EKD, BKE, XX, E1, SP1 = cols[2:13]
        nmax, den, rden = (small[:, 208 + 32 * j:240 + 32 * j] for j in range(3))
        MS, RSD = cols[19], cols[20]
        stat = small[:, 336:336 + 12]
        mv = small[:, 348:350]
        std = small[:, 350:354]
        rstd = small[:, 354:358]
        junk = sb("junk", [P, P])
        eps_l2, eps_rms, eps_ln, one_c = (sb(n, [P, 1]) for n in ("eps_l2", "eps_rms", "eps_ln", "one_c"))
        s_ple = XA[:, 4:6, :]
        logit = sb("logit", [P, NT, NE])
        topv = sb("topv", [P, NT, 8])
        topi = sb("topi", [P, NT, 8], U32)
        topf = sb("topf", [P, NT, TOPK])
        gate = sb("gate", [P, NT, TOPK])
        gsum = sb("gsum", [P, NT, 1])
        memb = sb("memb", [P, NT, NE])
        onehot = S2[:, 2, :].rearrange("p (n e) -> p n e", e=NE)
        work = DT[:, 1, :].rearrange("p (n e) -> p n e", e=NE)
        rowf = sb("rowf", [P, NT * TOPK])
        rowi = sb("rowi", [P, NT * TOPK], U32)
        gmat = sb("gmat", [P, NT, NE])
        gT = ZT[0:NE, 2, :]
        pay = sb("pay", [P, NT * TOPK, 4], I32)
        slots = sb("slots", [P, NE, 4], I32)
        xslot = sb("xslot", [P, 4], I32)
        extra_f = sb("extra_f", [P, 128])
        extra_i = sb("extra_i", [P, 64], I32)
        g_idx = sb("g_idx", [P, 1], I32)
        d_idx = sb("d_idx", [P, 2], I32)
        bias_t = C[0:3, C_STRIP:C_STRIP + FE].bitcast(BF16)
        ones3 = sb("ones3", [3, P], BF16)
        PS = ctx.enter_context(nc.psum_tensor("PS", [P, 8, 512], F32))
        SUM_BANK = (2, 3, 4, 5, 0, 1, 6, 7)
        bank = [PS[:, b, :] for b in range(8)]

        ld_c, ld_xa, ld_xb, ld_small, ld_bgu = (sem(n) for n in ("ld_c", "ld_xa", "ld_xb", "ld_small", "ld_bgu"))
        ld_w = [sem(f"ld_w{j}") for j in range(SLOTS)]

        def w_in_loads(blk):
            return 16 * (blk // SLOTS + (1 if blk % SLOTS else 0))

        ld_wout, ld_x, ld_ln, ld_pt, ld_pj, ld_pg, ld_ln2, ld_pb = (
            sem(n) for n in ("ld_wout", "ld_x", "ld_ln", "ld_pt", "ld_pj", "ld_pg", "ld_ln2", "ld_pb"))
        st_bias, st_table, st_x1, ld_slots = (sem(n) for n in ("st_bias", "st_table", "st_x1", "ld_slots"))
        ld_gu = [sem(f"ld_gu{k}") for k in range(KD)]
        ld_dn = [sem(f"ld_dn{q}") for q in range(KF // 2)]
        ld_bias, ld_xslot, st_out = (sem(n) for n in ("ld_bias", "ld_xslot", "st_out"))
        ld_y = [[sem(f"ld_y{t}_{pair}") for pair in range(2)] for t in range(NT)]
        (split_done, x_hi, x_lo, wi_hi, wi_lo, proj_done, evac_done, conv_done, ba_split, ba_mm, ba_rows, ba_done, silu_done,
         sc_mm, sc_read, sc_exp, sc_max, p_norm, tr_mm, tr_evac, o_mm, o_evac,
         sq_done, nrm_mm, nrm_ln, nrm_rs, nrm_done, gates_f, gc_mm, gsc_done,
         dp_bc, dp_arg, dp_kb, dp_e, dp_dec, dp_decs, dp_la, dp_lt, dp_tr, dp_kdec, dp_kbvb, dp_qdec,
         dd_ready, inv_a, inv_t1, inv_b, w_mm, w_evac,
         st_zero, scan_v, scan_vn, scan_s, scan_st, scan_o, sq_sum, rms_done, y_norm, y_gated, yt_mm, mix_ready,
         mix_mm, mix_read, ln_mv, ln_std, x1_ready, xt_mm, xt_evac,
         rt_t, rt_biased, rt_mm, rt_memb, pos_mm, route_exp, route_e, gm_ready, gT_mm, gT_evac, extra_ready,
         ple_gmm, ple_mm, ple_sig, ple_read, rows_ready, tab_done,
         dch, ach) = (sem(n) for n in (
            "split_done x_hi x_lo wi_hi wi_lo proj_done evac_done conv_done ba_split ba_mm ba_rows ba_done silu_done "
            "sc_mm sc_read sc_exp sc_max p_norm tr_mm tr_evac o_mm o_evac "
            "sq_done nrm_mm nrm_ln nrm_rs nrm_done gates_f gc_mm gsc_done "
            "dp_bc dp_arg dp_kb dp_e dp_dec dp_decs dp_la dp_lt dp_tr dp_kdec dp_kbvb dp_qdec "
            "dd_ready inv_a inv_t1 inv_b w_mm w_evac "
            "st_zero scan_v scan_vn scan_s scan_st scan_o sq_sum rms_done y_norm y_gated yt_mm mix_ready "
            "mix_mm mix_read ln_mv ln_std x1_ready xt_mm xt_evac "
            "rt_t rt_biased rt_mm rt_memb pos_mm route_exp route_e gm_ready gT_mm gT_evac extra_ready "
            "ple_gmm ple_mm ple_sig ple_read rows_ready tab_done dch ach").split())
        (xg_zero, gathered, xgt_mm, xh_ready, xl_ready, hi_ready, lo_ready, hi_used, w_used, h_read, g_ready, sig_ready, m_ready,
         act_ready, at_mm, ah_ready, al_ready, y_evac, y_sent, dg_ready, gi_ready,
         fin_pair, fin_rstd, fin_scaled, fin_done, fin_last, pool_steps) = (sem(n) for n in (
            "xg_zero gathered xgt_mm xh_ready xl_ready hi_ready lo_ready hi_used w_used h_read g_ready sig_ready m_ready "
            "act_ready at_mm ah_ready al_ready y_evac y_sent dg_ready gi_ready "
            "fin_pair fin_rstd fin_scaled fin_done fin_last pool_steps").split())

        block = ctx.enter_context(nc.Block())
        w_in_k = w_in[0].rearrange("(k p) n -> p k n", p=P)
        w_out_k = w_out[0].rearrange("(k p) n -> p k n", p=P)
        w_pg_k = w_ple_gate[0].rearrange("(k p) n -> p k n", p=P)
        w_pj_k = w_ple_proj[0].rearrange("(k p) n -> p k n", p=P)
        gu_d = w_gate_up[0].rearrange("e (k p) n -> e k p n", p=P)
        dn_d = w_down[0].rearrange("e (q j p) n -> e q p j n", p=P, j=2)
        dn_raw = [W[:, (KD + q) * TW:(KD + q + 1) * TW] for q in range(KF // 2)]
        dn_pair = [t.rearrange("p (j n) -> p j n", j=2) for t in dn_raw]

        def gu_at(i):
            return 0 if isinstance(i, int) and i == 0 else i * BLOCK_TILES - KF // 2

        def dn_at(i):
            return i * BLOCK_TILES + KD + BLOCK_TILES - KF // 2

        DN_LAST = NE * BLOCK_TILES - KF // 2

        def extra_at(j):
            return j * BLOCK_TILES + NE * BLOCK_TILES

        def bank_free(eng, g):
            if g >= 2:
                f = g - 2
                if f < 12:
                    eng.wait_ge(evac_done, f + 1)
                elif f < 24:
                    eng.wait_ge(conv_done, f - 11)
                else:
                    eng.wait_ge(evac_done, f - 11)

        @block.sync
        def _(sp):
            for part, loaded in ((slice(0, 4), ld_xa), (slice(4, 8), ld_xb)):
                sp.dma_start(XA[:, part, :], xT[:, part, :]).then_inc(loaded, 16)
                sp.dma_start(w_in_raw[0][:, part, :], w_in_k[:, part, 0:512]).then_inc(loaded, 16)
            sp.dma_start(w_in_raw[1], w_in_k[:, :, 512:1024]).then_inc(ld_w[1], 16)
            sp.dma_start(C[:, :], consts).then_inc(ld_c, 16)
            sp.dma_start(DT[0:NE, 0:4, :].rearrange("p a n -> p (a n)"), b_gate_up[0]).then_inc(ld_bgu, 16)
            sp.dma_start(w_in_raw[2], w_in_k[:, :, 1024:1536]).then_inc(ld_w[2], 16)
            sp.dma_start(w_ba[:, :, :], w_in_k[:, :, 3584:3592]).then_inc(ld_small, 16)
            sp.dma_start(cw[:, :, :], conv_w).then_inc(ld_small, 16)
            sp.dma_start(na[:, :], a_log.partition_broadcast(P)).then_inc(ld_small, 16)
            sp.dma_start(dtb[:, :], dt_bias.partition_broadcast(P)).then_inc(ld_small, 16)
            sp.dma_start(nw[:, :], gnorm_w.partition_broadcast(P)).then_inc(ld_small, 16)
            sp.dma_start(w_rt[:, :, :], w_router[0].rearrange("(k p) n -> p k n", p=P)).then_inc(ld_small, 16)
            sp.dma_start(b_rt[:, :], b_router.rearrange("o n -> n o")).then_inc(ld_small, 16)
            sp.dma_start(pay[:, :, :].rearrange("p n w -> p (n w)"), pay0).then_inc(ld_small, 16)
            sp.dma_start(table.rearrange("(p r) w -> p (r w)", p=P), table0).then_inc(st_table, 16)
            sp.wait_ge(split_done, 3)
            parts = DT[0:NE, 8:12, :].rearrange("p a n -> p (a n)").bitcast(BF16)
            sp.dma_start(bias_parts[:, 0, :], parts[:, 0:2 * FE]).then_inc(st_bias, 16)
            sp.dma_start(bias_parts[:, 1, :], parts[:, 2 * FE:4 * FE]).then_inc(st_bias, 16)
            low = DT[0:NE, 4:6, :].rearrange("p a n -> p (a n)").bitcast(BF16)
            sp.dma_start(bias_parts[:, 2, :], low[:, 0:2 * FE]).then_inc(st_bias, 16)
            for j in range(SLOTS, NBLK):
                sp.wait_ge(proj_done, 4 * (j - SLOTS + 1))
                sp.dma_start(w_in_raw[j % SLOTS], w_in_k[:, :, j * 512:(j + 1) * 512]).then_inc(ld_w[j % SLOTS], 16)
            sp.wait_ge(proj_done, 28)
            sp.wait_ge(nrm_mm, 8)
            sp.dma_start(W[:, 16384:24576].rearrange("p (k n) -> p k n", k=KD), w_out_k).then_inc(ld_wout, 16)
            sp.wait_ge(o_mm, HA)
            sp.dma_start(PJ, w_pj_k).then_inc(ld_pj, 16)
            sp.wait_ge(dp_la, HB)
            sp.wait_ge(dp_qdec, HB)
            sp.dma_start(X1, x.rearrange("(t p) n -> p t n", p=P)).then_inc(ld_x, 16)
            sp.wait_ge(dp_lt, 2 * HB)
            sp.dma_start(LN[:, 0, :], ln1_g.partition_broadcast(P)).then_inc(ld_ln, 16)
            sp.dma_start(LN[:, 1, :], ln1_b.partition_broadcast(P)).then_inc(ld_ln, 16)
            sp.dma_start(S2[:, 0:2, :], pT).then_inc(ld_pt, 16)
            sp.wait_ge(scan_o, NT)
            for k in range(KD):
                sp.dma_start(gu_tile[k], gu_d[0, k]).then_inc(ld_gu[k], 16)
            sp.wait_ge(st_bias, 48)
            sp.dma_start(bias_t, bias_parts[0]).then_inc(ld_bias, 16)
            sp.wait_ge(x1_ready, 1)
            sp.dma_start(x1_rows[0:P, :], X1[:, 0, :]).then_inc(st_x1, 16)
            sp.wait_ge(mix_mm, NT)
            for k in range(KD):
                sp.dma_start(ple_tile[k], w_pg_k[:, k, :]).then_inc(ld_pg, 16)
            sp.wait_ge(scan_vn, NT)
            sp.wait_ge(yt_mm, NT)
            sp.dma_start(b_dn, b_down[0]).then_inc(ld_pb, 16)
            for t in range(1, NT):
                sp.wait_ge(x1_ready, t + 1)
                sp.dma_start(x1_rows[t * P:(t + 1) * P, :], X1[:, t, :]).then_inc(st_x1, 16)
            sp.dma_start(b_pg, b_ple_gate).then_inc(ld_pb, 16)
            sp.wait_ge(tab_done, 16 * NT * TOPK)
            sp.dma_start(slots[:, :, :], table.rearrange("(e c) w -> c e w", c=CAP)[0:P]).then_inc(ld_slots, 16)
            sp.wait_ge(ple_mm, NT)
            for q in range(KF // 2):
                sp.dma_start(dn_pair[q], dn_d[0, q]).then_inc(ld_dn[q], 16)

            def load_gate_up(e, before):
                for k in range(KD):
                    sp.wait_ge(lo_ready, before + k + 1)
                    sp.dma_start(gu_tile[k], gu_d[e, k]).then_inc(ld_gu[k], 16)
                    if k == 2:
                        sp.wait_ge(w_used, before + 1)
                        sp.dma_start(bias_t, bias_parts[e]).then_inc(ld_bias, 16)

            def load_down(e, before):
                for q in range(KF // 2):
                    sp.wait_ge(lo_ready, before + q + 1)
                    sp.dma_start(dn_pair[q], dn_d[e, q]).then_inc(ld_dn[q], 16)

            load_gate_up(1, 0)
            load_gate_up(2, gu_at(1))
            load_down(1, dn_at(0))
            with sp.Fori(2, NE - 1) as i:
                load_gate_up(i + 1, gu_at(i))
                load_down(i, dn_at(i - 1))
            load_down(NE - 1, dn_at(NE - 2))
            sp.wait_ge(extra_ready, 1)
            n_extra = sp.value_load(extra_i[0:1, 32:33], min_val=0, max_val=15)
            with sp.If(n_extra > 0):
                with sp.Fori(0, n_extra) as j:
                    e = sp.value_load(extra_i[0:1, bass.ds(j, 1)], min_val=0, max_val=NE - 1)
                    row = sp.value_load(extra_i[0:1, bass.ds(j + 16, 1)], min_val=0, max_val=NE * CAP - P)
                    sp.wait_ge(y_sent, (j + NE) * 16)
                    sp.dma_start(xslot[:, :], table[bass.ds(row, P), :]).then_inc(ld_xslot, 16)
                    load_gate_up(e, extra_at(j - 1))
                    load_down(e, extra_at(j - 1) + KD)
            sp.wait_ge(y_sent, (n_extra + NE) * 16)
            sp.dma_start(LN2[:, 0, :], ln2_g.partition_broadcast(P)).then_inc(ld_ln2, 16)
            sp.dma_start(LN2[:, 1, :], ln2_b.partition_broadcast(P)).then_inc(ld_ln2, 16)
            for t in range(NT):
                rows = y_rows[t * P * TOPK:(t + 1) * P * TOPK, :].rearrange("(p k) n -> p k n", k=TOPK)
                for k in range(TOPK):
                    sp.dma_start(y_in(t, k), rows[:, k, :]).then_inc(ld_y[t][k // 2], 16)
            for t in range(NT):
                if t < NT - 1:
                    sp.wait_ge(fin_done, t + 1)
                else:
                    sp.wait_ge(fin_last, 1)
                sp.dma_start(out[t * P:(t + 1) * P, :], X1[:, t, :]).then_inc(st_out, 16)
            sp.wait_ge(st_out, 16 * NT)

        @block.tensor
        def _(pe):
            mm, tr = nc.tensor.matmul, nc.tensor.transpose

            def project(g):
                blk, j = divmod(g, 4)
                bank_free(pe, g)
                js = slice(j * P, (j + 1) * P)
                for half in range(2):
                    if g == 0:
                        pe.wait_ge(x_lo, half + 1)
                    if j == 0:
                        pe.wait_ge(wi_lo, 2 * blk + half + 1)
                    for k in range(4 * half, 4 * half + 4):
                        for x, w in ((XTH, w_in_hi[blk % 2]), (XTL, w_in_hi[blk % 2]), (XTH, w_in_lo[blk % SLOTS])):
                            ends = dict(start=(k == 0 and x is XTH and w is w_in_hi[blk % 2]),
                                        stop=(k == KD - 1 and w is w_in_lo[blk % SLOTS]))
                            if blk in (2, 6):
                                last = mm(bank[g % 2], x[:, k, js], w[:, k, :], **ends)
                            else:
                                last = mm(bank[g % 2], w[:, k, js], x[:, k, :], **ends)
                last.then_inc(proj_done, 1)

            def scores(n):
                h, i = divmod(n, NT)
                r0, c = (h % 2) * EA, h // 2
                if n >= 2:
                    pe.wait_ge(sc_read, n - 1)
                mm(bank[2 + n % 2][:, 0:(i + 1) * P], QK[r0:r0 + EA, c, i * P:(i + 1) * P],
                   QK[r0:r0 + EA, 4 + c, 0:(i + 1) * P], start=True, stop=True).then_inc(sc_mm, 1)

            def transpose_probs(n):
                i = n % NT
                pe.wait_ge(p_norm, n + 1)
                if n >= 2:
                    pe.wait_ge(tr_evac, n - 1)
                for kt in range(i + 1):
                    last = tr(bank[4 + n % 2][:, kt * P:(kt + 1) * P], S2[:, n % 3, kt * P:(kt + 1) * P], ident)
                last.then_inc(tr_mm, 1)

            def attend(h):
                r0 = (h % 2) * EA
                pe.wait_ge(tr_evac, NT * (h + 1))
                if h:
                    pe.wait_ge(o_evac, h)
                for kt in range(NT):
                    last = mm(bank[6][r0:r0 + EA, kt * P:SEQ], VT[:, kt, h * EA:(h + 1) * EA],
                              PT[:, kt, kt * P:SEQ], start=(kt == 0), stop=(kt == NT - 1))
                last.then_inc(o_mm, 1)

            for g in range(12):
                project(g)
                if g == 7:
                    pe.wait_ge(ba_split, 2)
                    for k in range(KD):
                        for x, w in ((XTH, w_ba_hi), (XTL, w_ba_hi), (XTH, w_ba_lo)):
                            last = mm(bank[7][0:2 * HB, :], w[:, k, :], x[:, k, :],
                                      start=(k == 0 and x is XTH and w is w_ba_hi), stop=(k == KD - 1 and w is w_ba_lo))
                    last.then_inc(ba_mm, 1)
            pe.wait_ge(ld_c, 16)
            pe.wait_ge(ba_rows, 1)
            for t in range(NT):
                last = tr(bank[7][:, t * 8:(t + 1) * 8], BAT[:, t * P:(t + 1) * P], ident[0:2 * HB, 0:2 * HB])
            last.then_inc(ba_done, 1)
            pe.wait_ge(evac_done, 12)
            for m in range(16):
                if m == 3:
                    pe.wait_ge(gates_f, 1)
                    mm(bank[7][:, 0:16], upper, GG, start=True, stop=True)
                    mm(bank[7][:, 16:32], ones, GG, start=True, stop=True).then_inc(gc_mm, 1)
                scores(2 * m)
                scores(2 * m + 1)
                if m >= 2 and m % 2 == 0:
                    attend(m // 2 - 1)
                project(12 + m)
                transpose_probs(2 * m)
                transpose_probs(2 * m + 1)
            attend(HA - 1)

            pe.wait_ge(sq_done, 8)
            pe.wait_ge(tr_evac, HA * NT)
            for n in range(8):
                if n == 4:
                    pe.wait_ge(gsc_done, 1)
                    pe.wait_ge(evac_done, 16)
                    pe.wait_ge(o_evac, HA)
                mm(bank[SUM_BANK[n]], ones, SQ[:, n, :], start=True, stop=True).then_inc(nrm_mm, 1)
            pe.wait_ge(nrm_done, 8)

            def spread(h):
                a = 4 * (h % 2)
                if h >= 2:
                    pe.wait_ge(dp_kdec, h - 1)
                    pe.wait_ge(dp_kbvb, h - 1)
                for t in range(NT):
                    mm(bank[a][:, t * P:(t + 1) * P], GG[:, t * HB + h:t * HB + h + 1].to_broadcast([P, P]), upper,
                       start=True, stop=True)
                    last = mm(bank[a + 1][:, t * P:(t + 1) * P],
                              BETA[:, t * HB + h:t * HB + h + 1].to_broadcast([P, P]), ident, start=True, stop=True)
                last.then_inc(dp_bc, 1)

            def grams(h):
                a = 4 * (h % 2)
                pe.wait_ge(dp_kb, h + 1)
                if h >= 2:
                    pe.wait_ge(dp_lt, 2 * (h - 1))
                for t in range(NT):
                    s = slice(t * P, (t + 1) * P)
                    mm(bank[a + 2][:, s], DT[:, 4 + h, s], QK[:, h, s], start=True, stop=True)
                    last = mm(bank[a + 3][:, s], DT[:, 4 + h, s], DT[:, h, s], start=True, stop=True)
                last.then_inc(dp_la, 1)
                pe.wait_ge(dp_arg, h + 1)
                pe.wait_ge(dp_e, h + 1)
                for t in range(NT):
                    s = slice(t * P, (t + 1) * P)
                    tr(bank[a][:, s], DT[:, 4 + h, s], ident)
                    last = tr(bank[a + 1][:, s], DT[:, 8 + h, s], ident)
                last.then_inc(dp_tr, 1)

            spread(0)
            spread(1)
            for h in range(HB):
                grams(h)
                if h + 2 < HB:
                    spread(h + 2)

            pe.wait_ge(dd_ready, HB)
            pe.wait_ge(dp_kdec, HB)
            pe.wait_ge(dp_kbvb, HB)
            pe.wait_ge(dp_lt, 2 * HB)

            with pe.Fori(0, LEVELS) as lv:
                def times_l(h):
                    pe.wait_ge(dd_ready, lv * HB + h + 1)
                    for c in range(NT):
                        last = mm(bank[3 * (h % 2)][:, c * P:(c + 1) * P], LT[:, h, c * P:(c + 1) * P],
                                  DD[:, h, c, 0, :], start=True, stop=True)
                    last.then_inc(inv_a, 1)

                def correct(h):
                    pe.wait_ge(inv_t1, lv * HB + h + 1)
                    pe.wait_ge(dd_ready, lv * HB + h + 3)
                    for c in range(NT):
                        b = bank[3 * (h % 2) + 1 + c // 2]
                        o = (c % 2) * 2 * P
                        mm(b[:, o:o + P], DD[:, h, c, 1, :], T1[:, h, c * P:(c + 1) * P], start=True, stop=True)
                        last = mm(b[:, o + P:o + 2 * P], T1[:, h, c * P:(c + 1) * P], DD[:, h, c, 1, :],
                                  start=True, stop=True)
                    last.then_inc(inv_b, 1)

                times_l(0)
                times_l(1)
                correct(0)
                times_l(2)
                correct(1)
                times_l(3)
                correct(2)
                correct(3)

            for h in range(HB):
                pe.wait_ge(dd_ready, LEVELS * HB + h + 1)
                if h >= 2:
                    pe.wait_ge(w_evac, h - 1)
                for c in range(NT):
                    last = mm(bank[6 + h % 2][:, c * P:(c + 1) * P], KB[:, h, c * P:(c + 1) * P], DD[:, h, c, 1, :],
                              start=True, stop=True)
                last.then_inc(w_mm, 1)
            pe.wait_ge(w_evac, HB)
            pe.wait_ge(st_zero, 1)
            pe.wait_ge(dp_qdec, HB)

            def scan(c):
                s = slice(c * P, (c + 1) * P)
                cur = ST[c % 2]
                if c:
                    pe.wait_ge(scan_st, HB * c)
                for h in range(HB):
                    hs = slice(h * P, (h + 1) * P)
                    mm(bank[0][:, hs], DD[:, h, c, 1, :], VB[:, h, s], start=True, stop=False)
                    last = mm(bank[0][:, hs], T1[:, h, s], cur[:, hs], start=False, stop=True)
                last.then_inc(scan_v, 1)
                pe.wait_ge(scan_vn, c + 1)
                for h in range(HB):
                    hs = slice(h * P, (h + 1) * P)
                    last = mm(bank[1][:, hs], KDEC[:, h, s], VN[:, hs], start=True, stop=True)
                last.then_inc(scan_s, 1)
                if c >= 2:
                    pe.wait_ge(y_norm, c - 1)
                for h in range(HB):
                    hs = slice(h * P, (h + 1) * P)
                    mm(bank[2 + c % 2][:, hs], DT[:, h, s], cur[:, hs], start=True, stop=False)
                    last = mm(bank[2 + c % 2][:, hs], AT[:, h, s], VN[:, hs], start=False, stop=True)
                last.then_inc(scan_o, 1)

            def y_transpose(c):
                pe.wait_ge(y_gated, c + 1)
                if c:
                    pe.wait_ge(mix_ready, c)
                for h in range(HB):
                    last = tr(bank[4][:, h * P:(h + 1) * P], YT[:, h * P:(h + 1) * P], ident)
                last.then_inc(yt_mm, 1)

            def mix(c):
                s = slice(c * P, (c + 1) * P)
                if c == 0:
                    pe.wait_ge(ld_wout, 16)
                else:
                    pe.wait_ge(mix_read, c)
                pe.wait_ge(mix_ready, c + 1)
                for half in range(2):
                    for k in range(KD):
                        y = MXA[:, k, s] if k < 4 else MXB[:, k - 4, s]
                        last = mm(bank[5 + half], y, dn_tile[k][:, half * 512:(half + 1) * 512],
                                  start=(k == 0), stop=(k == KD - 1))
                last.then_inc(mix_mm, 1)

            def x1_transpose(t):
                pe.wait_ge(x1_ready, t + 1)
                for q in range(2):
                    if t or q:
                        pe.wait_ge(xt_evac, 2 * t + q)
                    for j in range(4):
                        k = 4 * q + j
                        last = tr(bank[7][:, j * P:(j + 1) * P], X1[:, t, k * P:(k + 1) * P], ident)
                    last.then_inc(xt_mm, 1)

            scan(0)
            y_transpose(0)
            scan(1)
            y_transpose(1)
            mix(0)
            scan(2)
            y_transpose(2)
            mix(1)
            x1_transpose(0)
            scan(3)
            y_transpose(3)
            mix(2)
            x1_transpose(1)
            mix(3)
            x1_transpose(2)
            x1_transpose(3)

            pe.wait_ge(xt_evac, 2 * NT)
            for k in range(KD):
                last = mm(bank[0][0:NE, :], w_rt[:, k, :], X1T[:, k, :], start=(k == 0), stop=(k == KD - 1))
            last.then_inc(rt_t, 1)
            pe.wait_ge(rt_biased, 1)
            for t in range(NT):
                last = tr(bank[1][:, t * NE:(t + 1) * NE], logitT[:, t * P:(t + 1) * P], ident[0:NE, 0:NE])
            last.then_inc(rt_mm, 1)

            def ple_gate(t):
                s = slice(t * P, (t + 1) * P)
                if t == 0:
                    pe.wait_ge(ld_pg, 16 * KD)
                    pe.wait_ge(ld_pb, 32)
                else:
                    pe.wait_ge(ple_sig, t)
                for half in range(2):
                    hs = slice(half * 512, (half + 1) * 512)
                    for k in range(KD):
                        mm(bank[2 + half], X1T[:, k, s], ple_tile[k][:, hs], start=(k == 0), stop=False)
                    last = mm(bank[2 + half], ones[0:1, :], b_pg[:, hs], start=False, stop=True)
                last.then_inc(ple_gmm, 1)

            def ple_rest(t):
                s = slice(t * P, (t + 1) * P)
                if t == 0:
                    pe.wait_ge(ld_pt, 16)
                    pe.wait_ge(ld_pj, 16)
                    pe.wait_ge(gT_evac, 1)
                else:
                    pe.wait_ge(ple_read, t)
                for half in range(2):
                    hs = slice(half * 512, (half + 1) * 512)
                    for k in range(2):
                        mm(bank[4 + half], S2[:, k, s], PJ[:, k, hs], start=(k == 0), stop=(k == 1))
                    last = mm(bank[6 + half], gT[:, s], b_dn[:, hs], start=True, stop=True)
                last.then_inc(ple_mm, 1)

            ple_gate(0)
            pe.wait_ge(rt_memb, 1)
            for t in range(NT):
                for s in range(t):
                    mm(bank[1][:, t * NE:(t + 1) * NE], ones, memb[:, s, :], start=(s == 0), stop=False)
                mm(bank[1][:, t * NE:(t + 1) * NE], strict, memb[:, t, :], start=(t == 0), stop=True)
            for s in range(NT):
                last = mm(bank[1][:, 4 * NE:5 * NE], ones, memb[:, s, :], start=(s == 0), stop=(s == NT - 1))
            last.then_inc(pos_mm, 1)
            pe.wait_ge(gm_ready, 1)
            for t in range(NT):
                last = tr(bank[0][0:NE, t * P:(t + 1) * P], gmat[:, t, :], ident)
            last.then_inc(gT_mm, 1)
            def transpose_rows(i, src, done, first_bank=6):
                for q in range(2):
                    for j in range(4):
                        k = 4 * q + j
                        last = tr(bank[first_bank + q][:, j * P:(j + 1) * P], src[:, k * P:(k + 1) * P], ident)
                last.then_inc(done, 1)

            def gate_up(i, at):
                pe.wait_ge(ld_bias, i * 16 + 16)
                pe.wait_ge(xl_ready, i + 1)
                if not isinstance(i, int) or i:
                    pe.wait_ge(h_read, i)
                for n in range(4):
                    mm(bank[n], ones3[:, :], bias_t[:, n * 512:(n + 1) * 512], start=True, stop=False)
                for k in range(KD):
                    pe.wait_ge(hi_ready, at + k + 1)
                    for x in (xh, xl):
                        for n in range(4):
                            last = mm(bank[n], x[:, k, :], w_hi[:, k % 2, n * 512:(n + 1) * 512],
                                      start=False, stop=False)
                    last.then_inc(hi_used, 1)
                    pe.wait_ge(lo_ready, at + k + 1)
                    for n in range(4):
                        last = mm(bank[n], xh[:, k, :], w_lo[:, k % 2, n * 512:(n + 1) * 512],
                                  start=False, stop=(k == KD - 1))
                    last.then_inc(w_used, 1)

            def down(i, at):
                pe.wait_ge(al_ready, i + 1)
                pe.wait_ge(y_evac, i + 1)
                for q in range(KF // 2):
                    pe.wait_ge(hi_ready, at + q + 1)
                    for j in range(2):
                        k = 2 * q + j
                        for a in (ah, al):
                            for n in range(2):
                                last = mm(bank[4 + n], a[:, k, :],
                                          w_hi[:, q % 2, j * FE + n * 512:j * FE + (n + 1) * 512],
                                          start=(k == 0 and a is ah), stop=False)
                    last.then_inc(hi_used, 1)
                    pe.wait_ge(lo_ready, at + q + 1)
                    for j in range(2):
                        k = 2 * q + j
                        for n in range(2):
                            last = mm(bank[4 + n], ah[:, k, :], w_lo[:, q % 2, j * FE + n * 512:j * FE + (n + 1) * 512],
                                      start=False, stop=(k == KF - 1))
                    last.then_inc(w_used, 1)

            def rows_in(i):
                pe.wait_ge(gathered, i * 16 + 16)
                if not isinstance(i, int) or i >= 2:
                    pe.wait_ge(al_ready, i - 1)
                transpose_rows(i, xg, xgt_mm)

            def acts(i, rows):
                pe.wait_ge(act_ready, i + 1)
                pe.wait_ge(xl_ready, rows)
                transpose_rows(i, g_t, at_mm)

            ple_rest(0)
            ple_gate(1)
            ple_rest(1)
            pe.wait_ge(gathered, 16)
            pe.wait_ge(extra_ready, 1)
            transpose_rows(0, xg, xgt_mm, first_bank=0)
            ple_gate(2)
            ple_rest(2)
            ple_gate(3)
            ple_rest(3)
            pe.wait_ge(ple_sig, NT)
            gate_up(0, gu_at(0))
            pe.wait_ge(ple_read, NT)
            rows_in(1)
            acts(0, 2)
            with pe.Fori(1, NE - 1) as i:
                gate_up(i, gu_at(i))
                rows_in(i + 1)
                down(i - 1, dn_at(i - 1))
                acts(i, i + 2)
            gate_up(NE - 1, gu_at(NE - 1))
            down(NE - 2, dn_at(NE - 2))
            acts(NE - 1, NE)
            down(NE - 1, DN_LAST)
            pe.wait_ge(extra_ready, 1)
            n_extra = pe.value_load(extra_i[0:1, 32:33], min_val=0, max_val=15)
            with pe.If(n_extra > 0):
                with pe.Fori(0, n_extra) as j:
                    pe.wait_ge(al_ready, j + NE)
                    rows_in(j + NE)
                    gate_up(j + NE, extra_at(j))
                    acts(j + NE, j + NE + 1)
                    down(j + NE, extra_at(j) + KD)

        @block.scalar
        def _(act):
            A = nc.scalar.activation
            chain = [0]

            def link(ins):
                chain[0] += 1
                ins.then_inc(ach, 1)
                act.wait_ge(ach, chain[0])

            def w_in_upper(blk):
                for half in range(2):
                    ks = slice(4 * half, 4 * half + 4)
                    if blk == 0:
                        act.wait_ge((ld_xa, ld_xb)[half], 32)
                        A(XTH[:, ks, :], XA[:, ks, :], ACT.Copy).then_inc(x_hi, 1)
                    else:
                        act.wait_ge(ld_w[blk % SLOTS], w_in_loads(blk))
                    if blk >= 2:
                        act.wait_ge(proj_done, 4 * (blk - 1))
                    A(w_in_hi[blk % 2][:, ks, :], w_in_raw[blk % SLOTS][:, ks, :], ACT.Copy).then_inc(wi_hi, 1)

            w_in_upper(0)
            w_in_upper(1)
            act.wait_ge(ld_small, 128)
            act.wait_ge(dch, 1)
            A(w_ba_hi[:, :, :], w_ba[:, :, :], ACT.Copy).then_inc(ba_split, 1)
            link(A(na[:, :], na[:, :], ACT.Exp))
            link(nc.scalar.mul(na[:, :], na[:, :], -1.0))
            for g in range(12):
                if g in (4, 8):
                    w_in_upper(g // 4 + 1)
                act.wait_ge(proj_done, g + 1)
                blk, j = divmod(g, 4)
                dst = (QK[:, j, :], QK[:, 4 + j, :], VT[:, j, :])[blk]
                A(dst, bank[g % 2], ACT.Copy).then_inc(evac_done, 1)

            def exps(n):
                i = n % NT
                act.wait_ge(sc_max, n + 1)
                s = S2[:, n % 3, 0:(i + 1) * P]
                A(s, s, ACT.Exp, bias=nmax[:, n:n + 1], accum_out=den[:, n:n + 1]).then_inc(sc_exp, 1)

            def evac_probs(n):
                h, i = divmod(n, NT)
                act.wait_ge(tr_mm, n + 1)
                if h:
                    act.wait_ge(o_mm, h)
                A(PT[:, 0:i + 1, i * P:(i + 1) * P],
                  bank[4 + n % 2][:, 0:(i + 1) * P].rearrange("p (k n) -> p k n", n=P), ACT.Copy).then_inc(tr_evac, 1)

            def evac_out(h):
                r0 = (h % 2) * EA
                act.wait_ge(o_mm, h + 1)
                A(MXA[r0:r0 + EA, h // 2, :], bank[6][r0:r0 + EA, :], ACT.Copy).then_inc(o_evac, 1)

            def silu(t, n):
                A(t, t, ACT.Silu).then_inc(silu_done, 1)

            for m in range(16):
                if m in (1, 4, 8):
                    w_in_upper({1: 4, 4: 5, 8: 6}[m])
                if m == 1:
                    act.wait_ge(route_e, 1)
                    A(E1, BETA, ACT.Exp, scale=-1.0).then_inc(route_exp, 1)
                    link(A(SP1, SP1, ACT.Exp, scale=-1.0))
                    A(SP1, SP1, ACT.Ln, bias=one_c[:, :]).then_inc(route_exp, 1)
                if m == 5:
                    act.wait_ge(route_e, 2)
                    A(EGC, GC, ACT.Exp).then_inc(route_exp, 1)
                    A(EGL, GL, ACT.Exp).then_inc(route_exp, 1)
                    A(EKD, EKD, ACT.Exp).then_inc(route_exp, 1)
                if m >= 1:
                    evac_probs(2 * m - 2)
                    evac_probs(2 * m - 1)
                exps(2 * m)
                exps(2 * m + 1)
                if m >= 2 and m % 2 == 0:
                    evac_out(m // 2 - 1)
                if m in (5, 9, 13):
                    b = (m - 5) // 4
                    act.wait_ge(conv_done, 4 * (b + 1))
                    silu(DT[:, 4 * b:4 * b + 4, :], 4)
                if m >= 13:
                    g = 12 + m - 1
                    act.wait_ge(proj_done, g + 1)
                    A(ZT[:, g - 24, :], bank[g % 2], ACT.Copy).then_inc(evac_done, 1)
            evac_probs(30)
            evac_probs(31)
            evac_out(HA - 1)
            act.wait_ge(proj_done, 28)
            A(ZT[:, 3, :], bank[27 % 2], ACT.Copy).then_inc(evac_done, 1)
            sums = (PS[:, 2:6, :], PS[:, 0:2, :], PS[:, 6:8, :])
            for banks, upto in zip(sums, (4, 6, 8)):
                act.wait_ge(nrm_mm, upto)
                A(banks, banks, ACT.Ln, bias=eps_l2[:, :]).then_inc(nrm_ln, 1)
            for step, banks in enumerate(sums):
                act.wait_ge(nrm_ln, step + 1)
                A(banks, banks, ACT.Exp, scale=-0.5).then_inc(nrm_rs, 1)

            def spread_exp(h):
                a = 4 * (h % 2)
                act.wait_ge(dp_bc, h + 1)
                A(QK[:, 4 + h, :], bank[a], ACT.Exp).then_inc(dp_e, 1)
                act.wait_ge(dp_arg, h + 1)
                A(PT[:, h, :], PT[:, h, :], ACT.Exp).then_inc(dp_dec, 1)

            def evac_v(h):
                a = 4 * (h % 2)
                act.wait_ge(dp_tr, h + 1)
                for t in range(NT):
                    s = slice(t * P, (t + 1) * P)
                    j = t * HB + h
                    last = A(VB[:, h, s], bank[a + 1][:, s], ACT.Copy, scale=BETA[:, j:j + 1])
                last.then_inc(dp_kbvb, 1)

            act.wait_ge(gsc_done, 1)
            spread_exp(0)
            spread_exp(1)
            for h in range(HB):
                evac_v(h)
                if h + 2 < HB:
                    spread_exp(h + 2)
            act.wait_ge(evac_done, 16)
            silu(ZT[:, :, :], 4)
            for h in range(HB):
                act.wait_ge(w_mm, h + 1)
                A(T1[:, h, :], bank[6 + h % 2], ACT.Copy, scale=-1.0).then_inc(w_evac, 1)

            def scan_evac(c):
                act.wait_ge(scan_v, c + 1)
                A(VN, bank[0], ACT.Copy).then_inc(scan_vn, 1)

            def rms(c):
                act.wait_ge(scan_o, c + 1)
                for h in range(HB):
                    if c or h:
                        act.wait_ge(sq_sum, c * HB + h)
                    A(junk[:, :], bank[2 + c % 2][:, h * P:(h + 1) * P], ACT.Square,
                      accum_out=MS[:, c * HB + h:c * HB + h + 1]).then_inc(sq_sum, 1)
                act.wait_ge(sq_sum, HB * (c + 1))
                s = slice(c * HB, (c + 1) * HB)
                A(RSD[:, s], MS[:, s], ACT.Sqrt, scale=1.0 / P, bias=eps_rms[:, :]).then_inc(rms_done, 1)

            def y_evac_t(c):
                act.wait_ge(yt_mm, c + 1)
                A(MXB[:, :, c * P:(c + 1) * P], bank[4].rearrange("p (h n) -> p h n", n=P),
                  ACT.Copy).then_inc(mix_ready, 1)

            def deviation(t, norm=0):
                act.wait_ge(ln_mv, norm * NT + t + 1)
                A(std[:, t:t + 1], mv[:, 1:2], ACT.Sqrt, bias=eps_ln[:, :]).then_inc(ln_std, 1)

            def x1_evac(t):
                for q in range(2):
                    act.wait_ge(xt_mm, 2 * t + q + 1)
                    A(X1T[:, 4 * q:4 * q + 4, t * P:(t + 1) * P], bank[7].rearrange("p (k n) -> p k n", n=P),
                      ACT.Copy).then_inc(xt_evac, 1)

            for c in range(3):
                scan_evac(c)
                rms(c)
                y_evac_t(c)
            deviation(0)
            x1_evac(0)
            scan_evac(3)
            rms(3)
            y_evac_t(3)
            deviation(1)
            x1_evac(1)
            deviation(2)
            deviation(3)
            x1_evac(2)
            x1_evac(3)
            act.wait_ge(route_e, 3)
            A(gate[:, :, :], gate[:, :, :], ACT.Exp).then_inc(route_exp, 1)
            act.wait_ge(gT_mm, 1)
            A(gT, bank[0][0:NE, :], ACT.Copy).then_inc(gT_evac, 1)
            for t in range(NT):
                act.wait_ge(ple_gmm, t + 1)
                if t:
                    act.wait_ge(ple_read, t)
                A(s_ple, PS[:, 2:4, :], ACT.Sigmoid).then_inc(ple_sig, 1)
                if t == 1:
                    act.wait_ge(xgt_mm, 1)
                    A(xh[:, :, :], PS[:, 0:2, :].rearrange("p b n -> p (b n)").rearrange("p (k n) -> p k n", k=KD),
                      ACT.Copy).then_inc(xh_ready, 1)
                    act.wait_ge(ld_gu[0], 16)
                    A(w_hi[:, 0, :], gu_tile[0], ACT.Copy).then_inc(hi_ready, 1)

            six_seven = PS[:, 6:8, :].rearrange("p b n -> p (b n)").rearrange("p (k n) -> p k n", k=KD)

            def rows_out(i):
                act.wait_ge(xgt_mm, i + 1)
                A(xh[:, :, :], six_seven, ACT.Copy).then_inc(xh_ready, 1)

            def sigmoid(i):
                act.wait_ge(g_ready, i + 1)
                A(s_t, g_t, ACT.Sigmoid, scale=1.702).then_inc(sig_ready, 1)

            def acts_out(i):
                act.wait_ge(at_mm, i + 1)
                A(ah[:, :, :], six_seven, ACT.Copy).then_inc(ah_ready, 1)

            def y_out(i, at):
                act.wait_ge(w_used, at + KF // 2)
                act.wait_ge(dg_ready, i + 1)
                A(y_t, PS[:, 4:6, :].rearrange("p b n -> p (b n)"), ACT.Copy,
                  scale=d_idx[:, 1:2].bitcast(F32)).then_inc(y_evac, 1)

            def hi_parts(i, raws, loads, at, first, last):
                for k in range(first, last):
                    act.wait_ge(loads[k], i * 16 + 16)
                    if not isinstance(at, int) or at + k >= 2:
                        act.wait_ge(hi_used, at + k - 1)
                        act.wait_ge(lo_ready, at + k - 1)
                    A(w_hi[:, k % 2, :], raws[k], ACT.Copy).then_inc(hi_ready, 1)

            def hi_gu(i, at, first, last):
                hi_parts(i, gu_tile, ld_gu, at, first, last)

            def hi_dn(i, at, first, last):
                hi_parts(i, dn_raw, ld_dn, at, first, last)

            act.wait_ge(ple_read, NT)
            A(junk[:, 0:1], one_c[:, :], ACT.Copy).then_inc(y_evac, 1)
            hi_gu(0, gu_at(0), 1, KD)
            rows_out(1)
            sigmoid(0)

            def turn(i, rows=True, y=True):
                hi_gu(i, gu_at(i), 0, 2)
                if y:
                    y_out(i - 2, dn_at(i - 2))
                acts_out(i - 1)
                hi_gu(i, gu_at(i), 2, KD)
                hi_dn(i - 1, dn_at(i - 1), 0, 2)
                if rows:
                    rows_out(i + 1)
                sigmoid(i)
                hi_dn(i - 1, dn_at(i - 1), 2, 4)

            turn(1, y=False)
            with act.Fori(2, NE - 1) as i:
                turn(i)
            turn(NE - 1, rows=False)
            hi_dn(NE - 1, DN_LAST, 0, 2)
            y_out(NE - 2, dn_at(NE - 2))
            acts_out(NE - 1)
            hi_dn(NE - 1, DN_LAST, 2, 4)
            y_out(NE - 1, DN_LAST)
            act.wait_ge(extra_ready, 1)
            n_extra = act.value_load(extra_i[0:1, 32:33], min_val=0, max_val=15)
            with act.If(n_extra > 0):
                with act.Fori(0, n_extra) as j:
                    rows_out(j + NE)
                    hi_gu(j + NE, extra_at(j), 0, KD)
                    sigmoid(j + NE)
                    acts_out(j + NE)
                    hi_dn(j + NE, extra_at(j) + KD, 0, 4)
                    y_out(j + NE, extra_at(j) + KD)
            for t in range(NT):
                deviation(t, norm=1)
                if t < NT - 1:
                    act.wait_ge(fin_rstd, t + 1)
                    A(X1[:, t, :], X1[:, t, :], ACT.Copy, scale=rstd[:, t:t + 1]).then_inc(fin_scaled, 1)

        @block.vector
        def _(dve):
            V = nc.vector
            chain = [0]

            def link(ins):
                chain[0] += 1
                ins.then_inc(dch, 1)
                dve.wait_ge(dch, chain[0])

            V.memset(eps_l2[:, :], L2_EPS)
            V.memset(eps_rms[:, :], RMS_EPS)
            V.memset(eps_ln[:, :], LN_EPS)
            V.memset(one_c[:, :], 1.0)
            link(V.memset(ones3[:, :], 1.0))
            def w_in_lower(blk):
                for half in range(2):
                    ks = slice(4 * half, 4 * half + 4)
                    if blk == 0:
                        dve.wait_ge(x_hi, half + 1)
                        V.tensor_tensor(XTL[:, ks, :], XA[:, ks, :], XTH[:, ks, :].bitcast(F32),
                                        ALU.subtract).then_inc(x_lo, 1)
                    dve.wait_ge(wi_hi, 2 * blk + half + 1)
                    V.tensor_tensor(w_in_lo[blk % SLOTS][:, ks, :], w_in_raw[blk % SLOTS][:, ks, :],
                                    w_in_hi[blk % 2][:, ks, :].bitcast(F32), ALU.subtract).then_inc(wi_lo, 1)

            w_in_lower(0)
            w_in_lower(1)
            dve.wait_ge(ba_split, 1)
            V.tensor_tensor(w_ba_lo[:, :, :], w_ba[:, :, :], w_ba_hi[:, :, :].bitcast(F32),
                            ALU.subtract).then_inc(ba_split, 1)
            dve.wait_ge(ld_bgu, 16)
            b32 = DT[0:NE, 0:4, :].rearrange("p a n -> p (a n)")
            rest = DT[0:NE, 4:8, :].rearrange("p a n -> p (a n)")
            parts = DT[0:NE, 8:12, :].rearrange("p a n -> p (a n)").bitcast(BF16)
            hi, mid = parts[:, 0:2 * FE], parts[:, 2 * FE:4 * FE]
            low = DT[0:NE, 4:6, :].rearrange("p a n -> p (a n)").bitcast(BF16)
            link(V.tensor_copy(hi, b32))
            link(V.tensor_tensor(rest, b32, hi, ALU.subtract))
            link(V.tensor_copy(mid, rest))
            link(V.tensor_tensor(b32, rest, mid, ALU.subtract))
            V.tensor_copy(low, b32).then_inc(split_done, 3)
            w_in_lower(2)
            dve.wait_ge(ba_mm, 1)
            V.tensor_copy(BAT, bank[7][0:2 * HB, :]).then_inc(ba_rows, 1)
            w_in_lower(3)
            dve.wait_ge(ba_done, 1)
            link(V.tensor_copy(BA, bank[7][:, 0:32]))
            ba = BA.rearrange("p (t c) -> p t c", c=8)
            xx = XX.rearrange("p (t h) -> p t h", h=HB)
            V.tensor_copy(BETA.rearrange("p (t h) -> p t h", h=HB), ba[:, :, 0:HB])
            link(V.tensor_tensor(xx, ba[:, :, HB:8], dtb[:, :].unsqueeze(1).to_broadcast([P, NT, HB]), ALU.add))
            V.scalar_tensor_tensor(SP1, XX, -1.0, XX, ALU.mult, ALU.max).then_inc(route_e, 1)

            def score(n):
                i = n % NT
                w = (i + 1) * P
                dve.wait_ge(sc_mm, n + 1)
                if n >= 3:
                    dve.wait_ge(tr_mm, n - 2)
                s = S2[:, n % 3, 0:w]
                V.scalar_tensor_tensor(s, bank[2 + n % 2][:, 0:w], EA ** -0.5,
                                       C[:, C_STRIP + P * (NT - 1 - i):C_STRIP + SEQ],
                                       ALU.mult, ALU.add).then_inc(sc_read, 1)
                dve.wait_ge(sc_read, n + 1)
                V.tensor_reduce(nmax[:, n:n + 1], s, AX.X, ALU.max, negate=True).then_inc(sc_max, 1)

            def normalise(n):
                i = n % NT
                dve.wait_ge(sc_exp, n + 1)
                link(V.reciprocal(rden[:, n:n + 1], den[:, n:n + 1]))
                s = S2[:, n % 3, 0:(i + 1) * P]
                V.tensor_scalar(s, s, rden[:, n:n + 1], None, ALU.mult).then_inc(p_norm, 1)

            def conv(c):
                g = 12 + c
                dve.wait_ge(proj_done, g + 1)
                src, dst = bank[g % 2], DT[:, c, :]
                link(V.tensor_scalar(dst, src, cw[:, c, 3:4], None, ALU.mult))
                for back in range(1, 4):
                    ins = V.scalar_tensor_tensor(dst[:, back:SEQ], src[:, 0:SEQ - back], cw[:, c, 3 - back:4 - back],
                                                 dst[:, back:SEQ], ALU.mult, ALU.add)
                    if back < 3:
                        link(ins)
                ins.then_inc(conv_done, 1)

            dve.wait_ge(ld_c, 16)
            for m in range(16):
                if m in (1, 4, 8):
                    w_in_lower({1: 4, 4: 5, 8: 6}[m])
                if m == 2:
                    dve.wait_ge(route_exp, 2)
                    link(V.tensor_scalar(E1, E1, 1.0, None, ALU.add))
                    V.reciprocal(BETA, E1)
                    link(V.scalar_tensor_tensor(SP1, XX, 0.0, SP1, ALU.max, ALU.add))
                    V.tensor_tensor(GG.rearrange("p (t h) -> p t h", h=HB), SP1.rearrange("p (t h) -> p t h", h=HB),
                                    na[:, :].unsqueeze(1).to_broadcast([P, NT, HB]), ALU.mult).then_inc(gates_f, 1)
                if m == 4:
                    dve.wait_ge(gc_mm, 1)
                    V.tensor_copy(GC, bank[7][:, 0:16])
                    link(V.tensor_copy(GL, bank[7][:, 16:32]))
                    V.tensor_tensor(EKD, GL, GC, ALU.subtract).then_inc(route_e, 1)
                if m == 6:
                    dve.wait_ge(route_exp, 5)
                    V.tensor_tensor(BKE, BETA, EGC, ALU.mult).then_inc(gsc_done, 1)
                score(2 * m)
                score(2 * m + 1)
                if 1 <= m <= 12:
                    if m == 1:
                        dve.wait_ge(st_bias, 48)
                    conv(m - 1)
                normalise(2 * m)
                normalise(2 * m + 1)

            for n in range(8):
                dve.wait_ge(nrm_rs, 1 + (n >= 4) + (n >= 6))
                d = DT[:, n, :]
                V.scalar_tensor_tensor(d, d, P ** -0.5 if n < HB else 1.0, bank[SUM_BANK[n]],
                                       ALU.mult, ALU.mult).then_inc(nrm_done, 1)
            dve.wait_ge(nrm_done, 8)

            def decays(h):
                a = 4 * (h % 2)
                dve.wait_ge(dp_e, h + 1)
                for t in range(NT):
                    s = slice(t * P, (t + 1) * P)
                    last = V.scalar_tensor_tensor(PT[:, h, s], bank[a][:, s], GC[:, t * HB + h:t * HB + h + 1], negm,
                                                  ALU.subtract, ALU.add)
                last.then_inc(dp_arg, 1)
                V.tensor_tensor(QK[:, h, :], DT[:, 4 + h, :], bank[a + 1], ALU.mult).then_inc(dp_kb, 1)

            def grams(h):
                a = 4 * (h % 2)
                dve.wait_ge(dp_la, h + 1)
                dve.wait_ge(dp_decs, h + 1)
                V.tensor_tensor(LT[:, h, :], bank[a + 2], S2[:, h % 2, :], ALU.mult).then_inc(dp_lt, 1)
                V.tensor_tensor(AT[:, h, :], bank[a + 3], PT[:, h, :], ALU.mult).then_inc(dp_lt, 1)
                dve.wait_ge(dp_tr, h + 1)
                for t in range(NT):
                    s = slice(t * P, (t + 1) * P)
                    last = V.tensor_scalar(KDEC[:, h, s], bank[a][:, s], EKD[:, t * HB + h:t * HB + h + 1], None,
                                           ALU.mult)
                    last = V.tensor_scalar(KB[:, h, s], bank[a][:, s], BKE[:, t * HB + h:t * HB + h + 1], None,
                                           ALU.mult)
                last.then_inc(dp_kdec, 1)

            dve.wait_ge(gsc_done, 1)
            decays(0)
            decays(1)
            for h in range(HB):
                grams(h)
                if h + 2 < HB:
                    decays(h + 2)

            dve.wait_ge(dd_ready, HB)
            with dve.Fori(0, LEVELS) as lv:
                level = C[:, bass.ds(lv * P + C_LEVEL, P)].unsqueeze(1).to_broadcast([P, NT, P])

                def mask_t1(h):
                    dve.wait_ge(inv_a, lv * HB + h + 1)
                    V.tensor_tensor(T1[:, h, :].rearrange("p (c n) -> p c n", n=P),
                                    bank[3 * (h % 2)].rearrange("p (c n) -> p c n", n=P), level,
                                    ALU.mult).then_inc(inv_t1, 1)

                def update(h):
                    dve.wait_ge(inv_b, lv * HB + h + 1)
                    b = 3 * (h % 2) + 1
                    d = DD[:, h, :, :, :].rearrange("p c s n -> p (c s n)")
                    V.tensor_tensor(d, d, PS[:, b:b + 2, :].rearrange("p b n -> p (b n)"),
                                    ALU.subtract).then_inc(dd_ready, 1)

                mask_t1(0)
                mask_t1(1)
                update(0)
                mask_t1(2)
                update(1)
                mask_t1(3)
                update(2)
                update(3)

            def state(c):
                dve.wait_ge(scan_s, c + 1)
                for h in range(HB):
                    hs = slice(h * P, (h + 1) * P)
                    V.scalar_tensor_tensor(ST[(c + 1) % 2][:, hs], ST[c % 2][:, hs],
                                           EGL[:, c * HB + h:c * HB + h + 1], bank[1][:, hs],
                                           ALU.mult, ALU.add).then_inc(scan_st, 1)
                dve.wait_ge(scan_st, HB * (c + 1))

            def y_scale(c):
                dve.wait_ge(rms_done, c + 1)
                link(V.reciprocal(RSD[:, c * HB:(c + 1) * HB], RSD[:, c * HB:(c + 1) * HB]))
                if c:
                    dve.wait_ge(yt_mm, c)
                for h in range(HB):
                    hs = slice(h * P, (h + 1) * P)
                    last = V.scalar_tensor_tensor(YT[:, hs], bank[2 + c % 2][:, hs],
                                                  RSD[:, c * HB + h:c * HB + h + 1], nw[:, :], ALU.mult, ALU.mult)
                last.then_inc(y_norm, 1)

            def centre(t, g, norm=0):
                row = X1[:, t, :]
                V.bn_stats(stat[:, 0:6], row[:, 0:512])
                link(V.bn_stats(stat[:, 6:12], row[:, 512:1024]))
                V.bn_aggr(mv, stat).then_inc(ln_mv, 1)
                dve.wait_ge(ln_mv, norm * NT + t + 1)
                link(V.scalar_tensor_tensor(row, row, mv[:, 0:1], g, ALU.subtract, ALU.mult))

            def divide_shift(t, b, done, norm=0):
                dve.wait_ge(ln_std, norm * NT + t + 1)
                link(V.reciprocal(rstd[:, t:t + 1], std[:, t:t + 1]))
                row = X1[:, t, :]
                V.scalar_tensor_tensor(row, row, rstd[:, t:t + 1], b, ALU.mult, ALU.add).then_inc(done, 1)

            def residual(c):
                dve.wait_ge(mix_mm, c + 1)
                if c == 0:
                    dve.wait_ge(ld_x, 16)
                V.scalar_tensor_tensor(X1[:, c, :], X1[:, c, :], ALPHA, PS[:, 5:7, :].rearrange("p b n -> p (b n)"),
                                       ALU.mult, ALU.add).then_inc(mix_read, 1)
                dve.wait_ge(mix_read, c + 1)
                if c == 0:
                    dve.wait_ge(ld_ln, 32)
                centre(c, LN[:, 0, :])
                divide_shift(c, LN[:, 1, :], x1_ready)

            state(0)
            y_scale(0)
            state(1)
            y_scale(1)
            state(2)
            y_scale(2)
            residual(0)
            y_scale(3)
            residual(1)
            residual(2)
            residual(3)

            dve.wait_ge(rt_t, 1)
            V.tensor_scalar(logitT, bank[0][0:NE, :], b_rt[:, :], None, ALU.add).then_inc(rt_biased, 1)
            dve.wait_ge(rt_mm, 1)
            link(V.tensor_copy(logit[:, :, :].rearrange("p t e -> p (t e)"), bank[1][:, 0:NT * NE]))
            for t in range(NT):
                link(V.max(topv[:, t, :], logit[:, t, :]))
                last = V.max_index(topi[:, t, :], topv[:, t, :], logit[:, t, :])
            link(last)
            link(V.tensor_copy(topf[:, :, :], topi[:, :, 0:TOPK]))
            V.tensor_tensor(gate[:, :, :], topv[:, :, 0:TOPK], topv[:, :, 0:1].to_broadcast([P, NT, TOPK]),
                            ALU.subtract).then_inc(route_e, 1)
            esel = C[:, C_ESEL:C_ESEL + NE]
            ebase = C[:, C_EBASE:C_EBASE + NE]
            n_tk = NT * TOPK
            link(V.tensor_tensor(onehot, esel.unsqueeze(1).to_broadcast([P, n_tk, NE]),
                                 topf[:, :, :].rearrange("p t k -> p (t k)").unsqueeze(2).to_broadcast([P, n_tk, NE]),
                                 ALU.is_equal))
            V.tensor_reduce(memb[:, :, :], onehot.rearrange("p (t k) e -> p t e k", k=TOPK), AX.X,
                            ALU.add).then_inc(rt_memb, 1)
            dve.wait_ge(route_exp, 6)
            link(V.tensor_reduce(gsum[:, :, 0], gate[:, :, :], AX.X, ALU.add))
            link(V.reciprocal(gsum[:, :, 0], gsum[:, :, 0]))
            link(V.tensor_tensor(gate[:, :, :], gate[:, :, :], gsum[:, :, :].to_broadcast([P, NT, TOPK]), ALU.mult))
            gate_f = gate[:, :, :].rearrange("p t k -> p (t k)").unsqueeze(2)
            V.tensor_copy(pay[:, :, 2:3].bitcast(F32), gate_f)
            link(V.tensor_tensor(work, onehot, gate_f.to_broadcast([P, n_tk, NE]), ALU.mult))
            V.tensor_reduce(gmat[:, :, :], work.rearrange("p (t k) e -> p t e k", k=TOPK), AX.X,
                            ALU.add).then_inc(gm_ready, 1)
            dve.wait_ge(pos_mm, 1)
            dve.wait_ge(gm_ready, 1)
            link(V.tensor_tensor(logit[:, :, :], bank[1][:, 0:NT * NE].rearrange("p (t e) -> p t e", e=NE),
                                 ebase.unsqueeze(1).to_broadcast([P, NT, NE]), ALU.add))
            for t in range(NT):
                ks = slice(t * TOPK, (t + 1) * TOPK)
                last = V.tensor_tensor(work[:, ks, :], onehot[:, ks, :],
                                       logit[:, t, :].unsqueeze(1).to_broadcast([P, TOPK, NE]), ALU.mult)
            link(last)
            link(V.tensor_reduce(rowf[:, :], work, AX.X, ALU.add))
            V.tensor_copy(rowi[:, :], rowf[:, :]).then_inc(rows_ready, 1)
            count = bank[1][:, NT * NE:(NT + 1) * NE]
            more, upto = extra_f[:, 0:NE], extra_f[:, NE:2 * NE]
            xe, xs = extra_f[:, 64:80], extra_f[:, 80:96]
            jj = C[:, C_ESEL:C_ESEL + 16]
            link(V.tensor_scalar(more, count, float(P), None, ALU.is_gt))
            link(V.scalar_tensor_tensor(more, count, 2.0 * P, more, ALU.is_gt, ALU.add))
            link(V.scalar_tensor_tensor(more, count, 3.0 * P, more, ALU.is_gt, ALU.add))
            link(V.tensor_tensor_scan(upto, ones[:, 0:NE], more, 0.0, ALU.mult, ALU.add))
            link(V.tensor_tensor(work, upto.unsqueeze(1).to_broadcast([P, 16, NE]),
                                 jj.unsqueeze(2).to_broadcast([P, 16, NE]), ALU.is_le))
            link(V.tensor_reduce(xe, work, AX.X, ALU.add))
            link(V.tensor_tensor(work, work, more.unsqueeze(1).to_broadcast([P, 16, NE]), ALU.mult))
            link(V.tensor_reduce(xs, work, AX.X, ALU.add))
            link(V.tensor_scalar(xe, xe, float(NE - 1), None, ALU.min))
            link(V.tensor_tensor(xs, jj, xs, ALU.subtract))
            link(V.tensor_scalar(xs, xs, 1.0, float(P), ALU.add, ALU.mult))
            link(V.scalar_tensor_tensor(xs, xe, float(CAP), xs, ALU.mult, ALU.add))
            link(V.tensor_scalar(xs, xs, float(NE * CAP - P), None, ALU.min))
            V.tensor_copy(extra_i[:, 0:16], xe)
            V.tensor_copy(extra_i[:, 16:32], xs)
            V.tensor_copy(extra_i[:, 32:33], upto[:, NE - 1:NE]).then_inc(extra_ready, 1)

            dve.wait_ge(st_x1, 16 * NT)
            for t in range(NT):
                dve.wait_ge(ple_sig, t + 1)
                dve.wait_ge(ple_mm, t + 1)
                link(V.tensor_tensor(s_ple, s_ple, PS[:, 4:6, :], ALU.mult))
                row = X1[:, t, :].rearrange("p (b n) -> p b n", b=2)
                link(V.scalar_tensor_tensor(row, row, ALPHA, s_ple, ALU.mult, ALU.add))
                V.tensor_tensor(row, row, PS[:, 6:8, :], ALU.add).then_inc(ple_read, 1)
                if t == 1:
                    dve.wait_ge(xh_ready, 1)
                    V.tensor_tensor(xl[:, :, :],
                                    PS[:, 0:2, :].rearrange("p b n -> p (b n)").rearrange("p (k n) -> p k n", k=KD),
                                    xh[:, :, :].bitcast(F32), ALU.subtract).then_inc(xl_ready, 1)
                    dve.wait_ge(hi_ready, 1)
                    V.tensor_tensor(w_lo[:, 0, :], gu_tile[0], w_hi[:, 0, :].bitcast(F32),
                                    ALU.subtract).then_inc(lo_ready, 1)

            six_seven = PS[:, 6:8, :].rearrange("p b n -> p (b n)").rearrange("p (k n) -> p k n", k=KD)

            def lo_parts(raws, at, first, last):
                for k in range(first, last):
                    dve.wait_ge(hi_ready, at + k + 1)
                    if not isinstance(at, int) or at + k >= 2:
                        dve.wait_ge(w_used, at + k - 1)
                    V.tensor_tensor(w_lo[:, k % 2, :], raws[k], w_hi[:, k % 2, :].bitcast(F32),
                                    ALU.subtract).then_inc(lo_ready, 1)

            def clamp(i, at):
                dve.wait_ge(w_used, at + KD)
                if not isinstance(i, int) or i:
                    dve.wait_ge(at_mm, i)
                V.tensor_scalar(g_t, PS[:, 0:2, :].rearrange("p b n -> p (b n)"), 7.0, None,
                                ALU.min).then_inc(g_ready, 1)
                V.tensor_scalar(u_t, PS[:, 2:4, :].rearrange("p b n -> p (b n)"), 7.0, -7.0,
                                ALU.min, ALU.max).then_inc(h_read, 1)
                dve.wait_ge(sig_ready, i + 1)
                V.tensor_tensor(s_t, g_t, s_t, ALU.mult).then_inc(m_ready, 1)

            def swiglu(i):
                dve.wait_ge(h_read, i + 1)
                dve.wait_ge(m_ready, i + 1)
                V.scalar_tensor_tensor(g_t, u_t, 1.0, s_t, ALU.add, ALU.mult).then_inc(act_ready, 1)

            def rows_rest(i):
                dve.wait_ge(xh_ready, i + 1)
                V.tensor_tensor(xl[:, :, :], six_seven, xh[:, :, :].bitcast(F32), ALU.subtract).then_inc(xl_ready, 1)

            def acts_rest(i):
                dve.wait_ge(ah_ready, i + 1)
                V.tensor_tensor(al[:, :, :], six_seven, ah[:, :, :].bitcast(F32), ALU.subtract).then_inc(al_ready, 1)

            dve.wait_ge(ple_read, NT)
            lo_parts(gu_tile, gu_at(0), 1, KD)
            rows_rest(1)
            clamp(0, gu_at(0))
            swiglu(0)

            def turn(i, rows=True):
                lo_parts(gu_tile, gu_at(i), 0, 2)
                acts_rest(i - 1)
                lo_parts(gu_tile, gu_at(i), 2, KD)
                lo_parts(dn_raw, dn_at(i - 1), 0, 2)
                clamp(i, gu_at(i))
                lo_parts(dn_raw, dn_at(i - 1), 2, 3)
                swiglu(i)
                if rows:
                    rows_rest(i + 1)
                lo_parts(dn_raw, dn_at(i - 1), 3, 4)

            with dve.Fori(1, NE - 1) as i:
                turn(i)
            turn(NE - 1, rows=False)
            lo_parts(dn_raw, DN_LAST, 0, 2)
            acts_rest(NE - 1)
            lo_parts(dn_raw, DN_LAST, 2, 4)
            dve.wait_ge(extra_ready, 1)
            n_extra = dve.value_load(extra_i[0:1, 32:33], min_val=0, max_val=15)
            with dve.If(n_extra > 0):
                with dve.Fori(0, n_extra) as j:
                    rows_rest(j + NE)
                    lo_parts(gu_tile, extra_at(j), 0, KD)
                    clamp(j + NE, extra_at(j))
                    swiglu(j + NE)
                    acts_rest(j + NE)
                    lo_parts(dn_raw, extra_at(j) + KD, 0, 4)
            for t in range(NT):
                row = X1[:, t, :]
                dve.wait_ge(ld_y[t][1], 32)
                for k in (2, 3):
                    link(V.tensor_tensor(row, row, y_in(t, k), ALU.add))
                dve.wait_ge(fin_pair, t + 1)
                link(V.tensor_tensor(row, row, y_in(t, 0), ALU.add))
                if t == 0:
                    dve.wait_ge(ld_ln2, 32)
                centre(t, LN2[:, 0, :], norm=1)
                if t < NT - 1:
                    dve.wait_ge(ln_std, NT + t + 1)
                    V.reciprocal(rstd[:, t:t + 1], std[:, t:t + 1]).then_inc(fin_rstd, 1)
                else:
                    divide_shift(t, LN2[:, 1, :], fin_last, norm=1)

        @block.gpsimd
        def _(pool):
            G = nc.gpsimd
            pool.wait_ge(proj_done, 24)
            pool.wait_ge(silu_done, 2)
            for n in range(8):
                G.tensor_tensor(SQ[:, n, :], DT[:, n, :], DT[:, n, :], ALU.mult).then_inc(sq_done, 1)
            pool.wait_ge(proj_done, 28)
            G.memset(ST[0], 0.0).then_inc(st_zero, 1)
            pool.wait_ge(ld_c, 16)
            for h in range(HB):
                G.tensor_copy(DD[:, h, :, :, :].rearrange("p c s n -> p (c s) n"),
                              ident.unsqueeze(1).to_broadcast([P, 2 * NT, P])).then_inc(dd_ready, 1)

            def strict_decay(h):
                pool.wait_ge(dp_dec, h + 1)
                if h >= 2:
                    pool.wait_ge(dp_lt, 2 * (h - 1))
                G.tensor_tensor(S2[:, h % 2, :].rearrange("p (c n) -> p c n", n=P),
                                PT[:, h, :].rearrange("p (c n) -> p c n", n=P),
                                strict.unsqueeze(1).to_broadcast([P, NT, P]), ALU.mult).then_inc(dp_decs, 1)

            def decay_q(h):
                pool.wait_ge(dp_la, h + 1)
                pool.wait_ge(dp_e, h + 1)
                G.tensor_tensor(DT[:, h, :], DT[:, h, :], QK[:, 4 + h, :], ALU.mult).then_inc(dp_qdec, 1)

            pool.wait_ge(nrm_mm, 8)
            pool.wait_ge(nrm_done, 8)
            strict_decay(0)
            strict_decay(1)
            for h in range(HB):
                decay_q(h)
                if h + 2 < HB:
                    strict_decay(h + 2)

            def gate_y(c):
                pool.wait_ge(y_norm, c + 1)
                G.tensor_tensor(YT, YT, ZT[:, c, :], ALU.mult).then_inc(y_gated, 1)

            pool.wait_ge(silu_done, 4)
            for c in range(NT):
                gate_y(c)
            pool.wait_ge(y_gated, NT)
            G.memset(xg, 0.0).then_inc(xg_zero, 1)
            pool.wait_ge(st_table, 16)
            pool.wait_ge(rows_ready, 1)
            for n in range(NT * TOPK):
                G.indirect_dma_start(table, bass.IndirectOffsetOnAxis(rowi[:, n:n + 1], 0), pay[:, n, :], None
                                     ).then_inc(tab_done, 16)
            pool.wait_ge(ld_slots, 16)
            pool.wait_ge(st_x1, 16 * NT)
            pool.wait_ge(xg_zero, 1)

            def held():
                pool.sem_inc(pool_steps, 1)

            def gather(i, tokens):
                G.tensor_copy(g_idx[:, :], tokens).then_inc(gi_ready, 1)
                pool.wait_ge(gi_ready, i + 1)
                held()
                G.indirect_dma_start(xg, None, x1_rows,
                                     bass.IndirectOffsetOnAxis(g_idx[:, :].bitcast(U32), 0),
                                     bounds_check=SEQ - 1, oob_is_err=False).then_inc(gathered, 16)

            def take_slots(what):
                G.tensor_copy(d_idx[:, :], what).then_inc(dg_ready, 1)

            def send(i):
                pool.wait_ge(y_evac, i + 2)
                held()
                G.indirect_dma_start(y_rows, bass.IndirectOffsetOnAxis(d_idx[:, 0:1].bitcast(U32), 0), y_t, None,
                                     bounds_check=SEQ * TOPK - 1, oob_is_err=False).then_inc(y_sent, 16)

            gather(0, slots[:, 0, 0:1])
            pool.wait_ge(xgt_mm, 1)
            gather(1, slots[:, 1, 0:1])
            take_slots(slots[:, 0, 1:3])
            with pool.Fori(1, NE - 1) as i:
                pool.wait_ge(xgt_mm, i + 1)
                held()
                gather(i + 1, slots[:, bass.ds(i + 1, 1), 0:1].rearrange("p a b -> p (a b)"))
                send(i - 1)
                pool.wait_ge(y_sent, i * 16)
                held()
                take_slots(slots[:, bass.ds(i, 1), 1:3].rearrange("p a b -> p (a b)"))
            send(NE - 2)
            pool.wait_ge(y_sent, (NE - 1) * 16)
            take_slots(slots[:, NE - 1, 1:3])
            send(NE - 1)
            pool.wait_ge(extra_ready, 1)
            n_extra = pool.value_load(extra_i[0:1, 32:33], min_val=0, max_val=15)
            with pool.If(n_extra > 0):
                with pool.Fori(0, n_extra) as j:
                    pool.wait_ge(ld_xslot, j * 16 + 16)
                    pool.wait_ge(xgt_mm, j + NE)
                    pool.wait_ge(y_sent, (j + NE) * 16)
                    held()
                    gather(j + NE, xslot[:, 0:1])
                    take_slots(xslot[:, 1:3])
                    send(j + NE)
            def pair(t):
                pool.wait_ge(ld_y[t][0], 32)
                G.tensor_tensor(y_in(t, 0), y_in(t, 0), y_in(t, 1), ALU.add).then_inc(fin_pair, 1)

            def shift(t):
                pool.wait_ge(fin_scaled, t + 1)
                G.tensor_tensor(X1[:, t, :], X1[:, t, :], LN2[:, 1, :], ALU.add).then_inc(fin_done, 1)

            pool.wait_ge(ld_ln2, 32)
            pair(0)
            pair(1)
            for t in range(NT - 1):
                shift(t)
                if t + 2 < NT:
                    pair(t + 2)


_OUT = (SEQ, D)


def kernel(**inputs):
    import numpy as _np
    import concourse.bacc as _bacc
    from concourse import mybir as _mybir
    from concourse.bass_utils import run_bass_kernel_spmd as _run

    a = {k: _np.asarray(v) for k, v in inputs.items()}
    arrays = {
        "x": a["x"].reshape(SEQ, D),
        "xT": a["x"].reshape(SEQ, KD, P).transpose(2, 1, 0),
        "pT": a["p"].reshape(SEQ, PLE // P, P).transpose(2, 1, 0),
        "w_in": a["w_in"],
        "conv_w": a["conv_w"].reshape(4, 12, P).transpose(2, 1, 0),
        "a_log": a["a_log"].reshape(HB), "dt_bias": a["dt_bias"].reshape(HB), "gnorm_w": a["gnorm_w"].reshape(P),
        "w_out": a["w_out"], "ln1_g": a["ln1_g"].reshape(D), "ln1_b": a["ln1_b"].reshape(D),
        "w_router": a["w_router"], "b_router": a["b_router"],
        "w_gate_up": a["w_gate_up"], "b_gate_up": a["b_gate_up"], "w_down": a["w_down"], "b_down": a["b_down"],
        "w_ple_gate": a["w_ple_gate"], "b_ple_gate": a["b_ple_gate"], "w_ple_proj": a["w_ple_proj"],
        "ln2_g": a["ln2_g"].reshape(D), "ln2_b": a["ln2_b"].reshape(D),
        "consts": constants(), "table0": table_rows(), "pay0": payload(),
    }
    arrays = {f"in_{k}_dram": _np.ascontiguousarray(v) for k, v in arrays.items()}
    nc = _bacc.Bacc("TRN2", target_bir_lowering=False, num_devices=1)
    args = [nc.dram_tensor(n, v.shape, _mybir.dt.from_np(v.dtype), kind="ExternalInput").ap()
            for n, v in arrays.items()]
    args.append(nc.dram_tensor("out_0_dram", _OUT, _mybir.dt.float32, kind="ExternalOutput").ap())
    hybrid_layer(nc, *args)
    r = _run(nc, [arrays], core_ids=[0])
    return r.results[0]["out_0_dram"].reshape(1, SEQ, D)
```

```python
import math
from contextlib import ExitStack

import numpy as np
import concourse.bass as bass
from concourse import mybir

F32 = mybir.dt.float32
F32R = mybir.dt.float32r
BF16 = mybir.dt.bfloat16
I32 = mybir.dt.int32
U32 = mybir.dt.uint32
ALU = mybir.AluOpType
ACT = mybir.ActivationFunctionType
AX = mybir.AxisListType

P = 128
SEQ = 512
D = 1024
NT = SEQ // P
KD = D // P
HA, EA = 8, 64
HB = 4
PLE = 256
NE = 32
TOPK = 4
FE = 1024
KF = FE // P
TW = 2 * FE
BLOCK_TILES = KD + KF // 2
ALPHA = 2.0 ** 0.25
LN_EPS, RMS_EPS, L2_EPS = 1e-5, 1e-6, 1e-6
NEG = -1.0e30
LEVELS = 7
NBLK = 7
SLOTS = 3
BLK = KD * 512
CAP = SEQ
SKIP = 1 << 20

C_IDENT, C_ONES, C_UPPER, C_NEGM, C_STRICT = 0, 128, 256, 384, 512
C_STRIP = 640
C_LEVEL = C_STRIP + SEQ
C_ESEL = C_LEVEL + LEVELS * P
C_EBASE = C_ESEL + NE
C_TOTAL = C_EBASE + NE


def constants():
    c = np.zeros((P, C_TOTAL), np.float32)
    r = np.arange(P)
    c[:, C_IDENT:C_IDENT + P] = np.eye(P)
    c[:, C_ONES:C_ONES + P] = 1.0
    c[:, C_UPPER:C_UPPER + P] = r[:, None] <= r[None, :]
    c[:, C_NEGM:C_NEGM + P] = np.where(r[:, None] <= r[None, :], 0.0, NEG)
    c[:, C_STRICT:C_STRICT + P] = r[:, None] < r[None, :]
    dist = (SEQ - P) + r[:, None] - np.arange(SEQ)[None, :]
    count = np.zeros((P, SEQ))
    for window, dil in ((128, 1), (512, 4), (2048, 16)):
        count += (dist >= 0) & (dist % dil == 0) & (dist <= window // dil * dil)
    c[:, C_STRIP:C_STRIP + SEQ] = np.where(count > 0, np.log(np.maximum(count, 1)), NEG)
    for lv in range(LEVELS):
        m = 1 << lv
        same = (r[:, None] // (2 * m)) == (r[None, :] // (2 * m))
        off = ((r[:, None] // m) % 2 == 1) & ((r[None, :] // m) % 2 == 0)
        mask = same & off
        c[:, C_LEVEL + lv * P:C_LEVEL + (lv + 1) * P] = mask if lv else mask.T
    c[:, C_ESEL:C_ESEL + NE] = np.arange(NE)
    c[:, C_EBASE:C_EBASE + NE] = np.arange(NE) * CAP
    return c


def table_rows():
    t = np.zeros((P, NE * CAP // P * 4), np.int32)
    t[:, 0::4] = SKIP
    t[:, 1::4] = SKIP
    return t


def payload():
    t = np.zeros((P, NT, TOPK, 4), np.int32)
    for tt in range(NT):
        tok = tt * P + np.arange(P)
        t[:, tt, :, 0] = tok[:, None]
        t[:, tt, :, 1] = tok[:, None] * TOPK + np.arange(TOPK)
    return t.reshape(P, NT * TOPK * 4)


def hybrid_layer(nc, x, xT, pT, w_in, conv_w, a_log, dt_bias, gnorm_w, w_out, ln1_g, ln1_b,
                 w_router, b_router, w_gate_up, b_gate_up, w_down, b_down,
                 w_ple_gate, b_ple_gate, w_ple_proj, ln2_g, ln2_b, consts, table0, pay0, out):
    ctx = ExitStack()
    with ctx:
        def sb(name, shape, dt=F32):
            return ctx.enter_context(nc.sbuf_tensor(name, shape, dt))

        def sem(name):
            return ctx.enter_context(nc.semaphore(name))

        x1_rows = nc.dram_tensor("x1_rows", (SEQ, D), F32, kind="Internal").ap()
        x1_cols = nc.dram_tensor("x1_cols", (P, KD, SEQ), F32, kind="Internal").ap()
        y_rows = nc.dram_tensor("y_rows", (SEQ * TOPK, D), F32, kind="Internal").ap()
        table = nc.dram_tensor("dispatch_table", (NE * CAP, 4), I32, kind="Internal").ap()
        bias_parts = nc.dram_tensor("bias_parts", (NE, 3, 2 * FE), BF16, kind="Internal").ap()

        with nc.sbuf_tensor("W", [P, 3 * FE * KD], F32) as W:
            pass
        WR = sb("WR", [P, 3 * FE * KD], F32R)

        def w_in_view(ring, s):
            return ring[:, s * BLK:(s + 1) * BLK].rearrange("p (k n) -> p k n", k=KD)

        w_in_raw = [w_in_view(W, s) for s in range(SLOTS)]
        w_in_lo = [w_in_view(WR, s) for s in range(SLOTS)]
        w_in_hi = [w_in_view(WR, SLOTS + s) for s in range(2)]
        XTH = w_in_view(WR, SLOTS + 2)
        gu_tile = [W[:, k * 2 * FE:(k + 1) * 2 * FE] for k in range(KD)]
        dn_tile = [W[:, (2 * KD + k) * FE:(2 * KD + k + 1) * FE] for k in range(KF)]
        LT = W[:, 0:2048].rearrange("p (h n) -> p h n", h=HB)
        KB = W[:, 2048:4096].rearrange("p (h n) -> p h n", h=HB)
        KDEC = W[:, 4096:6144].rearrange("p (h n) -> p h n", h=HB)
        VB = W[:, 6144:8192].rearrange("p (h n) -> p h n", h=HB)
        AT = W[:, 8192:10240].rearrange("p (h n) -> p h n", h=HB)
        T1 = W[:, 10240:12288].rearrange("p (h n) -> p h n", h=HB)
        SQ = W[:, (SLOTS + 1) * BLK:(SLOTS + 2) * BLK].rearrange("p (n c) -> p n c", n=8)
        DD = W[:, 12288:16384].rearrange("p (h c s n) -> p h c s n", h=HB, c=NT, s=2)
        PG = [W[:, o:o + BLK].rearrange("p (k n) -> p k n", k=KD) for o in (6 * TW, 6 * TW)]
        X1C = W[:, 4 * TW:6 * TW].rearrange("p (k n) -> p k n", k=KD)

        QK = sb("QK", [P, KD, SEQ])
        X1 = QK[:, :, :].rearrange("p k n -> p (k n)").rearrange("p (t n) -> p t n", t=NT)
        ZT = sb("ZT", [P, NT, SEQ])
        S2 = sb("S2", [P, 3, SEQ])
        with ExitStack() as front:
            def sf(name, shape):
                return front.enter_context(nc.sbuf_tensor(name, shape, F32))

            with nc.sbuf_tensor("XA", [P, KD, SEQ], F32) as XA:
                pass
            XTL = front.enter_context(nc.sbuf_tensor("XTL", [P, KD, SEQ], F32R))
            MXA = sf("MXA", [P, 4, SEQ])
            PT = sf("PT", [P, 4, SEQ])
            DT = sf("DT", [P, 12, SEQ])
            VT = sf("VT", [P, NT, SEQ])
        w_hi = sb("w_hi", [P, 2, TW], F32R)
        w_lo = sb("w_lo", [P, 2, TW], F32R)
        xh, xl, ah, al = (sb(n, [P, KD, P], F32R) for n in ("xh", "xl", "ah", "al"))
        ET = sb("ET", [P, 4, FE])
        g_t, u_t, s_t, y_t = (ET[:, j, :] for j in range(4))
        MXB = XA[:, 0:4, :]
        ST = [XA[:, 4, :], XA[:, 5, :]]
        VN = XA[:, 6, :]
        YT = XA[:, 7, :]
        X1T = DT[:, 4:12, :]
        xg = ZT[:, 0:2, :].rearrange("p a n -> p (a n)")
        PJ = (VT[:, 0:2, :], ZT[:, 2:4, :])
        LN = PT[:, :, :].rearrange("p a n -> p (a n)").rearrange("p (k n) -> p k n", k=2)
        LN2 = W[:, 8 * TW:9 * TW].rearrange("p (k n) -> p k n", k=2)

        def y_in(t, k):
            tile = ((0, 1), (2, 3), (9, 10), (11, 0))[t][k // 2]
            return W[:, tile * TW + (k % 2) * D:tile * TW + (k % 2 + 1) * D]

        C = sb("C", [P, C_TOTAL])
        ident = C[:, C_IDENT:C_IDENT + P]
        ones = C[:, C_ONES:C_ONES + P]
        upper = C[:, C_UPPER:C_UPPER + P]
        negm = C[:, C_NEGM:C_NEGM + P]
        strict = C[:, C_STRICT:C_STRICT + P]
        w_ba = sb("w_ba", [P, KD, 2 * HB])
        w_ba_hi, w_ba_lo = (sb(n, [P, KD, 2 * HB], F32R) for n in ("w_ba_hi", "w_ba_lo"))
        cw = sb("cw", [P, 12, 4])
        na = sb("na", [P, HB])
        dtb = sb("dtb", [P, HB])
        nw = sb("nw", [P, P])
        w_rt = sb("w_rt", [P, KD, NE])
        b_rt = sb("b_rt", [NE, 1])
        logitT = DT[0:NE, 1, :]
        b_dn = XA[0:NE, 6:8, :].rearrange("p a n -> p (a n)")
        b_pg = (VT[0:1, 2, :], S2[0:1, 2, :])
        small = sb("small", [P, 512])
        cols = [small[:, j * 16:(j + 1) * 16] for j in range(32)]
        BA = small[:, 0:32]
        BAT = S2[0:2 * HB, 2, :]
        BETA, GG, GC, GL, EGC, EGL, EKD, BKE, XX, E1, SP1 = cols[2:13]
        nmax, den, rden = (small[:, 208 + 32 * j:240 + 32 * j] for j in range(3))
        MS, RSD = cols[19], cols[20]
        stat = small[:, 336:336 + 12]
        mv = small[:, 348:350]
        std = small[:, 350:354]
        rstd = small[:, 354:358]
        shift_by = small[:, 358:362]
        junk = sb("junk", [P, P])
        eps_l2, eps_rms, eps_ln, one_c = (sb(n, [P, 1]) for n in ("eps_l2", "eps_rms", "eps_ln", "one_c"))
        s_ple = (XA[:, 4:6, :], ET[:, 1, :].rearrange("p (a n) -> p a n", a=2))
        logit = sb("logit", [P, NT, NE])
        topv = sb("topv", [P, NT, 8])
        topi = sb("topi", [P, NT, 8], U32)
        topf = sb("topf", [P, NT, TOPK])
        gate = sb("gate", [P, NT, TOPK])
        gsum = sb("gsum", [P, NT, 1])
        memb = sb("memb", [P, NT, NE])
        onehot = S2[:, 2, :].rearrange("p (n e) -> p n e", e=NE)
        work = DT[:, 1, :].rearrange("p (n e) -> p n e", e=NE)
        rowf = sb("rowf", [P, NT * TOPK])
        rowi = sb("rowi", [P, NT * TOPK], U32)
        gmat = sb("gmat", [P, NT, NE])
        gT = ZT[0:NE, 2, :]
        pay = sb("pay", [P, NT * TOPK, 4], I32)
        slots = sb("slots", [P, NE, 4], I32)
        xslot = sb("xslot", [P, 4], I32)
        extra_f = sb("extra_f", [P, 128])
        extra_i = sb("extra_i", [P, 64], I32)
        g_idx = sb("g_idx", [P, 1], I32)
        d_idx = sb("d_idx", [P, 2], I32)
        bias_t = C[0:3, C_STRIP:C_STRIP + FE].bitcast(BF16)
        ones3 = sb("ones3", [3, P], BF16)
        PS = ctx.enter_context(nc.psum_tensor("PS", [P, 8, 512], F32))
        PROJ_BANK = (4, 6)
        SUM_BANK = (2, 3, 4, 5, 0, 1, 6, 7)
        bank = [PS[:, b, :] for b in range(8)]

        ld_c, ld_small, ld_bgu = (sem(n) for n in ("ld_c", "ld_small", "ld_bgu"))
        ld_x0 = [sem(f"ld_x0_{q}") for q in range(4)]
        ld_w = [sem(f"ld_w{j}") for j in range(SLOTS)]

        def w_in_loads(blk):
            return 16 * (blk // SLOTS + (1 if blk % SLOTS else 0))

        ld_wout, ld_x, ld_ln, ld_ple = (sem(n) for n in ("ld_wout", "ld_x", "ld_ln", "ld_ple"))
        PLE_LOADS = (16 * 4, 16 * 8)
        st_bias, st_table, st_x1, ld_slots = (sem(n) for n in ("st_bias", "st_table", "st_x1", "ld_slots"))
        ld_gu = [sem(f"ld_gu{k}") for k in range(KD)]
        ld_dn = [sem(f"ld_dn{q}") for q in range(KF // 2)]
        ld_bias, ld_xslot, st_out = (sem(n) for n in ("ld_bias", "ld_xslot", "st_out"))
        ld_y = [[sem(f"ld_y{t}_{pair}") for pair in range(2)] for t in range(NT)]
        (split_done, x_hi, x_lo, wi_hi, wi_lo, proj_done, evac_done, conv_done, ba_split, ba_mm, ba_rows, ba_done, silu_done,
         sc_mm, sc_read, sc_exp, sc_max, p_norm, tr_mm, tr_evac, o_mm, o_evac,
         sq_done, nrm_mm, nrm_ln, nrm_rs, nrm_done, gates_f, gc_mm, gsc_done,
         dp_bc, dp_arg, dp_kb, dp_e, dp_dec, dp_decs, dp_la, dp_lt, dp_tr, dp_kdec, dp_kbvb, dp_qdec,
         dt_ready, dt_mm, dd_ready, inv_a, inv_t1, inv_b, w_mm, w_evac,
         st_zero, scan_v, scan_vn, scan_s, scan_st, scan_o, sq_sum, rms_done, y_norm, y_gated, yt_mm, mix_ready,
         mix_mm, mix_read, ln_mv, ln_std, x1_ready, xt_mm, xt_evac,
         rt_t, rt_biased, rt_mm, rt_memb, pos_mm, route_exp, route_e, gm_ready, gT_mm, gT_evac, extra_ready,
         ple_gmm, ple_mm, ple_sig, ple_read, rows_ready, tab_done,
         dch, ach) = (sem(n) for n in (
            "split_done x_hi x_lo wi_hi wi_lo proj_done evac_done conv_done ba_split ba_mm ba_rows ba_done silu_done "
            "sc_mm sc_read sc_exp sc_max p_norm tr_mm tr_evac o_mm o_evac "
            "sq_done nrm_mm nrm_ln nrm_rs nrm_done gates_f gc_mm gsc_done "
            "dp_bc dp_arg dp_kb dp_e dp_dec dp_decs dp_la dp_lt dp_tr dp_kdec dp_kbvb dp_qdec "
            "dt_ready dt_mm dd_ready inv_a inv_t1 inv_b w_mm w_evac "
            "st_zero scan_v scan_vn scan_s scan_st scan_o sq_sum rms_done y_norm y_gated yt_mm mix_ready "
            "mix_mm mix_read ln_mv ln_std x1_ready xt_mm xt_evac "
            "rt_t rt_biased rt_mm rt_memb pos_mm route_exp route_e gm_ready gT_mm gT_evac extra_ready "
            "ple_gmm ple_mm ple_sig ple_read rows_ready tab_done dch ach").split())
        (xg_zero, gathered, xgt_mm, xh_ready, xl_ready, hi_ready, lo_ready, hi_used, w_used, h_read, g_ready, sig_ready, m_ready,
         act_ready, at_mm, ah_ready, al_ready, y_evac, y_sent, dg_ready, gi_ready,
         fin_pair, fin_rstd, fin_scaled, fin_times, fin_done, pool_steps) = (sem(n) for n in (
            "xg_zero gathered xgt_mm xh_ready xl_ready hi_ready lo_ready hi_used w_used h_read g_ready sig_ready m_ready "
            "act_ready at_mm ah_ready al_ready y_evac y_sent dg_ready gi_ready "
            "fin_pair fin_rstd fin_scaled fin_times fin_done pool_steps").split())

        block = ctx.enter_context(nc.Block())
        w_in_k = w_in[0].rearrange("(k p) n -> p k n", p=P)
        w_out_k = w_out[0].rearrange("(k p) n -> p k n", p=P)
        w_pg_k = w_ple_gate[0].rearrange("(k p) n -> p k n", p=P)
        w_pj_k = w_ple_proj[0].rearrange("(k p) n -> p k n", p=P)
        gu_d = w_gate_up[0].rearrange("e (k p) n -> e k p n", p=P)
        dn_d = w_down[0].rearrange("e (q j p) n -> e q p j n", p=P, j=2)
        dn_raw = [W[:, (KD + q) * TW:(KD + q + 1) * TW] for q in range(KF // 2)]
        dn_pair = [t.rearrange("p (j n) -> p j n", j=2) for t in dn_raw]
        dn_last = gu_tile[0:KF // 2]

        def gu_at(i):
            return 0 if isinstance(i, int) and i == 0 else i * BLOCK_TILES - KF // 2

        def dn_at(i):
            return i * BLOCK_TILES + KD + BLOCK_TILES - KF // 2

        DN_LAST = NE * BLOCK_TILES - KF // 2

        def extra_at(j):
            return j * BLOCK_TILES + NE * BLOCK_TILES

        QUARTERS = [slice(q, q + KD // 4) for q in range(0, KD, KD // 4)]
        HALVES = [slice(q, q + KD // 2) for q in range(0, KD, KD // 2)]

        def split_steps(blk):
            return 2 * (blk + 1) if blk else 0

        def bank_free(eng, g):
            if g >= 2:
                f = g - 2
                if f < 12:
                    eng.wait_ge(evac_done, f + 1)
                elif f < 24:
                    eng.wait_ge(conv_done, f - 11)
                else:
                    eng.wait_ge(evac_done, f - 11)

        @block.sync
        def _(sp):
            for part, loaded in zip(QUARTERS, ld_x0):
                sp.dma_start(XA[:, part, :], xT[:, part, :]).then_inc(loaded, 16)
                sp.dma_start(w_in_raw[0][:, part, :], w_in_k[:, part, 0:512]).then_inc(loaded, 16)
            sp.dma_start(w_in_raw[1], w_in_k[:, :, 512:1024]).then_inc(ld_w[1], 16)
            sp.dma_start(C[:, :], consts).then_inc(ld_c, 16)
            sp.dma_start(DT[0:NE, 0:4, :].rearrange("p a n -> p (a n)"), b_gate_up[0]).then_inc(ld_bgu, 16)
            sp.dma_start(w_in_raw[2], w_in_k[:, :, 1024:1536]).then_inc(ld_w[2], 16)
            sp.dma_start(w_ba[:, :, :], w_in_k[:, :, 3584:3592]).then_inc(ld_small, 16)
            sp.dma_start(cw[:, :, :], conv_w).then_inc(ld_small, 16)
            sp.dma_start(na[:, :], a_log.partition_broadcast(P)).then_inc(ld_small, 16)
            sp.dma_start(dtb[:, :], dt_bias.partition_broadcast(P)).then_inc(ld_small, 16)
            sp.dma_start(nw[:, :], gnorm_w.partition_broadcast(P)).then_inc(ld_small, 16)
            sp.dma_start(w_rt[:, :, :], w_router[0].rearrange("(k p) n -> p k n", p=P)).then_inc(ld_small, 16)
            sp.dma_start(b_rt[:, :], b_router.rearrange("o n -> n o")).then_inc(ld_small, 16)
            sp.dma_start(pay[:, :, :].rearrange("p n w -> p (n w)"), pay0).then_inc(ld_small, 16)
            sp.dma_start(table.rearrange("(p r) w -> p (r w)", p=P), table0).then_inc(st_table, 16)
            sp.wait_ge(split_done, 3)
            parts = DT[0:NE, 8:12, :].rearrange("p a n -> p (a n)").bitcast(BF16)
            sp.dma_start(bias_parts[:, 0, :], parts[:, 0:2 * FE]).then_inc(st_bias, 16)
            sp.dma_start(bias_parts[:, 1, :], parts[:, 2 * FE:4 * FE]).then_inc(st_bias, 16)
            low = DT[0:NE, 4:6, :].rearrange("p a n -> p (a n)").bitcast(BF16)
            sp.dma_start(bias_parts[:, 2, :], low[:, 0:2 * FE]).then_inc(st_bias, 16)
            for j in range(SLOTS, NBLK):
                sp.wait_ge(proj_done, 4 * (j - SLOTS + 1))
                sp.dma_start(w_in_raw[j % SLOTS], w_in_k[:, :, j * 512:(j + 1) * 512]).then_inc(ld_w[j % SLOTS], 16)
            sp.wait_ge(proj_done, 28)
            sp.wait_ge(nrm_mm, 8)
            sp.dma_start(W[:, 16384:24576].rearrange("p (k n) -> p k n", k=KD), w_out_k).then_inc(ld_wout, 16)
            sp.wait_ge(o_mm, HA)
            sp.dma_start(PJ[0], w_pj_k[:, :, 0:512]).then_inc(ld_ple, 16)
            sp.wait_ge(dp_la, HB)
            sp.wait_ge(dp_qdec, HB)
            sp.dma_start(X1, x.rearrange("(t p) n -> p t n", p=P)).then_inc(ld_x, 16)
            sp.wait_ge(dp_lt, 2 * HB)
            sp.dma_start(LN[:, 0, :], ln1_g.partition_broadcast(P)).then_inc(ld_ln, 16)
            sp.dma_start(LN[:, 1, :], ln1_b.partition_broadcast(P)).then_inc(ld_ln, 16)
            sp.dma_start(S2[:, 0:2, :], pT).then_inc(ld_ple, 16)
            sp.dma_start(b_pg[0], b_ple_gate[:, 0:512]).then_inc(ld_ple, 16)
            sp.wait_ge(scan_o, NT)
            sp.dma_start(PG[0], w_pg_k[:, :, 0:512]).then_inc(ld_ple, 16)
            for k in range(6):
                sp.dma_start(gu_tile[k], gu_d[0, k]).then_inc(ld_gu[k], 16)
            sp.wait_ge(st_bias, 48)
            sp.dma_start(bias_t, bias_parts[0]).then_inc(ld_bias, 16)
            sp.wait_ge(x1_ready, 1)
            sp.dma_start(x1_rows[0:P, :], X1[:, 0, :]).then_inc(st_x1, 16)
            sp.wait_ge(mix_mm, NT)
            for q in range(KF // 2):
                sp.dma_start(dn_pair[q], dn_d[0, q]).then_inc(ld_dn[q], 16)
            sp.wait_ge(scan_vn, NT)
            sp.wait_ge(yt_mm, NT)
            sp.dma_start(b_dn, b_down[0]).then_inc(ld_wout, 16)
            for t in range(1, NT):
                sp.wait_ge(x1_ready, t + 1)
                sp.dma_start(x1_rows[t * P:(t + 1) * P, :], X1[:, t, :]).then_inc(st_x1, 16)
            sp.wait_ge(xt_evac, 2 * NT)
            sp.dma_start(x1_cols, X1T).then_inc(st_x1, 16)
            sp.wait_ge(tab_done, 16 * NT * TOPK)
            sp.dma_start(slots[:, :, :], table.rearrange("(e c) w -> c e w", c=CAP)[0:P]).then_inc(ld_slots, 16)
            sp.wait_ge(ple_mm, NT)
            for k in (6, 7):
                sp.dma_start(gu_tile[k], gu_d[0, k]).then_inc(ld_gu[k], 16)
            sp.dma_start(PJ[1], w_pj_k[:, :, 512:1024]).then_inc(ld_ple, 16)
            sp.dma_start(b_pg[1], b_ple_gate[:, 512:1024]).then_inc(ld_ple, 16)

            def load_gate_up(e, before):
                for k in range(KD):
                    sp.wait_ge(lo_ready, before + k + 1)
                    sp.dma_start(gu_tile[k], gu_d[e, k]).then_inc(ld_gu[k], 16)
                    if k == 2:
                        sp.wait_ge(w_used, before + 1)
                        sp.dma_start(bias_t, bias_parts[e]).then_inc(ld_bias, 16)

            def load_down(e, before):
                for q in range(KF // 2):
                    sp.wait_ge(lo_ready, before + q + 1)
                    sp.dma_start(dn_pair[q], dn_d[e, q]).then_inc(ld_dn[q], 16)

            load_gate_up(1, 0)
            load_gate_up(2, gu_at(1))
            load_down(1, dn_at(0))
            with sp.Fori(2, NE - 1) as i:
                load_gate_up(i + 1, gu_at(i))
                load_down(i, dn_at(i - 1))
            for q in range(KF // 2):
                sp.wait_ge(lo_ready, gu_at(NE - 1) + q + 1)
                sp.dma_start(dn_last[q].rearrange("p (j n) -> p j n", j=2), dn_d[NE - 1, q]).then_inc(ld_x0[q], 16)
            sp.wait_ge(extra_ready, 1)
            n_extra = sp.value_load(extra_i[0:1, 32:33], min_val=0, max_val=15)
            with sp.If(n_extra > 0):
                sp.wait_ge(lo_ready, NE * BLOCK_TILES)
                with sp.Fori(0, n_extra) as j:
                    e = sp.value_load(extra_i[0:1, bass.ds(j, 1)], min_val=0, max_val=NE - 1)
                    row = sp.value_load(extra_i[0:1, bass.ds(j + 16, 1)], min_val=0, max_val=NE * CAP - P)
                    sp.wait_ge(y_sent, (j + NE) * 16)
                    sp.dma_start(xslot[:, :], table[bass.ds(row, P), :]).then_inc(ld_xslot, 16)
                    load_gate_up(e, extra_at(j - 1))
                    load_down(e, extra_at(j - 1) + KD)
            sp.wait_ge(lo_ready, extra_at(n_extra - 1) + KD)
            sp.dma_start(X1C, x1_cols).then_inc(ld_ple, 16)
            sp.dma_start(PG[1], w_pg_k[:, :, 512:1024]).then_inc(ld_ple, 16)
            sp.wait_ge(y_sent, (n_extra + NE) * 16)
            for t in range(NT):
                rows = y_rows[t * P * TOPK:(t + 1) * P * TOPK, :].rearrange("(p k) n -> p k n", k=TOPK)
                for k in range(TOPK):
                    if (t, k) == (3, 2):
                        sp.wait_ge(ln_mv, NT + 1)
                    sp.dma_start(y_in(t, k), rows[:, k, :]).then_inc(ld_y[t][k // 2], 16)
                if t == 0:
                    sp.dma_start(LN2[:, 0, :], ln2_g.partition_broadcast(P)).then_inc(ld_ln, 16)
                    sp.dma_start(LN2[:, 1, :], ln2_b.partition_broadcast(P)).then_inc(ld_ln, 16)
            for t in range(NT):
                if t < NT - 1:
                    sp.wait_ge(fin_done, t + 1)
                else:
                    sp.wait_ge(x1_ready, NT + 1)
                sp.dma_start(out[t * P:(t + 1) * P, :], X1[:, t, :]).then_inc(st_out, 16)
            sp.wait_ge(st_out, 16 * NT)

        @block.tensor
        def _(pe):
            mm, tr = nc.tensor.matmul, nc.tensor.transpose

            def project(g):
                blk, j = divmod(g, 4)
                bank_free(pe, g)
                js = slice(j * P, (j + 1) * P)
                for n, ks in enumerate(QUARTERS if blk == 0 else HALVES):
                    if g == 0:
                        pe.wait_ge(x_lo, n + 1)
                    if j == 0:
                        pe.wait_ge(wi_lo, split_steps(blk) + n + 1)
                    for k in range(ks.start, ks.stop):
                        for x, w in ((XTH, w_in_hi[blk % 2]), (XTL, w_in_hi[blk % 2]), (XTH, w_in_lo[blk % SLOTS])):
                            ends = dict(start=(k == 0 and x is XTH and w is w_in_hi[blk % 2]),
                                        stop=(k == KD - 1 and w is w_in_lo[blk % SLOTS]))
                            if blk in (2, 6):
                                last = mm(bank[g % 2], x[:, k, js], w[:, k, :], **ends)
                            else:
                                last = mm(bank[g % 2], w[:, k, js], x[:, k, :], **ends)
                last.then_inc(proj_done, 1)

            def scores(n):
                h, i = divmod(n, NT)
                r0, c = (h % 2) * EA, h // 2
                if n >= 2:
                    pe.wait_ge(sc_read, n - 1)
                mm(bank[2 + n % 2][:, 0:(i + 1) * P], QK[r0:r0 + EA, c, i * P:(i + 1) * P],
                   QK[r0:r0 + EA, 4 + c, 0:(i + 1) * P], start=True, stop=True).then_inc(sc_mm, 1)

            def transpose_probs(n):
                i = n % NT
                pe.wait_ge(p_norm, n + 1)
                if n >= 2:
                    pe.wait_ge(tr_evac, n - 1)
                for kt in range(i + 1):
                    last = tr(bank[4 + n % 2][:, kt * P:(kt + 1) * P], S2[:, n % 3, kt * P:(kt + 1) * P], ident)
                last.then_inc(tr_mm, 1)

            def attend(h):
                r0 = (h % 2) * EA
                pe.wait_ge(tr_evac, NT * (h + 1))
                if h:
                    pe.wait_ge(o_evac, h)
                for kt in range(NT):
                    last = mm(bank[6][r0:r0 + EA, kt * P:SEQ], VT[:, kt, h * EA:(h + 1) * EA],
                              PT[:, kt, kt * P:SEQ], start=(kt == 0), stop=(kt == NT - 1))
                last.then_inc(o_mm, 1)

            for g in range(12):
                project(g)
                if g == 7:
                    pe.wait_ge(ba_split, 2)
                    for k in range(KD):
                        for x, w in ((XTH, w_ba_hi), (XTL, w_ba_hi), (XTH, w_ba_lo)):
                            last = mm(bank[7][0:2 * HB, :], w[:, k, :], x[:, k, :],
                                      start=(k == 0 and x is XTH and w is w_ba_hi), stop=(k == KD - 1 and w is w_ba_lo))
                    last.then_inc(ba_mm, 1)
            pe.wait_ge(ld_c, 16)
            pe.wait_ge(ba_rows, 1)
            for t in range(NT):
                last = tr(bank[7][:, t * 8:(t + 1) * 8], BAT[:, t * P:(t + 1) * P], ident[0:2 * HB, 0:2 * HB])
            last.then_inc(ba_done, 1)
            pe.wait_ge(evac_done, 12)
            for m in range(16):
                if m == 3:
                    pe.wait_ge(gates_f, 1)
                    mm(bank[7][:, 0:16], upper, GG, start=True, stop=True)
                    mm(bank[7][:, 16:32], ones, GG, start=True, stop=True).then_inc(gc_mm, 1)
                scores(2 * m)
                scores(2 * m + 1)
                if m >= 2 and m % 2 == 0:
                    attend(m // 2 - 1)
                project(12 + m)
                transpose_probs(2 * m)
                transpose_probs(2 * m + 1)
            attend(HA - 1)

            pe.wait_ge(sq_done, 8)
            pe.wait_ge(tr_evac, HA * NT)
            for n in range(8):
                if n == 4:
                    pe.wait_ge(gsc_done, 1)
                    pe.wait_ge(evac_done, 16)
                    pe.wait_ge(o_evac, HA)
                mm(bank[SUM_BANK[n]], ones, SQ[:, n, :], start=True, stop=True).then_inc(nrm_mm, 1)
            pe.wait_ge(nrm_done, 8)

            def spread(h):
                a = 4 * (h % 2)
                if h >= 2:
                    pe.wait_ge(dp_kdec, h - 1)
                    pe.wait_ge(dp_kbvb, h - 1)
                for t in range(NT):
                    mm(bank[a][:, t * P:(t + 1) * P], GG[:, t * HB + h:t * HB + h + 1].to_broadcast([P, P]), upper,
                       start=True, stop=True)
                    last = mm(bank[a + 1][:, t * P:(t + 1) * P],
                              BETA[:, t * HB + h:t * HB + h + 1].to_broadcast([P, P]), ident, start=True, stop=True)
                last.then_inc(dp_bc, 1)

            def grams(h):
                a = 4 * (h % 2)
                pe.wait_ge(dp_kb, h + 1)
                if h >= 2:
                    pe.wait_ge(dp_lt, 2 * (h - 1))
                for t in range(NT):
                    s = slice(t * P, (t + 1) * P)
                    mm(bank[a + 2][:, s], DT[:, 4 + h, s], QK[:, h, s], start=True, stop=True)
                    last = mm(bank[a + 3][:, s], DT[:, 4 + h, s], DT[:, h, s], start=True, stop=True)
                last.then_inc(dp_la, 1)
                pe.wait_ge(dp_arg, h + 1)
                pe.wait_ge(dp_e, h + 1)
                for t in range(NT):
                    s = slice(t * P, (t + 1) * P)
                    tr(bank[a][:, s], DT[:, 4 + h, s], ident)
                    last = tr(bank[a + 1][:, s], DT[:, 8 + h, s], ident)
                last.then_inc(dp_tr, 1)

            spread(0)
            spread(1)
            for h in range(HB):
                grams(h)
                if h + 2 < HB:
                    spread(h + 2)

            pe.wait_ge(dp_kdec, HB)
            pe.wait_ge(dp_kbvb, HB)
            pe.wait_ge(dp_lt, 2 * HB)
            for h in range(HB):
                pe.wait_ge(dt_ready, h + 1)
                if h >= 2:
                    pe.wait_ge(dd_ready, h - 1)
                for c in range(NT):
                    last = tr(bank[6 + h % 2][:, c * P:(c + 1) * P], DD[:, h, c, 1, :], ident)
                last.then_inc(dt_mm, 1)
            pe.wait_ge(dd_ready, HB)

            with pe.Fori(0, LEVELS - 2) as lv:
                def times_l(h, lv=lv):
                    pe.wait_ge(dd_ready, lv * HB + h + 1)
                    for c in range(NT):
                        last = mm(bank[3 * (h % 2)][:, c * P:(c + 1) * P], LT[:, h, c * P:(c + 1) * P],
                                  DD[:, h, c, 0, :], start=True, stop=True)
                    last.then_inc(inv_a, 1)

                def correct(h):
                    pe.wait_ge(inv_t1, lv * HB + h + 1)
                    pe.wait_ge(dd_ready, lv * HB + h + 3)
                    for c in range(NT):
                        b = bank[3 * (h % 2) + 1 + c // 2]
                        o = (c % 2) * 2 * P
                        mm(b[:, o:o + P], DD[:, h, c, 1, :], T1[:, h, c * P:(c + 1) * P], start=True, stop=True)
                        last = mm(b[:, o + P:o + 2 * P], T1[:, h, c * P:(c + 1) * P], DD[:, h, c, 1, :],
                                  start=True, stop=True)
                    last.then_inc(inv_b, 1)

                times_l(0)
                times_l(1)
                correct(0)
                times_l(2)
                correct(1)
                times_l(3)
                correct(2)
                correct(3)

            def correct_last(h):
                pe.wait_ge(inv_t1, (LEVELS - 2) * HB + h + 1)
                pe.wait_ge(dd_ready, (LEVELS - 2) * HB + h + 3)
                for c in range(NT):
                    last = mm(bank[3 * (h % 2) + 1][:, c * P:(c + 1) * P], T1[:, h, c * P:(c + 1) * P],
                              DD[:, h, c, 1, :], start=True, stop=True)
                last.then_inc(inv_b, 1)

            times_l(0, LEVELS - 2)
            times_l(1, LEVELS - 2)
            correct_last(0)
            times_l(2, LEVELS - 2)
            correct_last(1)
            times_l(3, LEVELS - 2)
            correct_last(2)
            correct_last(3)

            for h in range(HB):
                pe.wait_ge(dd_ready, (LEVELS - 1) * HB + h + 1)
                if h >= 2:
                    pe.wait_ge(w_evac, h - 1)
                for c in range(NT):
                    last = mm(bank[6 + h % 2][:, c * P:(c + 1) * P], KB[:, h, c * P:(c + 1) * P], DD[:, h, c, 1, :],
                              start=True, stop=True)
                last.then_inc(w_mm, 1)
            pe.wait_ge(w_evac, HB)
            pe.wait_ge(st_zero, 1)
            pe.wait_ge(dp_qdec, HB)

            def scan(c):
                s = slice(c * P, (c + 1) * P)
                cur = ST[c % 2]
                if c:
                    pe.wait_ge(scan_st, HB * c)
                for h in range(HB):
                    hs = slice(h * P, (h + 1) * P)
                    mm(bank[0][:, hs], DD[:, h, c, 1, :], VB[:, h, s], start=True, stop=False)
                    last = mm(bank[0][:, hs], T1[:, h, s], cur[:, hs], start=False, stop=True)
                last.then_inc(scan_v, 1)
                pe.wait_ge(scan_vn, c + 1)
                for h in range(HB):
                    hs = slice(h * P, (h + 1) * P)
                    last = mm(bank[1][:, hs], KDEC[:, h, s], VN[:, hs], start=True, stop=True)
                last.then_inc(scan_s, 1)
                if c >= 2:
                    pe.wait_ge(y_norm, c - 1)
                for h in range(HB):
                    hs = slice(h * P, (h + 1) * P)
                    mm(bank[2 + c % 2][:, hs], DT[:, h, s], cur[:, hs], start=True, stop=False)
                    last = mm(bank[2 + c % 2][:, hs], AT[:, h, s], VN[:, hs], start=False, stop=True)
                last.then_inc(scan_o, 1)

            def y_transpose(c):
                pe.wait_ge(y_gated, c + 1)
                if c:
                    pe.wait_ge(mix_ready, c)
                for h in range(HB):
                    last = tr(bank[4][:, h * P:(h + 1) * P], YT[:, h * P:(h + 1) * P], ident)
                last.then_inc(yt_mm, 1)

            def mix(c):
                s = slice(c * P, (c + 1) * P)
                if c == 0:
                    pe.wait_ge(ld_wout, 16)
                else:
                    pe.wait_ge(mix_read, c)
                pe.wait_ge(mix_ready, c + 1)
                for half in range(2):
                    for k in range(KD):
                        y = MXA[:, k, s] if k < 4 else MXB[:, k - 4, s]
                        last = mm(bank[5 + half], y, dn_tile[k][:, half * 512:(half + 1) * 512],
                                  start=(k == 0), stop=(k == KD - 1))
                last.then_inc(mix_mm, 1)

            def x1_transpose(t):
                pe.wait_ge(x1_ready, t + 1)
                for q in range(2):
                    if t or q:
                        pe.wait_ge(xt_evac, 2 * t + q)
                    for j in range(4):
                        k = 4 * q + j
                        last = tr(bank[7][:, j * P:(j + 1) * P], X1[:, t, k * P:(k + 1) * P], ident)
                    last.then_inc(xt_mm, 1)

            def ple_gate(n):
                half, t = divmod(n, NT)
                if t == 0:
                    pe.wait_ge(ld_ple, PLE_LOADS[half])
                if n == 0:
                    pe.wait_ge(y_norm, NT)
                    pe.wait_ge(xt_evac, 2)
                if n >= 2:
                    pe.wait_ge(ple_sig, n - 1)
                for k in range(KD):
                    mm(bank[2 + n % 2], (X1T, X1C)[half][:, k, t * P:(t + 1) * P], PG[half][:, k, :],
                       start=(k == 0), stop=False)
                mm(bank[2 + n % 2], ones[0:1, :], b_pg[half], start=False, stop=True).then_inc(ple_gmm, 1)

            scan(0)
            scan(1)
            y_transpose(0)
            scan(2)
            mix(0)
            y_transpose(1)
            scan(3)
            mix(1)
            x1_transpose(0)
            y_transpose(2)
            mix(2)
            x1_transpose(1)
            y_transpose(3)
            mix(3)
            x1_transpose(2)
            ple_gate(0)
            x1_transpose(3)

            pe.wait_ge(xt_evac, 2 * NT)
            for k in range(KD):
                last = mm(bank[0][0:NE, :], w_rt[:, k, :], X1T[:, k, :], start=(k == 0), stop=(k == KD - 1))
            last.then_inc(rt_t, 1)
            pe.wait_ge(rt_biased, 1)
            for t in range(NT):
                last = tr(bank[1][:, t * NE:(t + 1) * NE], logitT[:, t * P:(t + 1) * P], ident[0:NE, 0:NE])
            last.then_inc(rt_mm, 1)

            def ple_rest(n):
                half, t = divmod(n, NT)
                s = slice(t * P, (t + 1) * P)
                if n == 0:
                    pe.wait_ge(gT_evac, 1)
                    pe.wait_ge(ld_wout, 32)
                if half == 0:
                    if n:
                        pe.wait_ge(ple_read, n)
                    for q in range(2):
                        mm(bank[6 + q], gT[:, s], b_dn[:, q * 512:(q + 1) * 512], start=True, stop=True)
                elif n >= 2:
                    pe.wait_ge(ple_read, n - 1)
                b = bank[PROJ_BANK[half] + n % 2]
                mm(b, S2[:, 0, s], PJ[half][:, 0, :], start=True, stop=False)
                mm(b, S2[:, 1, s], PJ[half][:, 1, :], start=False, stop=True).then_inc(ple_mm, 1)

            pe.wait_ge(rt_memb, 1)
            for t in range(NT):
                for s in range(t):
                    mm(bank[1][:, t * NE:(t + 1) * NE], ones, memb[:, s, :], start=(s == 0), stop=False)
                mm(bank[1][:, t * NE:(t + 1) * NE], strict, memb[:, t, :], start=(t == 0), stop=True)
            for s in range(NT):
                last = mm(bank[1][:, 4 * NE:5 * NE], ones, memb[:, s, :], start=(s == 0), stop=(s == NT - 1))
            last.then_inc(pos_mm, 1)
            pe.wait_ge(gm_ready, 1)
            for t in range(NT):
                last = tr(bank[0][0:NE, t * P:(t + 1) * P], gmat[:, t, :], ident)
            last.then_inc(gT_mm, 1)
            def transpose_rows(i, src, done, first_bank=6):
                for q in range(2):
                    for j in range(4):
                        k = 4 * q + j
                        last = tr(bank[first_bank + q][:, j * P:(j + 1) * P], src[:, k * P:(k + 1) * P], ident)
                last.then_inc(done, 1)

            def gate_up(i, at):
                pe.wait_ge(ld_bias, i * 16 + 16)
                pe.wait_ge(xl_ready, i + 1)
                if not isinstance(i, int) or i:
                    pe.wait_ge(h_read, i)
                for n in range(4):
                    mm(bank[n], ones3[:, :], bias_t[:, n * 512:(n + 1) * 512], start=True, stop=False)
                for k in range(KD):
                    pe.wait_ge(hi_ready, at + k + 1)
                    for x in (xh, xl):
                        for n in range(4):
                            last = mm(bank[n], x[:, k, :], w_hi[:, k % 2, n * 512:(n + 1) * 512],
                                      start=False, stop=False)
                    last.then_inc(hi_used, 1)
                    pe.wait_ge(lo_ready, at + k + 1)
                    for n in range(4):
                        last = mm(bank[n], xh[:, k, :], w_lo[:, k % 2, n * 512:(n + 1) * 512],
                                  start=False, stop=(k == KD - 1))
                    last.then_inc(w_used, 1)

            def down(i, at):
                pe.wait_ge(al_ready, i + 1)
                pe.wait_ge(y_evac, i + 1)
                for q in range(KF // 2):
                    pe.wait_ge(hi_ready, at + q + 1)
                    for j in range(2):
                        k = 2 * q + j
                        for a in (ah, al):
                            for n in range(2):
                                last = mm(bank[4 + n], a[:, k, :],
                                          w_hi[:, q % 2, j * FE + n * 512:j * FE + (n + 1) * 512],
                                          start=(k == 0 and a is ah), stop=False)
                    last.then_inc(hi_used, 1)
                    pe.wait_ge(lo_ready, at + q + 1)
                    for j in range(2):
                        k = 2 * q + j
                        for n in range(2):
                            last = mm(bank[4 + n], ah[:, k, :], w_lo[:, q % 2, j * FE + n * 512:j * FE + (n + 1) * 512],
                                      start=False, stop=(k == KF - 1))
                    last.then_inc(w_used, 1)

            def rows_in(i):
                pe.wait_ge(gathered, i * 16 + 16)
                if not isinstance(i, int) or i >= 2:
                    pe.wait_ge(al_ready, i - 1)
                transpose_rows(i, xg, xgt_mm)

            def acts(i, rows):
                pe.wait_ge(act_ready, i + 1)
                pe.wait_ge(xl_ready, rows)
                transpose_rows(i, g_t, at_mm)

            ple_gate(1)
            ple_rest(0)
            for t in range(2, NT):
                ple_gate(t)
                ple_rest(t - 1)
            pe.wait_ge(gathered, 16)
            pe.wait_ge(extra_ready, 1)
            transpose_rows(0, xg, xgt_mm, first_bank=0)
            ple_rest(NT - 1)
            pe.wait_ge(ple_sig, NT)
            gate_up(0, gu_at(0))
            pe.wait_ge(ple_read, NT)
            rows_in(1)
            gate_up(1, gu_at(1))
            acts(0, 2)
            rows_in(2)
            down(0, dn_at(0))
            acts(1, 3)
            with pe.Fori(2, NE - 1) as i:
                gate_up(i, gu_at(i))
                rows_in(i + 1)
                down(i - 1, dn_at(i - 1))
                acts(i, i + 2)
            gate_up(NE - 1, gu_at(NE - 1))
            down(NE - 2, dn_at(NE - 2))
            acts(NE - 1, NE)
            down(NE - 1, DN_LAST)
            pe.wait_ge(extra_ready, 1)
            n_extra = pe.value_load(extra_i[0:1, 32:33], min_val=0, max_val=15)
            with pe.If(n_extra > 0):
                with pe.Fori(0, n_extra) as j:
                    pe.wait_ge(al_ready, j + NE)
                    rows_in(j + NE)
                    gate_up(j + NE, extra_at(j))
                    acts(j + NE, j + NE + 1)
                    down(j + NE, extra_at(j) + KD)
            for t in range(NT):
                ple_gate(NT + t)
                ple_rest(NT + t)

        @block.scalar
        def _(act):
            A = nc.scalar.activation
            chain = [0]

            def link(ins):
                chain[0] += 1
                ins.then_inc(ach, 1)
                act.wait_ge(ach, chain[0])

            def w_in_upper(blk):
                for n, ks in enumerate(QUARTERS if blk == 0 else HALVES):
                    if blk == 0:
                        act.wait_ge(ld_x0[n], 32)
                        A(XTH[:, ks, :], XA[:, ks, :], ACT.Copy).then_inc(x_hi, 1)
                    else:
                        act.wait_ge(ld_w[blk % SLOTS], w_in_loads(blk))
                    if blk >= 2:
                        act.wait_ge(proj_done, 4 * (blk - 1))
                    A(w_in_hi[blk % 2][:, ks, :], w_in_raw[blk % SLOTS][:, ks, :], ACT.Copy).then_inc(wi_hi, 1)

            w_in_upper(0)
            w_in_upper(1)
            act.wait_ge(ld_small, 128)
            act.wait_ge(dch, 1)
            A(w_ba_hi[:, :, :], w_ba[:, :, :], ACT.Copy).then_inc(ba_split, 1)
            link(A(na[:, :], na[:, :], ACT.Exp))
            link(nc.scalar.mul(na[:, :], na[:, :], -1.0))
            for g in range(12):
                if g in (4, 8):
                    w_in_upper(g // 4 + 1)
                act.wait_ge(proj_done, g + 1)
                blk, j = divmod(g, 4)
                dst = (QK[:, j, :], QK[:, 4 + j, :], VT[:, j, :])[blk]
                A(dst, bank[g % 2], ACT.Copy).then_inc(evac_done, 1)

            def exps(n):
                i = n % NT
                act.wait_ge(sc_max, n + 1)
                s = S2[:, n % 3, 0:(i + 1) * P]
                A(s, s, ACT.Exp, bias=nmax[:, n:n + 1], accum_out=den[:, n:n + 1]).then_inc(sc_exp, 1)

            def evac_probs(n):
                h, i = divmod(n, NT)
                act.wait_ge(tr_mm, n + 1)
                if h:
                    act.wait_ge(o_mm, h)
                A(PT[:, 0:i + 1, i * P:(i + 1) * P],
                  bank[4 + n % 2][:, 0:(i + 1) * P].rearrange("p (k n) -> p k n", n=P), ACT.Copy).then_inc(tr_evac, 1)

            def evac_out(h):
                r0 = (h % 2) * EA
                act.wait_ge(o_mm, h + 1)
                A(MXA[r0:r0 + EA, h // 2, :], bank[6][r0:r0 + EA, :], ACT.Copy).then_inc(o_evac, 1)

            def silu(t):
                A(t, t, ACT.Silu).then_inc(silu_done, 1)

            for m in range(16):
                if m in (1, 4, 8):
                    w_in_upper({1: 4, 4: 5, 8: 6}[m])
                if m == 1:
                    act.wait_ge(route_e, 1)
                    A(E1, BETA, ACT.Exp, scale=-1.0).then_inc(route_exp, 1)
                    link(A(SP1, SP1, ACT.Exp, scale=-1.0))
                    A(SP1, SP1, ACT.Ln, bias=one_c[:, :]).then_inc(route_exp, 1)
                if m == 5:
                    act.wait_ge(route_e, 2)
                    A(EGC, GC, ACT.Exp).then_inc(route_exp, 1)
                    A(EGL, GL, ACT.Exp).then_inc(route_exp, 1)
                    A(EKD, EKD, ACT.Exp).then_inc(route_exp, 1)
                if m >= 1:
                    evac_probs(2 * m - 2)
                    evac_probs(2 * m - 1)
                exps(2 * m)
                exps(2 * m + 1)
                if m >= 2 and m % 2 == 0:
                    evac_out(m // 2 - 1)
                if m in (5, 9, 13):
                    b = (m - 5) // 4
                    act.wait_ge(conv_done, 4 * (b + 1))
                    silu(DT[:, 4 * b:4 * b + 4, :])
                if m >= 13:
                    g = 12 + m - 1
                    act.wait_ge(proj_done, g + 1)
                    A(ZT[:, g - 24, :], bank[g % 2], ACT.Copy).then_inc(evac_done, 1)
            evac_probs(30)
            evac_probs(31)
            evac_out(HA - 1)
            act.wait_ge(proj_done, 28)
            A(ZT[:, 3, :], bank[27 % 2], ACT.Copy).then_inc(evac_done, 1)
            sums = (PS[:, 2:6, :], PS[:, 0:2, :], PS[:, 6:8, :])
            for banks, upto in zip(sums, (4, 6, 8)):
                act.wait_ge(nrm_mm, upto)
                A(banks, banks, ACT.Ln, bias=eps_l2[:, :]).then_inc(nrm_ln, 1)
            for step, banks in enumerate(sums):
                act.wait_ge(nrm_ln, step + 1)
                A(banks, banks, ACT.Exp, scale=-0.5).then_inc(nrm_rs, 1)

            def spread_exp(h):
                a = 4 * (h % 2)
                act.wait_ge(dp_bc, h + 1)
                A(QK[:, 4 + h, :], bank[a], ACT.Exp).then_inc(dp_e, 1)
                act.wait_ge(dp_arg, h + 1)
                A(PT[:, h, :], PT[:, h, :], ACT.Exp).then_inc(dp_dec, 1)

            def evac_tokens(h):
                a = 4 * (h % 2)
                act.wait_ge(dp_tr, h + 1)
                for t in range(NT):
                    s = slice(t * P, (t + 1) * P)
                    j = t * HB + h
                    last = A(VB[:, h, s], bank[a + 1][:, s], ACT.Copy, scale=BETA[:, j:j + 1])
                last.then_inc(dp_kbvb, 1)
                for t in range(NT):
                    s = slice(t * P, (t + 1) * P)
                    j = t * HB + h
                    A(KDEC[:, h, s], bank[a][:, s], ACT.Copy, scale=EKD[:, j:j + 1])
                    last = A(KB[:, h, s], bank[a][:, s], ACT.Copy, scale=BKE[:, j:j + 1])
                last.then_inc(dp_kdec, 1)

            act.wait_ge(gsc_done, 1)
            spread_exp(0)
            spread_exp(1)
            for h in range(HB):
                evac_tokens(h)
                if h + 2 < HB:
                    spread_exp(h + 2)
            for h in range(HB):
                act.wait_ge(dt_mm, h + 1)
                A(DD[:, h, :, 0, :], bank[6 + h % 2].rearrange("p (c n) -> p c n", n=P), ACT.Copy).then_inc(dd_ready, 1)
            act.wait_ge(evac_done, 16)
            silu(ZT[:, :, :])
            for h in range(HB):
                act.wait_ge(w_mm, h + 1)
                A(T1[:, h, :], bank[6 + h % 2], ACT.Copy, scale=-1.0).then_inc(w_evac, 1)

            def scan_evac(c):
                act.wait_ge(scan_v, c + 1)
                A(VN, bank[0], ACT.Copy).then_inc(scan_vn, 1)

            def rms(c):
                act.wait_ge(scan_o, c + 1)
                for h in range(HB):
                    if c or h:
                        act.wait_ge(sq_sum, c * HB + h)
                    A(junk[:, :], bank[2 + c % 2][:, h * P:(h + 1) * P], ACT.Square,
                      accum_out=MS[:, c * HB + h:c * HB + h + 1]).then_inc(sq_sum, 1)
                act.wait_ge(sq_sum, HB * (c + 1))
                s = slice(c * HB, (c + 1) * HB)
                A(RSD[:, s], MS[:, s], ACT.Sqrt, scale=1.0 / P, bias=eps_rms[:, :]).then_inc(rms_done, 1)

            def y_evac_t(c):
                act.wait_ge(yt_mm, c + 1)
                A(MXB[:, :, c * P:(c + 1) * P], bank[4].rearrange("p (h n) -> p h n", n=P),
                  ACT.Copy).then_inc(mix_ready, 1)

            def deviation(t, norm=0):
                act.wait_ge(ln_mv, norm * NT + t + 1)
                A(std[:, t:t + 1], mv[:, 1:2], ACT.Sqrt, bias=eps_ln[:, :]).then_inc(ln_std, 1)

            def x1_evac(t):
                for q in range(2):
                    act.wait_ge(xt_mm, 2 * t + q + 1)
                    A(X1T[:, 4 * q:4 * q + 4, t * P:(t + 1) * P], bank[7].rearrange("p (k n) -> p k n", n=P),
                      ACT.Copy).then_inc(xt_evac, 1)

            scan_evac(0)
            rms(0)
            scan_evac(1)
            y_evac_t(0)
            rms(1)
            scan_evac(2)
            rms(2)
            y_evac_t(1)
            scan_evac(3)
            deviation(0)
            rms(3)
            x1_evac(0)
            y_evac_t(2)
            deviation(1)
            x1_evac(1)
            y_evac_t(3)
            deviation(2)
            x1_evac(2)
            deviation(3)
            x1_evac(3)
            act.wait_ge(route_e, 3)
            A(gate[:, :, :], gate[:, :, :], ACT.Exp).then_inc(route_exp, 1)
            act.wait_ge(gT_mm, 1)
            A(gT, bank[0][0:NE, :], ACT.Copy).then_inc(gT_evac, 1)

            def ple_sigmoid(n):
                act.wait_ge(ple_gmm, n + 1)
                if n >= 2:
                    act.wait_ge(ple_read, n - 1)
                A(s_ple[n // NT][:, n % 2, :], bank[2 + n % 2], ACT.Sigmoid).then_inc(ple_sig, 1)

            for t in range(NT):
                ple_sigmoid(t)
                if t == NT - 1:
                    act.wait_ge(xgt_mm, 1)
                    A(xh[:, :, :], PS[:, 0:2, :].rearrange("p b n -> p (b n)").rearrange("p (k n) -> p k n", k=KD),
                      ACT.Copy).then_inc(xh_ready, 1)
                if t == 1:
                    act.wait_ge(ld_gu[0], 16)
                    A(w_hi[:, 0, :], gu_tile[0], ACT.Copy).then_inc(hi_ready, 1)

            six_seven = PS[:, 6:8, :].rearrange("p b n -> p (b n)").rearrange("p (k n) -> p k n", k=KD)

            def rows_out(i):
                act.wait_ge(xgt_mm, i + 1)
                A(xh[:, :, :], six_seven, ACT.Copy).then_inc(xh_ready, 1)

            def sigmoid(i):
                act.wait_ge(g_ready, i + 1)
                A(s_t, g_t, ACT.Sigmoid, scale=1.702).then_inc(sig_ready, 1)

            def acts_out(i):
                act.wait_ge(at_mm, i + 1)
                A(ah[:, :, :], six_seven, ACT.Copy).then_inc(ah_ready, 1)

            def y_out(i, at):
                act.wait_ge(w_used, at + KF // 2)
                act.wait_ge(dg_ready, i + 1)
                A(y_t, PS[:, 4:6, :].rearrange("p b n -> p (b n)"), ACT.Copy,
                  scale=d_idx[:, 1:2].bitcast(F32)).then_inc(y_evac, 1)

            def hi_parts(i, raws, loads, at, first, last):
                for k in range(first, last):
                    act.wait_ge(loads[k], i * 16 + 16)
                    if not isinstance(at, int) or at + k >= 2:
                        act.wait_ge(hi_used, at + k - 1)
                        act.wait_ge(lo_ready, at + k - 1)
                    A(w_hi[:, k % 2, :], raws[k], ACT.Copy).then_inc(hi_ready, 1)

            def hi_gu(i, at, first, last):
                hi_parts(i, gu_tile, ld_gu, at, first, last)

            def hi_dn(i, at, first, last):
                hi_parts(i, dn_raw, ld_dn, at, first, last)

            def hi_dn_last(first, last):
                hi_parts(2, dn_last, ld_x0, DN_LAST, first, last)

            act.wait_ge(ple_read, NT)
            act.wait_ge(st_x1, 16 * (NT + 1))
            A(junk[:, 0:1], one_c[:, :], ACT.Copy).then_inc(y_evac, 1)
            hi_gu(0, gu_at(0), 1, KD)
            rows_out(1)
            sigmoid(0)

            def turn(i, rows=True, first=False):
                hi_gu(i, gu_at(i), 0, 2)
                if first:
                    hi_gu(i, gu_at(i), 2, KD)
                    acts_out(i - 1)
                else:
                    y_out(i - 2, dn_at(i - 2))
                    acts_out(i - 1)
                    hi_gu(i, gu_at(i), 2, KD)
                hi_dn(i - 1, dn_at(i - 1), 0, 2)
                if rows:
                    rows_out(i + 1)
                sigmoid(i)
                hi_dn(i - 1, dn_at(i - 1), 2, 4)

            turn(1, first=True)
            with act.Fori(2, NE - 1) as i:
                turn(i)
            turn(NE - 1, rows=False)
            hi_dn_last(0, 2)
            y_out(NE - 2, dn_at(NE - 2))
            acts_out(NE - 1)
            hi_dn_last(2, 4)
            y_out(NE - 1, DN_LAST)
            act.wait_ge(extra_ready, 1)
            n_extra = act.value_load(extra_i[0:1, 32:33], min_val=0, max_val=15)
            with act.If(n_extra > 0):
                with act.Fori(0, n_extra) as j:
                    rows_out(j + NE)
                    hi_gu(j + NE, extra_at(j), 0, KD)
                    sigmoid(j + NE)
                    acts_out(j + NE)
                    hi_dn(j + NE - 1, extra_at(j) + KD, 0, 4)
                    y_out(j + NE, extra_at(j) + KD)
            for t in range(NT):
                ple_sigmoid(NT + t)
                deviation(t, norm=1)
                if t < NT - 1:
                    act.wait_ge(fin_rstd, t + 1)
                    A(X1[:, t, :], X1[:, t, :], ACT.Identity, scale=rstd[:, t:t + 1],
                      bias=shift_by[:, t:t + 1]).then_inc(fin_scaled, 1)

        @block.vector
        def _(dve):
            V = nc.vector
            chain = [0]

            def link(ins):
                chain[0] += 1
                ins.then_inc(dch, 1)
                dve.wait_ge(dch, chain[0])

            V.memset(eps_l2[:, :], L2_EPS)
            V.memset(eps_rms[:, :], RMS_EPS)
            V.memset(eps_ln[:, :], LN_EPS)
            V.memset(one_c[:, :], 1.0)
            link(V.memset(ones3[:, :], 1.0))
            def w_in_lower(blk):
                for n, ks in enumerate(QUARTERS if blk == 0 else HALVES):
                    if blk == 0:
                        dve.wait_ge(x_hi, n + 1)
                        V.tensor_tensor(XTL[:, ks, :], XA[:, ks, :], XTH[:, ks, :].bitcast(F32),
                                        ALU.subtract).then_inc(x_lo, 1)
                    dve.wait_ge(wi_hi, split_steps(blk) + n + 1)
                    V.tensor_tensor(w_in_lo[blk % SLOTS][:, ks, :], w_in_raw[blk % SLOTS][:, ks, :],
                                    w_in_hi[blk % 2][:, ks, :].bitcast(F32), ALU.subtract).then_inc(wi_lo, 1)

            w_in_lower(0)
            w_in_lower(1)
            dve.wait_ge(ba_split, 1)
            V.tensor_tensor(w_ba_lo[:, :, :], w_ba[:, :, :], w_ba_hi[:, :, :].bitcast(F32),
                            ALU.subtract).then_inc(ba_split, 1)
            dve.wait_ge(ld_bgu, 16)
            b32 = DT[0:NE, 0:4, :].rearrange("p a n -> p (a n)")
            rest = DT[0:NE, 4:8, :].rearrange("p a n -> p (a n)")
            parts = DT[0:NE, 8:12, :].rearrange("p a n -> p (a n)").bitcast(BF16)
            hi, mid = parts[:, 0:2 * FE], parts[:, 2 * FE:4 * FE]
            low = DT[0:NE, 4:6, :].rearrange("p a n -> p (a n)").bitcast(BF16)
            link(V.tensor_copy(hi, b32))
            link(V.tensor_tensor(rest, b32, hi, ALU.subtract))
            link(V.tensor_copy(mid, rest))
            link(V.tensor_tensor(b32, rest, mid, ALU.subtract))
            V.tensor_copy(low, b32).then_inc(split_done, 3)
            w_in_lower(2)
            dve.wait_ge(ba_mm, 1)
            V.tensor_copy(BAT, bank[7][0:2 * HB, :]).then_inc(ba_rows, 1)
            w_in_lower(3)
            dve.wait_ge(ba_done, 1)
            link(V.tensor_copy(BA, bank[7][:, 0:32]))
            ba = BA.rearrange("p (t c) -> p t c", c=8)
            xx = XX.rearrange("p (t h) -> p t h", h=HB)
            V.tensor_copy(BETA.rearrange("p (t h) -> p t h", h=HB), ba[:, :, 0:HB])
            link(V.tensor_tensor(xx, ba[:, :, HB:8], dtb[:, :].unsqueeze(1).to_broadcast([P, NT, HB]), ALU.add))
            V.scalar_tensor_tensor(SP1, XX, -1.0, XX, ALU.mult, ALU.max).then_inc(route_e, 1)

            def score(n):
                i = n % NT
                w = (i + 1) * P
                dve.wait_ge(sc_mm, n + 1)
                if n >= 3:
                    dve.wait_ge(tr_mm, n - 2)
                s = S2[:, n % 3, 0:w]
                V.scalar_tensor_tensor(s, bank[2 + n % 2][:, 0:w], EA ** -0.5,
                                       C[:, C_STRIP + P * (NT - 1 - i):C_STRIP + SEQ],
                                       ALU.mult, ALU.add).then_inc(sc_read, 1)
                dve.wait_ge(sc_read, n + 1)
                V.tensor_reduce(nmax[:, n:n + 1], s, AX.X, ALU.max, negate=True).then_inc(sc_max, 1)

            def normalise(n):
                i = n % NT
                dve.wait_ge(sc_exp, n + 1)
                link(V.reciprocal(rden[:, n:n + 1], den[:, n:n + 1]))
                s = S2[:, n % 3, 0:(i + 1) * P]
                V.tensor_scalar(s, s, rden[:, n:n + 1], None, ALU.mult).then_inc(p_norm, 1)

            def conv(c):
                g = 12 + c
                dve.wait_ge(proj_done, g + 1)
                src, dst = bank[g % 2], DT[:, c, :]
                link(V.tensor_scalar(dst, src, cw[:, c, 3:4], None, ALU.mult))
                for back in range(1, 4):
                    ins = V.scalar_tensor_tensor(dst[:, back:SEQ], src[:, 0:SEQ - back], cw[:, c, 3 - back:4 - back],
                                                 dst[:, back:SEQ], ALU.mult, ALU.add)
                    if back < 3:
                        link(ins)
                ins.then_inc(conv_done, 1)

            dve.wait_ge(ld_c, 16)
            for m in range(16):
                if m in (1, 4, 8):
                    w_in_lower({1: 4, 4: 5, 8: 6}[m])
                if m == 2:
                    dve.wait_ge(route_exp, 2)
                    link(V.tensor_scalar(E1, E1, 1.0, None, ALU.add))
                    V.reciprocal(BETA, E1)
                    link(V.scalar_tensor_tensor(SP1, XX, 0.0, SP1, ALU.max, ALU.add))
                    V.tensor_tensor(GG.rearrange("p (t h) -> p t h", h=HB), SP1.rearrange("p (t h) -> p t h", h=HB),
                                    na[:, :].unsqueeze(1).to_broadcast([P, NT, HB]), ALU.mult).then_inc(gates_f, 1)
                if m == 4:
                    dve.wait_ge(gc_mm, 1)
                    V.tensor_copy(GC, bank[7][:, 0:16])
                    link(V.tensor_copy(GL, bank[7][:, 16:32]))
                    V.tensor_tensor(EKD, GL, GC, ALU.subtract).then_inc(route_e, 1)
                if m == 6:
                    dve.wait_ge(route_exp, 5)
                    V.tensor_tensor(BKE, BETA, EGC, ALU.mult).then_inc(gsc_done, 1)
                score(2 * m)
                score(2 * m + 1)
                if 1 <= m <= 12:
                    if m == 1:
                        dve.wait_ge(st_bias, 48)
                    conv(m - 1)
                normalise(2 * m)
                normalise(2 * m + 1)

            for n in range(8):
                dve.wait_ge(nrm_rs, 1 + (n >= 4) + (n >= 6))
                d = DT[:, n, :]
                V.scalar_tensor_tensor(d, d, P ** -0.5 if n < HB else 1.0, bank[SUM_BANK[n]],
                                       ALU.mult, ALU.mult).then_inc(nrm_done, 1)
            dve.wait_ge(nrm_done, 8)

            def decays(h):
                a = 4 * (h % 2)
                dve.wait_ge(dp_e, h + 1)
                for t in range(NT):
                    s = slice(t * P, (t + 1) * P)
                    last = V.scalar_tensor_tensor(PT[:, h, s], bank[a][:, s], GC[:, t * HB + h:t * HB + h + 1], negm,
                                                  ALU.subtract, ALU.add)
                last.then_inc(dp_arg, 1)
                V.tensor_tensor(QK[:, h, :], DT[:, 4 + h, :], bank[a + 1], ALU.mult).then_inc(dp_kb, 1)

            def grams(h):
                a = 4 * (h % 2)
                dve.wait_ge(dp_la, h + 1)
                dve.wait_ge(dp_decs, h + 1)
                V.tensor_tensor(LT[:, h, :], bank[a + 2], S2[:, h % 2, :], ALU.mult).then_inc(dp_lt, 1)
                V.tensor_tensor(AT[:, h, :], bank[a + 3], PT[:, h, :], ALU.mult).then_inc(dp_lt, 1)

            dve.wait_ge(gsc_done, 1)
            decays(0)
            decays(1)
            def pairs_inverse(h):
                t1 = T1[:, h, :].rearrange("p (c n) -> p c n", n=P)
                pairs = C[:, C_LEVEL:C_LEVEL + P].unsqueeze(1).to_broadcast([P, NT, P])
                if h == 0:
                    dve.wait_ge(proj_done, 28)
                dve.wait_ge(dp_lt, 2 * h + 1)
                link(V.tensor_tensor(t1, LT[:, h, :].rearrange("p (c n) -> p c n", n=P), pairs, ALU.mult))
                V.tensor_tensor(DD[:, h, :, 1, :], ident.unsqueeze(1).to_broadcast([P, NT, P]), t1,
                                ALU.subtract).then_inc(dt_ready, 1)

            for h in range(HB):
                grams(h)
                if h + 2 < HB:
                    decays(h + 2)
                pairs_inverse(h)

            def mask_t1(h, lv, level):
                dve.wait_ge(inv_a, lv * HB + h + 1)
                V.tensor_tensor(T1[:, h, :].rearrange("p (c n) -> p c n", n=P),
                                bank[3 * (h % 2)].rearrange("p (c n) -> p c n", n=P), level,
                                ALU.mult).then_inc(inv_t1, 1)

            with dve.Fori(0, LEVELS - 2) as lv:
                level = C[:, bass.ds(lv * P + C_LEVEL + P, P)].unsqueeze(1).to_broadcast([P, NT, P])

                def update(h):
                    dve.wait_ge(inv_b, lv * HB + h + 1)
                    b = 3 * (h % 2) + 1
                    d = DD[:, h, :, :, :].rearrange("p c s n -> p (c s n)")
                    V.tensor_tensor(d, d, PS[:, b:b + 2, :].rearrange("p b n -> p (b n)"),
                                    ALU.subtract).then_inc(dd_ready, 1)

                mask_t1(0, lv, level)
                mask_t1(1, lv, level)
                update(0)
                mask_t1(2, lv, level)
                update(1)
                mask_t1(3, lv, level)
                update(2)
                update(3)

            def update_last(h):
                dve.wait_ge(inv_b, (LEVELS - 2) * HB + h + 1)
                d = DD[:, h, :, 1, :]
                V.tensor_tensor(d, d, bank[3 * (h % 2) + 1].rearrange("p (c n) -> p c n", n=P),
                                ALU.subtract).then_inc(dd_ready, 1)

            level = C[:, C_LEVEL + (LEVELS - 1) * P:C_LEVEL + LEVELS * P].unsqueeze(1).to_broadcast([P, NT, P])
            mask_t1(0, LEVELS - 2, level)
            mask_t1(1, LEVELS - 2, level)
            update_last(0)
            mask_t1(2, LEVELS - 2, level)
            update_last(1)
            mask_t1(3, LEVELS - 2, level)
            update_last(2)
            update_last(3)

            def state(c):
                dve.wait_ge(scan_s, c + 1)
                for h in range(HB):
                    hs = slice(h * P, (h + 1) * P)
                    V.scalar_tensor_tensor(ST[(c + 1) % 2][:, hs], ST[c % 2][:, hs],
                                           EGL[:, c * HB + h:c * HB + h + 1], bank[1][:, hs],
                                           ALU.mult, ALU.add).then_inc(scan_st, 1)
                dve.wait_ge(scan_st, HB * (c + 1))

            def y_scale(c):
                dve.wait_ge(rms_done, c + 1)
                link(V.reciprocal(RSD[:, c * HB:(c + 1) * HB], RSD[:, c * HB:(c + 1) * HB]))
                if c:
                    dve.wait_ge(yt_mm, c)
                for h in range(HB):
                    hs = slice(h * P, (h + 1) * P)
                    last = V.scalar_tensor_tensor(YT[:, hs], bank[2 + c % 2][:, hs],
                                                  RSD[:, c * HB + h:c * HB + h + 1], nw[:, :], ALU.mult, ALU.mult)
                last.then_inc(y_norm, 1)

            def moments(t, norm=0):
                row = X1[:, t, :]
                V.bn_stats(stat[:, 0:6], row[:, 0:512])
                link(V.bn_stats(stat[:, 6:12], row[:, 512:1024]))
                V.bn_aggr(mv, stat).then_inc(ln_mv, 1)
                dve.wait_ge(ln_mv, norm * NT + t + 1)

            def centre(t, g, norm=0):
                moments(t, norm)
                row = X1[:, t, :]
                link(V.scalar_tensor_tensor(row, row, mv[:, 0:1], g, ALU.subtract, ALU.mult))

            def divide_shift(t, b, done, norm=0):
                dve.wait_ge(ln_std, norm * NT + t + 1)
                link(V.reciprocal(rstd[:, t:t + 1], std[:, t:t + 1]))
                row = X1[:, t, :]
                V.scalar_tensor_tensor(row, row, rstd[:, t:t + 1], b, ALU.mult, ALU.add).then_inc(done, 1)

            def residual(c):
                dve.wait_ge(mix_mm, c + 1)
                if c == 0:
                    dve.wait_ge(ld_x, 16)
                V.scalar_tensor_tensor(X1[:, c, :], X1[:, c, :], ALPHA, PS[:, 5:7, :].rearrange("p b n -> p (b n)"),
                                       ALU.mult, ALU.add).then_inc(mix_read, 1)
                dve.wait_ge(mix_read, c + 1)
                if c == 0:
                    dve.wait_ge(ld_ln, 32)
                centre(c, LN[:, 0, :])
                divide_shift(c, LN[:, 1, :], x1_ready)

            state(0)
            y_scale(0)
            state(1)
            y_scale(1)
            state(2)
            residual(0)
            y_scale(2)
            residual(1)
            y_scale(3)
            residual(2)
            residual(3)

            dve.wait_ge(rt_t, 1)
            V.tensor_scalar(logitT, bank[0][0:NE, :], b_rt[:, :], None, ALU.add).then_inc(rt_biased, 1)
            dve.wait_ge(rt_mm, 1)
            link(V.tensor_copy(logit[:, :, :].rearrange("p t e -> p (t e)"), bank[1][:, 0:NT * NE]))
            for t in range(NT):
                link(V.max(topv[:, t, :], logit[:, t, :]))
                last = V.max_index(topi[:, t, :], topv[:, t, :], logit[:, t, :])
            link(last)
            link(V.tensor_copy(topf[:, :, :], topi[:, :, 0:TOPK]))
            V.tensor_tensor(gate[:, :, :], topv[:, :, 0:TOPK], topv[:, :, 0:1].to_broadcast([P, NT, TOPK]),
                            ALU.subtract).then_inc(route_e, 1)
            esel = C[:, C_ESEL:C_ESEL + NE]
            ebase = C[:, C_EBASE:C_EBASE + NE]
            n_tk = NT * TOPK
            link(V.tensor_tensor(onehot, esel.unsqueeze(1).to_broadcast([P, n_tk, NE]),
                                 topf[:, :, :].rearrange("p t k -> p (t k)").unsqueeze(2).to_broadcast([P, n_tk, NE]),
                                 ALU.is_equal))
            V.tensor_reduce(memb[:, :, :], onehot.rearrange("p (t k) e -> p t e k", k=TOPK), AX.X,
                            ALU.add).then_inc(rt_memb, 1)
            dve.wait_ge(route_exp, 6)
            link(V.tensor_reduce(gsum[:, :, 0], gate[:, :, :], AX.X, ALU.add))
            link(V.reciprocal(gsum[:, :, 0], gsum[:, :, 0]))
            link(V.tensor_tensor(gate[:, :, :], gate[:, :, :], gsum[:, :, :].to_broadcast([P, NT, TOPK]), ALU.mult))
            gate_f = gate[:, :, :].rearrange("p t k -> p (t k)").unsqueeze(2)
            V.tensor_copy(pay[:, :, 2:3].bitcast(F32), gate_f)
            link(V.tensor_tensor(work, onehot, gate_f.to_broadcast([P, n_tk, NE]), ALU.mult))
            V.tensor_reduce(gmat[:, :, :], work.rearrange("p (t k) e -> p t e k", k=TOPK), AX.X,
                            ALU.add).then_inc(gm_ready, 1)
            dve.wait_ge(pos_mm, 1)
            dve.wait_ge(gm_ready, 1)
            link(V.tensor_tensor(logit[:, :, :], bank[1][:, 0:NT * NE].rearrange("p (t e) -> p t e", e=NE),
                                 ebase.unsqueeze(1).to_broadcast([P, NT, NE]), ALU.add))
            for t in range(NT):
                ks = slice(t * TOPK, (t + 1) * TOPK)
                last = V.tensor_tensor(work[:, ks, :], onehot[:, ks, :],
                                       logit[:, t, :].unsqueeze(1).to_broadcast([P, TOPK, NE]), ALU.mult)
            link(last)
            link(V.tensor_reduce(rowf[:, :], work, AX.X, ALU.add))
            V.tensor_copy(rowi[:, :], rowf[:, :]).then_inc(rows_ready, 1)
            count = bank[1][:, NT * NE:(NT + 1) * NE]
            more, upto = extra_f[:, 0:NE], extra_f[:, NE:2 * NE]
            xe, xs = extra_f[:, 64:80], extra_f[:, 80:96]
            jj = C[:, C_ESEL:C_ESEL + 16]
            link(V.tensor_scalar(more, count, float(P), None, ALU.is_gt))
            link(V.scalar_tensor_tensor(more, count, 2.0 * P, more, ALU.is_gt, ALU.add))
            link(V.scalar_tensor_tensor(more, count, 3.0 * P, more, ALU.is_gt, ALU.add))
            link(V.tensor_tensor_scan(upto, ones[:, 0:NE], more, 0.0, ALU.mult, ALU.add))
            link(V.tensor_tensor(work, upto.unsqueeze(1).to_broadcast([P, 16, NE]),
                                 jj.unsqueeze(2).to_broadcast([P, 16, NE]), ALU.is_le))
            link(V.tensor_reduce(xe, work, AX.X, ALU.add))
            link(V.tensor_tensor(work, work, more.unsqueeze(1).to_broadcast([P, 16, NE]), ALU.mult))
            link(V.tensor_reduce(xs, work, AX.X, ALU.add))
            link(V.tensor_scalar(xe, xe, float(NE - 1), None, ALU.min))
            link(V.tensor_tensor(xs, jj, xs, ALU.subtract))
            link(V.tensor_scalar(xs, xs, 1.0, float(P), ALU.add, ALU.mult))
            link(V.scalar_tensor_tensor(xs, xe, float(CAP), xs, ALU.mult, ALU.add))
            link(V.tensor_scalar(xs, xs, float(NE * CAP - P), None, ALU.min))
            V.tensor_copy(extra_i[:, 0:16], xe)
            V.tensor_copy(extra_i[:, 16:32], xs)
            V.tensor_copy(extra_i[:, 32:33], upto[:, NE - 1:NE]).then_inc(extra_ready, 1)

            dve.wait_ge(st_x1, 16 * (NT + 1))

            def ple_product(n):
                dve.wait_ge(ple_sig, n + 1)
                dve.wait_ge(ple_mm, n + 1)
                g = s_ple[n // NT][:, n % 2, :]
                link(V.tensor_tensor(g, g, bank[PROJ_BANK[n // NT] + n % 2], ALU.mult))

            for t in range(NT):
                if t == NT - 1:
                    dve.wait_ge(xh_ready, 1)
                    V.tensor_tensor(xl[:, :, :], PS[:, 0:2, :].rearrange("p b n -> p (b n)").rearrange("p (k n) -> p k n", k=KD),
                                    xh[:, :, :].bitcast(F32), ALU.subtract).then_inc(xl_ready, 1)
                ple_product(t)
                row = X1[:, t, :].rearrange("p (b n) -> p b n", b=2)
                V.scalar_tensor_tensor(row[:, 1, :], row[:, 1, :], ALPHA, PS[:, 7, :], ALU.mult, ALU.add)
                link(V.scalar_tensor_tensor(row[:, 0, :], row[:, 0, :], ALPHA, s_ple[0][:, t % 2, :],
                                            ALU.mult, ALU.add))
                V.tensor_tensor(row[:, 0, :], row[:, 0, :], PS[:, 6, :], ALU.add).then_inc(ple_read, 1)
                if t == 1:
                    dve.wait_ge(hi_ready, 1)
                    V.tensor_tensor(w_lo[:, 0, :], gu_tile[0], w_hi[:, 0, :].bitcast(F32),
                                    ALU.subtract).then_inc(lo_ready, 1)

            six_seven = PS[:, 6:8, :].rearrange("p b n -> p (b n)").rearrange("p (k n) -> p k n", k=KD)

            def lo_parts(raws, at, first, last):
                for k in range(first, last):
                    dve.wait_ge(hi_ready, at + k + 1)
                    if not isinstance(at, int) or at + k >= 2:
                        dve.wait_ge(w_used, at + k - 1)
                    V.tensor_tensor(w_lo[:, k % 2, :], raws[k], w_hi[:, k % 2, :].bitcast(F32),
                                    ALU.subtract).then_inc(lo_ready, 1)

            def clamp(i, at):
                dve.wait_ge(w_used, at + KD)
                if not isinstance(i, int) or i:
                    dve.wait_ge(at_mm, i)
                V.tensor_scalar(g_t, PS[:, 0:2, :].rearrange("p b n -> p (b n)"), 7.0, None,
                                ALU.min).then_inc(g_ready, 1)
                V.tensor_scalar(u_t, PS[:, 2:4, :].rearrange("p b n -> p (b n)"), 7.0, -7.0,
                                ALU.min, ALU.max).then_inc(h_read, 1)

            def gated(i):
                dve.wait_ge(g_ready, i + 1)
                dve.wait_ge(sig_ready, i + 1)
                V.tensor_tensor(s_t, g_t, s_t, ALU.mult).then_inc(m_ready, 1)

            def swiglu(i):
                dve.wait_ge(h_read, i + 1)
                dve.wait_ge(m_ready, i + 1)
                V.scalar_tensor_tensor(g_t, u_t, 1.0, s_t, ALU.add, ALU.mult).then_inc(act_ready, 1)

            def rows_rest(i):
                dve.wait_ge(xh_ready, i + 1)
                V.tensor_tensor(xl[:, :, :], six_seven, xh[:, :, :].bitcast(F32), ALU.subtract).then_inc(xl_ready, 1)

            def acts_rest(i):
                dve.wait_ge(ah_ready, i + 1)
                V.tensor_tensor(al[:, :, :], six_seven, ah[:, :, :].bitcast(F32), ALU.subtract).then_inc(al_ready, 1)

            dve.wait_ge(ple_read, NT)
            lo_parts(gu_tile, gu_at(0), 1, KD)
            rows_rest(1)
            clamp(0, gu_at(0))
            gated(0)
            swiglu(0)

            def turn(i, rows=True, first=False):
                lo_parts(gu_tile, gu_at(i), 0, 2)
                if first:
                    lo_parts(gu_tile, gu_at(i), 2, KD)
                    acts_rest(i - 1)
                else:
                    acts_rest(i - 1)
                    lo_parts(gu_tile, gu_at(i), 2, KD)
                lo_parts(dn_raw, dn_at(i - 1), 0, 1)
                clamp(i, gu_at(i))
                lo_parts(dn_raw, dn_at(i - 1), 1, 2)
                gated(i)
                lo_parts(dn_raw, dn_at(i - 1), 2, 3)
                if rows:
                    rows_rest(i + 1)
                lo_parts(dn_raw, dn_at(i - 1), 3, 4)
                swiglu(i)

            turn(1, first=True)
            with dve.Fori(2, NE - 1) as i:
                turn(i)
            turn(NE - 1, rows=False)
            lo_parts(dn_last, DN_LAST, 0, 2)
            acts_rest(NE - 1)
            lo_parts(dn_last, DN_LAST, 2, 4)
            dve.wait_ge(extra_ready, 1)
            n_extra = dve.value_load(extra_i[0:1, 32:33], min_val=0, max_val=15)
            with dve.If(n_extra > 0):
                with dve.Fori(0, n_extra) as j:
                    rows_rest(j + NE)
                    lo_parts(gu_tile, extra_at(j), 0, KD)
                    clamp(j + NE, extra_at(j))
                    gated(j + NE)
                    swiglu(j + NE)
                    acts_rest(j + NE)
                    lo_parts(dn_raw, extra_at(j) + KD, 0, 4)
            def add_ple(t):
                ple_product(NT + t)
                half = X1[:, t, 512:1024]
                V.tensor_tensor(half, half, s_ple[1][:, t % 2, :], ALU.add).then_inc(ple_read, 1)
                dve.wait_ge(ple_read, NT + t + 1)

            add_ple(0)
            for t in range(NT):
                row = X1[:, t, :]
                dve.wait_ge(ld_y[t][1], 32)
                for k in (2, 3):
                    link(V.tensor_tensor(row, row, y_in(t, k), ALU.add))
                dve.wait_ge(fin_pair, t + 1)
                link(V.tensor_tensor(row, row, y_in(t, 0), ALU.add))
                if t:
                    add_ple(t)
                if t < NT - 1:
                    moments(t, norm=1)
                    dve.wait_ge(ln_std, NT + t + 1)
                    link(V.reciprocal(rstd[:, t:t + 1], std[:, t:t + 1]))
                    V.scalar_tensor_tensor(shift_by[:, t:t + 1], mv[:, 0:1], -1.0, rstd[:, t:t + 1], ALU.mult,
                                           ALU.mult).then_inc(fin_rstd, 1)
                else:
                    dve.wait_ge(ld_ln, 64)
                    centre(t, LN2[:, 0, :], norm=1)
                    divide_shift(t, LN2[:, 1, :], x1_ready, norm=1)

        @block.gpsimd
        def _(pool):
            G = nc.gpsimd
            pool.wait_ge(proj_done, 24)
            pool.wait_ge(silu_done, 2)
            for n in range(8):
                G.tensor_tensor(SQ[:, n, :], DT[:, n, :], DT[:, n, :], ALU.mult).then_inc(sq_done, 1)
            pool.wait_ge(proj_done, 28)
            G.memset(ST[0], 0.0).then_inc(st_zero, 1)
            pool.wait_ge(ld_c, 16)

            def strict_decay(h):
                pool.wait_ge(dp_dec, h + 1)
                if h >= 2:
                    pool.wait_ge(dp_lt, 2 * (h - 1))
                G.tensor_tensor(S2[:, h % 2, :].rearrange("p (c n) -> p c n", n=P),
                                PT[:, h, :].rearrange("p (c n) -> p c n", n=P),
                                strict.unsqueeze(1).to_broadcast([P, NT, P]), ALU.mult).then_inc(dp_decs, 1)

            def decay_q(h):
                pool.wait_ge(dp_la, h + 1)
                pool.wait_ge(dp_e, h + 1)
                G.tensor_tensor(DT[:, h, :], DT[:, h, :], QK[:, 4 + h, :], ALU.mult).then_inc(dp_qdec, 1)

            pool.wait_ge(nrm_mm, 8)
            pool.wait_ge(nrm_done, 8)
            strict_decay(0)
            strict_decay(1)
            for h in range(HB):
                decay_q(h)
                if h + 2 < HB:
                    strict_decay(h + 2)

            def gate_y(c):
                pool.wait_ge(y_norm, c + 1)
                G.tensor_tensor(YT, YT, ZT[:, c, :], ALU.mult).then_inc(y_gated, 1)

            pool.wait_ge(silu_done, 4)
            for c in range(NT):
                gate_y(c)
            pool.wait_ge(y_gated, NT)
            G.memset(xg, 0.0).then_inc(xg_zero, 1)
            pool.wait_ge(st_table, 16)
            pool.wait_ge(rows_ready, 1)
            for n in range(NT * TOPK):
                G.indirect_dma_start(table, bass.IndirectOffsetOnAxis(rowi[:, n:n + 1], 0), pay[:, n, :], None
                                     ).then_inc(tab_done, 16)
            pool.wait_ge(ld_slots, 16)
            pool.wait_ge(st_x1, 16 * (NT + 1))
            pool.wait_ge(xg_zero, 1)

            def held():
                pool.sem_inc(pool_steps, 1)

            def gather(i, tokens):
                G.tensor_copy(g_idx[:, :], tokens).then_inc(gi_ready, 1)
                pool.wait_ge(gi_ready, i + 1)
                held()
                G.indirect_dma_start(xg, None, x1_rows,
                                     bass.IndirectOffsetOnAxis(g_idx[:, :].bitcast(U32), 0),
                                     bounds_check=SEQ - 1, oob_is_err=False).then_inc(gathered, 16)

            def take_slots(what):
                G.tensor_copy(d_idx[:, :], what).then_inc(dg_ready, 1)

            def send(i):
                pool.wait_ge(y_evac, i + 2)
                held()
                G.indirect_dma_start(y_rows, bass.IndirectOffsetOnAxis(d_idx[:, 0:1].bitcast(U32), 0), y_t, None,
                                     bounds_check=SEQ * TOPK - 1, oob_is_err=False).then_inc(y_sent, 16)

            gather(0, slots[:, 0, 0:1])
            pool.wait_ge(xgt_mm, 1)
            gather(1, slots[:, 1, 0:1])
            take_slots(slots[:, 0, 1:3])
            pool.wait_ge(xgt_mm, 2)
            gather(2, slots[:, 2, 0:1])
            with pool.Fori(2, NE - 1) as i:
                pool.wait_ge(xgt_mm, i + 1)
                held()
                gather(i + 1, slots[:, bass.ds(i + 1, 1), 0:1].rearrange("p a b -> p (a b)"))
                send(i - 2)
                pool.wait_ge(y_sent, i * 16 - 16)
                held()
                take_slots(slots[:, bass.ds(i - 1, 1), 1:3].rearrange("p a b -> p (a b)"))
            send(NE - 3)
            pool.wait_ge(y_sent, (NE - 2) * 16)
            take_slots(slots[:, NE - 2, 1:3])
            send(NE - 2)
            pool.wait_ge(y_sent, (NE - 1) * 16)
            take_slots(slots[:, NE - 1, 1:3])
            send(NE - 1)
            pool.wait_ge(extra_ready, 1)
            n_extra = pool.value_load(extra_i[0:1, 32:33], min_val=0, max_val=15)
            with pool.If(n_extra > 0):
                with pool.Fori(0, n_extra) as j:
                    pool.wait_ge(ld_xslot, j * 16 + 16)
                    pool.wait_ge(xgt_mm, j + NE)
                    pool.wait_ge(y_sent, (j + NE) * 16)
                    held()
                    gather(j + NE, xslot[:, 0:1])
                    take_slots(xslot[:, 1:3])
                    send(j + NE)
            def pair(t):
                pool.wait_ge(ld_y[t][0], 32)
                G.tensor_tensor(y_in(t, 0), y_in(t, 0), y_in(t, 1), ALU.add).then_inc(fin_pair, 1)

            def shift(t):
                pool.wait_ge(fin_scaled, t + 1)
                G.tensor_tensor(X1[:, t, :], X1[:, t, :], LN2[:, 0, :], ALU.mult).then_inc(fin_times, 1)
                pool.wait_ge(fin_times, t + 1)
                G.tensor_tensor(X1[:, t, :], X1[:, t, :], LN2[:, 1, :], ALU.add).then_inc(fin_done, 1)

            pool.wait_ge(ld_ln, 64)
            pair(0)
            pair(1)
            for t in range(NT - 1):
                shift(t)
                if t + 2 < NT:
                    pair(t + 2)


_OUT = (SEQ, D)


def kernel(**inputs):
    import numpy as _np
    import concourse.bacc as _bacc
    from concourse import mybir as _mybir
    from concourse.bass_utils import run_bass_kernel_spmd as _run

    a = {k: _np.asarray(v) for k, v in inputs.items()}
    arrays = {
        "x": a["x"].reshape(SEQ, D),
        "xT": a["x"].reshape(SEQ, KD, P).transpose(2, 1, 0),
        "pT": a["p"].reshape(SEQ, PLE // P, P).transpose(2, 1, 0),
        "w_in": a["w_in"],
        "conv_w": a["conv_w"].reshape(4, 12, P).transpose(2, 1, 0),
        "a_log": a["a_log"].reshape(HB), "dt_bias": a["dt_bias"].reshape(HB), "gnorm_w": a["gnorm_w"].reshape(P),
        "w_out": a["w_out"], "ln1_g": a["ln1_g"].reshape(D), "ln1_b": a["ln1_b"].reshape(D),
        "w_router": a["w_router"], "b_router": a["b_router"],
        "w_gate_up": a["w_gate_up"], "b_gate_up": a["b_gate_up"], "w_down": a["w_down"], "b_down": a["b_down"],
        "w_ple_gate": a["w_ple_gate"], "b_ple_gate": a["b_ple_gate"], "w_ple_proj": a["w_ple_proj"],
        "ln2_g": a["ln2_g"].reshape(D), "ln2_b": a["ln2_b"].reshape(D),
        "consts": constants(), "table0": table_rows(), "pay0": payload(),
    }
    arrays = {f"in_{k}_dram": _np.ascontiguousarray(v) for k, v in arrays.items()}
    nc = _bacc.Bacc("TRN2", target_bir_lowering=False, num_devices=1)
    args = [nc.dram_tensor(n, v.shape, _mybir.dt.from_np(v.dtype), kind="ExternalInput").ap()
            for n, v in arrays.items()]
    args.append(nc.dram_tensor("out_0_dram", _OUT, _mybir.dt.float32, kind="ExternalOutput").ap())
    hybrid_layer(nc, *args)
    r = _run(nc, [arrays], core_ids=[0])
    return r.results[0]["out_0_dram"].reshape(1, SEQ, D)
```
